# Optimizing a Trainium2 kernel written in Bass

```python
import jax, jax.numpy as jnp
from jax import lax
import numpy as np

D_MODEL = 1024
BATCH = 1
SEQ = 1024
DEPTH = 2

GRID_W = 64
CTX_LEN = 256
Q_BLOCK = 128
ROPE_THETA = 10000.0
EPS = 1e-6

GQA_HEADS = 16
GQA_KV_HEADS = 4
GQA_HEAD_DIM = D_MODEL // GQA_HEADS
GQA_GROUP = GQA_HEADS // GQA_KV_HEADS

MLA_HEADS = 16
MLA_NOPE_DIM = 64
MLA_ROPE_DIM = 32
MLA_V_DIM = 64
MLA_Q_RANK = 384
MLA_KV_RANK = 256
MLA_QK_DIM = MLA_NOPE_DIM + MLA_ROPE_DIM

D_FF = -(-8 * D_MODEL // (3 * 256)) * 256

N_MIXERS = 2
N_A = (DEPTH + 1) // 2
N_B = DEPTH // 2

kernel_name = "hybrid_gqa_mla_prefix_dit"

def rmsnorm(x, g):
    x32 = x.astype(jnp.float32)
    y = x32 * lax.rsqrt(jnp.mean(x32 * x32, axis=-1, keepdims=True) + EPS)
    return (y * g.astype(jnp.float32)).astype(x.dtype)

def modulate(h, shift, scale):
    return h * (1 + scale) + shift

def axial_rope(rows, rot_dim):
    n = rot_dim // 4
    inv = ROPE_THETA ** (-jnp.arange(n, dtype=jnp.float32) / n)
    row = jnp.repeat(jnp.arange(rows, dtype=jnp.float32), GRID_W)
    col = jnp.tile(jnp.arange(GRID_W, dtype=jnp.float32), rows)
    ang = jnp.concatenate([row[:, None] * inv, col[:, None] * inv], axis=-1)
    return jnp.cos(ang), jnp.sin(ang)

def apply_rope(x, cos, sin):
    half = x.shape[-1] // 2
    x32 = x.astype(jnp.float32)
    x1, x2 = x32[..., :half], x32[..., half:]
    c = cos[None, :, None, :]
    s = sin[None, :, None, :]
    return jnp.concatenate([x1 * c - x2 * s, x2 * c + x1 * s], axis=-1).astype(x.dtype)

def attend_blocks(q, k, v, scale):
    B, S, Hkv, G, dq = q.shape
    nb = S // Q_BLOCK
    qb = q.reshape(B, nb, Q_BLOCK, Hkv, G, dq).transpose(1, 0, 2, 3, 4, 5)

    def one(qblk):
        s = jnp.einsum('bqhgd,bthd->bhgqt', qblk, k).astype(jnp.float32) * scale
        p = jax.nn.softmax(s, axis=-1).astype(v.dtype)
        return jnp.einsum('bhgqt,bthd->bqhgd', p, v)

    out = lax.map(one, qb)
    dv = v.shape[-1]
    return out.transpose(1, 0, 2, 3, 4, 5).reshape(B, S, Hkv * G * dv)

def gqa_mixer(h, hc, cos, sin, w_qkv, q_norm, k_norm, w_o, with_ctx_out):
    def project(t):
        B, T, _ = t.shape
        qkv = t @ w_qkv
        q = qkv[..., :GQA_HEADS * GQA_HEAD_DIM].reshape(B, T, GQA_HEADS, GQA_HEAD_DIM)
        k = qkv[..., GQA_HEADS * GQA_HEAD_DIM:(GQA_HEADS + GQA_KV_HEADS) * GQA_HEAD_DIM].reshape(B, T, GQA_KV_HEADS, GQA_HEAD_DIM)
        v = qkv[..., (GQA_HEADS + GQA_KV_HEADS) * GQA_HEAD_DIM:].reshape(B, T, GQA_KV_HEADS, GQA_HEAD_DIM)
        return rmsnorm(q, q_norm), rmsnorm(k, k_norm), v

    B, S, _ = h.shape
    q, k, v = project(h)
    qc, kc, vc = project(hc)
    q = apply_rope(q, cos, sin)
    k = apply_rope(k, cos, sin)
    scale = GQA_HEAD_DIM ** -0.5
    k_all = jnp.concatenate([kc, k], axis=1)
    v_all = jnp.concatenate([vc, v], axis=1)
    y = attend_blocks(q.reshape(B, S, GQA_KV_HEADS, GQA_GROUP, GQA_HEAD_DIM), k_all, v_all, scale) @ w_o
    yc = None
    if with_ctx_out:
        Bc, Tc = hc.shape[0], hc.shape[1]
        yc = attend_blocks(qc.reshape(Bc, Tc, GQA_KV_HEADS, GQA_GROUP, GQA_HEAD_DIM), kc, vc, scale) @ w_o
    return y, yc

def mla_mixer(h, hc, cos, sin, w_in, q_a_norm, q_b, kv_a_norm, kv_b, w_o, with_ctx_out):
    def project(t):
        B, T, _ = t.shape
        a = t @ w_in
        q_a = a[..., :MLA_Q_RANK]
        kv_a = a[..., MLA_Q_RANK:MLA_Q_RANK + MLA_KV_RANK]
        k_rope = a[..., MLA_Q_RANK + MLA_KV_RANK:][:, :, None, :]
        q = (rmsnorm(q_a, q_a_norm) @ q_b).reshape(B, T, MLA_HEADS, MLA_QK_DIM)
        kv = (rmsnorm(kv_a, kv_a_norm) @ kv_b).reshape(B, T, MLA_HEADS, MLA_NOPE_DIM + MLA_V_DIM)
        return q[..., :MLA_NOPE_DIM], q[..., MLA_NOPE_DIM:], kv[..., :MLA_NOPE_DIM], k_rope, kv[..., MLA_NOPE_DIM:]

    def assemble(q_nope, q_rope, k_nope, k_rope):
        q = jnp.concatenate([q_nope, q_rope], axis=-1)
        k = jnp.concatenate([k_nope, jnp.broadcast_to(k_rope, k_nope.shape[:3] + (MLA_ROPE_DIM,))], axis=-1)
        return q, k

    B, S, _ = h.shape
    q_nope, q_rope, k_nope, k_rope, v = project(h)
    q_rope = apply_rope(q_rope, cos, sin)
    k_rope = apply_rope(k_rope, cos, sin)
    q, k = assemble(q_nope, q_rope, k_nope, k_rope)
    qc_nope, qc_rope, kc_nope, kc_rope, vc = project(hc)
    qc, kc = assemble(qc_nope, qc_rope, kc_nope, kc_rope)
    scale = MLA_QK_DIM ** -0.5
    k_all = jnp.concatenate([kc, k], axis=1)
    v_all = jnp.concatenate([vc, v], axis=1)
    y = attend_blocks(q[:, :, :, None, :], k_all, v_all, scale) @ w_o
    yc = None
    if with_ctx_out:
        yc = attend_blocks(qc[:, :, :, None, :], kc, vc, scale) @ w_o
    return y, yc

def swiglu(h, w_gate_up, w_down):
    gu = h @ w_gate_up
    return (jax.nn.silu(gu[..., :D_FF]) * gu[..., D_FF:]) @ w_down

def setup_inputs(seed: int = 0) -> dict:
    key = jax.random.key(seed)
    ks = jax.random.split(key, 24)

    def nrm(k, shape, scale):
        return jax.random.normal(k, shape, jnp.float32) * scale

    D = D_MODEL
    return {
        "x": nrm(ks[0], (BATCH, SEQ, D), 1.0),
        "c": nrm(ks[1], (BATCH, D), 1.0),
        "ctx": nrm(ks[2], (BATCH, CTX_LEN, D), 1.0),
        "c_ctx": nrm(ks[3], (D,), 1.0),
        "norm1": 1.0 + nrm(ks[4], (DEPTH, D), 0.02),
        "norm2": 1.0 + nrm(ks[5], (DEPTH, D), 0.02),
        "w_mod": nrm(ks[6], (DEPTH, D, 6 * D), 0.5 * D ** -0.5),
        "b_mod": nrm(ks[7], (DEPTH, 6 * D), 0.02),
        "w_gate_up": nrm(ks[8], (DEPTH, D, 2 * D_FF), D ** -0.5),
        "w_down": nrm(ks[9], (DEPTH, D_FF, D), D_FF ** -0.5),
        "gqa_w_qkv": nrm(ks[10], (N_A, D, (GQA_HEADS + 2 * GQA_KV_HEADS) * GQA_HEAD_DIM), D ** -0.5),
        "gqa_q_norm": 1.0 + nrm(ks[11], (N_A, GQA_HEAD_DIM), 0.02),
        "gqa_k_norm": 1.0 + nrm(ks[12], (N_A, GQA_HEAD_DIM), 0.02),
        "gqa_w_o": nrm(ks[13], (N_A, GQA_HEADS * GQA_HEAD_DIM, D), (GQA_HEADS * GQA_HEAD_DIM) ** -0.5),
        "mla_w_in": nrm(ks[14], (N_B, D, MLA_Q_RANK + MLA_KV_RANK + MLA_ROPE_DIM), D ** -0.5),
        "mla_q_a_norm": 1.0 + nrm(ks[15], (N_B, MLA_Q_RANK), 0.02),
        "mla_q_b": nrm(ks[16], (N_B, MLA_Q_RANK, MLA_HEADS * MLA_QK_DIM), MLA_Q_RANK ** -0.5),
        "mla_kv_a_norm": 1.0 + nrm(ks[17], (N_B, MLA_KV_RANK), 0.02),
        "mla_kv_b": nrm(ks[18], (N_B, MLA_KV_RANK, MLA_HEADS * (MLA_NOPE_DIM + MLA_V_DIM)), MLA_KV_RANK ** -0.5),
        "mla_w_o": nrm(ks[19], (N_B, MLA_HEADS * MLA_V_DIM, D), (MLA_HEADS * MLA_V_DIM) ** -0.5),
        "final_norm": 1.0 + nrm(ks[20], (D,), 0.02),
    }

def reference(x, c, ctx, c_ctx, norm1, norm2, w_mod, b_mod, w_gate_up, w_down,
              gqa_w_qkv, gqa_q_norm, gqa_k_norm, gqa_w_o,
              mla_w_in, mla_q_a_norm, mla_q_b, mla_kv_a_norm, mla_kv_b, mla_w_o,
              final_norm):
    S = x.shape[1]
    rows = S // GRID_W
    cos_a, sin_a = axial_rope(rows, GQA_HEAD_DIM)
    cos_b, sin_b = axial_rope(rows, MLA_ROPE_DIM)
    sc = jax.nn.silu(c)
    scc = jax.nn.silu(c_ctx)
    xc = ctx
    for i in range(DEPTH):
        last = i == DEPTH - 1
        mod = sc @ w_mod[i] + b_mod[i]
        modc = scc @ w_mod[i] + b_mod[i]
        sh1, s1, g1, sh2, s2, g2 = [m[:, None, :] for m in jnp.split(mod, 6, axis=-1)]
        sh1c, s1c, g1c, sh2c, s2c, g2c = jnp.split(modc, 6, axis=-1)
        h = modulate(rmsnorm(x, norm1[i]), sh1, s1)
        hc = modulate(rmsnorm(xc, norm1[i]), sh1c, s1c)
        j = i // N_MIXERS
        if i % N_MIXERS == 0:
            y, yc = gqa_mixer(h, hc, cos_a, sin_a, gqa_w_qkv[j], gqa_q_norm[j], gqa_k_norm[j], gqa_w_o[j],
                              not last)
        else:
            y, yc = mla_mixer(h, hc, cos_b, sin_b, mla_w_in[j], mla_q_a_norm[j], mla_q_b[j],
                              mla_kv_a_norm[j], mla_kv_b[j], mla_w_o[j], not last)
        x = x + g1 * y
        x = x + g2 * swiglu(modulate(rmsnorm(x, norm2[i]), sh2, s2), w_gate_up[i], w_down[i])
        if not last:
            xc = xc + g1c * yc
            xc = xc + g2c * swiglu(modulate(rmsnorm(xc, norm2[i]), sh2c, s2c), w_gate_up[i], w_down[i])
    return rmsnorm(x, final_norm)


_drawn_inputs = setup_inputs


def setup_inputs(seed=0):
    import zlib

    import numpy as np

    out = dict(_drawn_inputs(seed))
    spreads = {}
    factors = {'ctx': 5.906,
     'norm1': 8.0,
     'norm2': 6.318,
     'gqa_q_norm': 8.0,
     'gqa_k_norm': 8.0,
     'mla_q_a_norm': 8.0,
     'mla_kv_a_norm': 8.0,
     'final_norm': 2.963}
    for name, (base, spread) in spreads.items():
        noise = np.random.default_rng([zlib.crc32(name.encode()), seed]).standard_normal(out[name].shape)
        drawn = base * np.exp(spread * noise) if base else spread * noise
        out[name] = __import__('jax').numpy.asarray(drawn.astype(out[name].dtype))
    for name, factor in factors.items():
        out[name] = (out[name] * factor).astype(out[name].dtype)
    return out
```

```python
from contextlib import ExitStack

import concourse.bass as bass
import numpy as np
from concourse import mybir

F32 = mybir.dt.float32
F32R = mybir.dt.float32r
ALU = mybir.AluOpType
ACT = mybir.ActivationFunctionType
AX_X = mybir.AxisListType.X

P = 128
D = 1024
KD = D // P
CTX = 256
SEQ = 1024
TOK = CTX + SEQ
NKT = TOK // P
DFF = 2816
NFF = DFF // P
HEADS = 16
GQA_HD = 64
GQA_KV = 4
NOPE = 64
ROPE = 32
QK_MLA = NOPE + ROPE
V_DIM = 64
Q_RANK = 384
KV_RANK = 256
W_IN_TILES = 6
GRID_W = 64
EPS = 1e-6
BANK = 512
MOD_COLS = 6 * KD

LAT_CHUNKS = ((256, 512), (768, 512))
ALL_CHUNKS = LAT_CHUNKS + ((0, 256),)


def stream_of(chunk):
    return 0 if chunk[0] >= CTX else 1


def semaphores(nc, ctx, tag):
    taken = []

    def sem(name):
        taken.append(nc.alloc_semaphore(tag + name))
        return taken[-1]

    def give_back():
        nc.clear_and_free_semaphores(taken)
        nc.all_engine_barrier(sem_only=True)

    ctx.callback(give_back)
    return sem


def modulation(nc, g, layer):
    n_chunks = 12
    with ExitStack() as ctx:
        tag = f"mod{layer}_"
        sb = lambda n, s, d=F32: ctx.enter_context(nc.sbuf_tensor(tag + n, s, d))
        ps = lambda n, s, d=F32: ctx.enter_context(nc.psum_tensor(tag + n, s, d))
        sem = semaphores(nc, ctx, tag)
        w_slot = sb("w_slot", [P, 2, KD, BANK])
        rows = sb("rows", [2, 2, BANK])
        row_ps = ps("row_ps", [2, 2, BANK])
        col_ps = ps("col_ps", [P, 2, 512])
        w_loaded = [sem("w_loaded0"), sem("w_loaded1")]
        rows_done, row_copied, turned, mod_added = (
            sem("rows_done"), sem("row_copied"), sem("turned"), sem("mod_added"))
        affine = sem("affine")
        block = ctx.enter_context(nc.Block(no_gpsimd_drain=True))

        @block.sync
        def _(sp):
            with sp.Fori(0, n_chunks // 2) as i:
                for u in range(2):
                    sp.wait_ge(rows_done, 2 * i + u + 1)
                    sp.dma_start(
                        w_slot[:, u].rearrange("p k n -> p (k n)"),
                        g.w_mod[layer][bass.ds(2 * i + u, 1)].rearrange("a p n -> p (a n)"),
                    ).then_inc(w_loaded[u], 16)

        @block.tensor
        def _(pe):
            pe.sem_inc(rows_done, 2)
            with pe.Fori(0, n_chunks // 2) as i:
                for u in range(2):
                    pe.wait_ge(w_loaded[u], 16 * i + 16)
                    for k in range(KD):
                        last = nc.tensor.matmul(row_ps[:, u, :], g.silu_c[:, k, :], w_slot[:, u, k, :],
                                                start=(k == 0), stop=(k == KD - 1))
                    last.then_inc(rows_done, 1)
                    pe.wait_ge(row_copied, 2 * i + u + 1)
                    pe.wait_ge(mod_added, 2 * i + u + 1)
                    for j in range(4):
                        last = nc.tensor.matmul(col_ps[:, u, 2 * j:2 * j + 2], rows[:, u, j * P:(j + 1) * P],
                                                g.ident[0:2, 0:2], start=True, stop=True)
                    last.then_inc(turned, 1)

        @block.vector
        def _(dve):
            dve.sem_inc(mod_added, 2)
            with dve.Fori(0, n_chunks // 2) as i:
                for u in range(2):
                    dve.wait_ge(rows_done, 2 * i + u + 3)
                    nc.vector.tensor_copy(rows[:, u, :], row_ps[:, u, :]).then_inc(row_copied, 1)
                    dve.wait_ge(turned, 2 * i + u + 1)
                    nc.vector.tensor_tensor(
                        g.mod_t[:, bass.ds(8 * i + 4 * u, 4), :],
                        col_ps[:, u, 0:8].rearrange("p (j s) -> p j s", s=2),
                        g.b_mod[:, layer, bass.ds(8 * i + 4 * u, 4), :], ALU.add,
                    ).then_inc(mod_added, 1)
            dve.wait_ge(mod_added, 2 + n_chunks)
            for j, gain in ((0, g.gain1), (1, g.gain2)):
                scale = g.mod_t[:, (3 * j + 1) * KD:(3 * j + 2) * KD, :]
                nc.vector.tensor_scalar(gain[:, :, :], scale, 1.0, None, ALU.add).then_inc(affine, 1)
            dve.wait_ge(affine, 2)
            for j, gain in ((0, g.gain1), (1, g.gain2)):
                nc.vector.tensor_tensor(gain[:, :, :], gain[:, :, :], g.norms[:, layer, j, :, :],
                                        ALU.mult).then_inc(affine, 1)


def norm(nc, g, tag, src, n_k, gain, shift, out_hi, out_lo, chunks, out_dram=None):
    width = n_k * P
    with ExitStack() as ctx:
        sb = lambda n, s, d=F32: ctx.enter_context(nc.sbuf_tensor(tag + n, s, d))
        sem = semaphores(nc, ctx, tag)
        squares = sb("squares", [P, 2, BANK])
        root = sb("root", [P, 2, BANK])
        rinv = sb("rinv", [P, 2, BANK])
        n_t = 4
        scaled = sb("scaled", [P, n_t, BANK])
        ssq = ctx.enter_context(nc.psum_tensor(tag + "ssq", [P, 2, BANK], F32))
        sq_ready, ssq_added, root_ready, rinv_ready = (
            sem("sq_ready"), sem("ssq_added"), sem("root_ready"), sem("rinv_ready"))
        t_ready, hi_ready, lo_ready = sem("t_ready"), sem("hi_ready"), sem("lo_ready")
        stored = [sem(f"stored{j}") for j in range(n_t)] if out_dram is not None else None
        n_c = len(chunks)
        block = ctx.enter_context(nc.Block(no_gpsimd_drain=True))

        @block.scalar
        def _(act):
            def square_chunk(ci):
                t0, n = chunks[ci]
                for k in range(n_k):
                    s = ci * n_k + k
                    if s >= 2:
                        act.wait_ge(ssq_added, s - 1)
                    nc.scalar.activation(squares[:, s % 2, 0:n], src[:, k, t0:t0 + n],
                                         ACT.Square).then_inc(sq_ready, 1)

            def root_chunk(ci):
                n = chunks[ci][1]
                act.wait_ge(ssq_added, (ci + 1) * n_k)
                if ci >= 2:
                    act.wait_ge(rinv_ready, ci - 1)
                nc.scalar.activation(root[:, ci % 2, 0:n], ssq[:, ci % 2, 0:n], ACT.Sqrt,
                                     bias=g.eps[:, 0:1], scale=1.0 / width).then_inc(root_ready, 1)

            def hi_chunk(ci):
                if out_dram is not None:
                    return
                t0, n = chunks[ci]
                for k in range(n_k):
                    s = ci * n_k + k
                    act.wait_ge(t_ready, s + 1)
                    bias = shift(k, stream_of(chunks[ci])) if shift else 0.0
                    nc.scalar.activation(out_hi[:, k, t0:t0 + n], scaled[:, s % n_t, 0:n], ACT.Identity,
                                         bias=bias).then_inc(hi_ready, 1)

            for ci in range(n_c):
                square_chunk(ci)
                if ci:
                    hi_chunk(ci - 1)
                root_chunk(ci)
            hi_chunk(n_c - 1)

        @block.tensor
        def _(pe):
            for ci, (_, n) in enumerate(chunks):
                if ci >= 2:
                    pe.wait_ge(root_ready, ci - 1)
                for k in range(n_k):
                    pe.wait_ge(sq_ready, ci * n_k + k + 1)
                    nc.tensor.matmul(ssq[:, ci % 2, 0:n], g.ones[:, :], squares[:, (ci * n_k + k) % 2, 0:n],
                                     start=(k == 0), stop=(k == n_k - 1)).then_inc(ssq_added, 1)

        @block.vector
        def _(dve):
            def lo_of(s):
                ci, k = divmod(s, n_k)
                t0, n = chunks[ci]
                dve.wait_ge(hi_ready, s + 1)
                hi = out_hi[:, k, t0:t0 + n].bitcast(F32)
                lo = out_lo[:, k, t0:t0 + n]
                t = scaled[:, s % n_t, 0:n]
                if shift:
                    nc.vector.scalar_tensor_tensor(lo, t, shift(k, stream_of(chunks[ci])), hi,
                                                   ALU.add, ALU.subtract).then_inc(lo_ready, 1)
                else:
                    nc.vector.tensor_tensor(lo, t, hi, ALU.subtract).then_inc(lo_ready, 1)

            for ci, (t0, n) in enumerate(chunks):
                dve.wait_ge(root_ready, ci + 1)
                if ci >= 2:
                    dve.wait_ge(t_ready, (ci - 1) * n_k)
                nc.vector.reciprocal(rinv[:, ci % 2, 0:n], root[:, ci % 2, 0:n]).then_inc(rinv_ready, 1)
                dve.wait_ge(rinv_ready, ci + 1)
                for k in range(n_k):
                    s = ci * n_k + k
                    if out_dram is not None and s >= n_t:
                        dve.wait_ge(stored[s % n_t], 16 * (s // n_t))
                    if out_dram is None and s >= n_t:
                        dve.wait_ge(lo_ready, s - n_t + 1)
                    nc.vector.scalar_tensor_tensor(
                        scaled[:, s % n_t, 0:n], src[:, k, t0:t0 + n], gain(k, stream_of(chunks[ci])),
                        rinv[:, ci % 2, 0:n], ALU.mult, ALU.mult).then_inc(t_ready, 1)
                    if out_dram is None and s >= 2:
                        lo_of(s - 2)
            if out_dram is None:
                for s in range(max(0, n_c * n_k - 2), n_c * n_k):
                    lo_of(s)

        if out_dram is not None:
            @block.sync
            def _(sp):
                for s in range(n_c * n_k):
                    ci, k = divmod(s, n_k)
                    t0, n = chunks[ci]
                    sp.wait_ge(t_ready, s + 1)
                    sp.dma_start(out_dram[k * P:(k + 1) * P, t0 - CTX:t0 - CTX + n],
                                 scaled[:, s % n_t, 0:n]).then_inc(stored[s % n_t], 16)
                for j in range(n_t):
                    sp.wait_ge(stored[j], 16 * len(range(j, n_c * n_k, n_t)))


class Split:

    def __init__(self, nc, ctx, tag, n_k, sem, slots=2):
        self.nc, self.n_k, self.slots = nc, n_k, slots
        width = n_k * P
        self.raw = ctx.enter_context(nc.sbuf_tensor(tag + "w_raw", [P, slots, width], F32))
        self.hi = ctx.enter_context(nc.sbuf_tensor(tag + "w_hi", [P, slots, width], F32R))
        self.lo = ctx.enter_context(nc.sbuf_tensor(tag + "w_lo", [P, slots, width], F32R))
        self.loaded = [sem(f"w_loaded{j}") for j in range(slots)]
        self.hi_done = sem("w_hi_done")
        self.lo_done = sem("w_lo_done")

    def passes(self, slot, k, x_hi, x_lo):
        w_hi, w_lo = (x[:, slot, k * P:(k + 1) * P] for x in (self.hi, self.lo))
        return ((w_hi, x_hi), (w_hi, x_lo), (w_lo, x_hi))

    def high(self, slot):
        return self.nc.scalar.copy(self.hi[:, slot, :], self.raw[:, slot, :]).then_inc(self.hi_done, 1)

    def low(self, slot):
        return self.nc.gpsimd.tensor_tensor(self.lo[:, slot, :], self.raw[:, slot, :],
                                            self.hi[:, slot, :].bitcast(F32), ALU.subtract
                                            ).then_inc(self.lo_done, 1)


def project(nc, g, tag, w_dram, src_hi, src_lo, n_k, n_tiles, chunks, mode, dst, scale=1.0, gains=None,
            turn=None, cos=None, sin=None):
    n_c = len(chunks)
    per = 2 * n_c
    n_bodies = n_tiles // 2
    assert n_tiles % 2 == 0
    rotated = mode != "plain"
    normed = mode == "norm_rope"
    with ExitStack() as ctx:
        sb = lambda n, s, d=F32: ctx.enter_context(nc.sbuf_tensor(tag + n, s, d))
        ps = lambda n, s, d=F32: ctx.enter_context(nc.psum_tensor(tag + n, s, d))
        sem = semaphores(nc, ctx, tag)
        w = Split(nc, ctx, tag, n_k, sem)
        hi_out = sb("hi_out", [P, 2, BANK], F32R)
        lo_out = sb("lo_out", [P, 2, BANK], F32R)
        acc = ps("acc", [P, 2, 3, BANK])
        acc_done = sem("acc_done")
        hi_done, lo_done = sem("hi_done"), sem("lo_done")
        lo_start = 0 if rotated else per
        stored = [sem("stored0"), sem("stored1")]
        if rotated:
            aux = ps("aux", [P, 2, BANK])
            base = sb("base", [P, 2, BANK])
            with_cos = sb("with_cos", [P, 2, BANK])
            with_sin = sb("with_sin", [P, 2, BANK])
            whole = sb("whole", [P, 2, BANK])
            base_done, cos_done, turn_done, sin_done, whole_done = (
                sem("base_done"), sem("cos_done"), sem("turn_done"), sem("sin_done"), sem("whole_done"))
        if normed:
            squares = sb("squares", [P, 2, BANK])
            root = sb("root", [P, 2, BANK])
            rinv = sb("rinv", [P, 2, BANK])
            sq_done, ssq_done, root_done, rinv_done = (
                sem("sq_done"), sem("ssq_done"), sem("root_done"), sem("rinv_done"))
        acc_free = base_done if rotated else lo_done
        block = ctx.enter_context(nc.Block(no_gpsimd_drain=True))

        @block.sync
        def _(sp):
            sp.sem_inc(stored[0], 16)
            sp.sem_inc(stored[1], 16)

            def load(i):
                for u in range(2):
                    sp.wait_ge(w.lo_done, 2 * i + u + 1)
                    sp.dma_start(w.raw[:, u, :], w_dram[bass.ds(2 * i + u, 1)].rearrange("a p n -> p (a n)")
                                 ).then_inc(w.loaded[u], 16)

            def store(i):
                for b in range(per):
                    u, c = divmod(b, n_c)
                    t0, n = chunks[c]
                    sp.wait_ge(lo_done, per * i + b + 1 + lo_start)
                    for part, tile in ((1, lo_out), (0, hi_out)):
                        sp.dma_start(dst(part, 2 * i + u, t0, n), tile[:, b % 2, 0:n].bitcast(F32)).then_inc(stored[b % 2], 16)

            load(0)
            if n_bodies > 1:
                with sp.Fori(0, n_bodies - 1) as i:
                    load(i + 1)
                    store(i)
            store(n_bodies - 1)
            for j in range(2):
                sp.wait_ge(stored[j], 16 + 32 * (per // 2) * n_bodies)

        @block.tensor
        def _(pe):
            pe.sem_inc(acc_done, per)
            with pe.Fori(0, n_bodies) as i:
                def main(b):
                    u, c = divmod(b, n_c)
                    t0, n = chunks[c]
                    if c == 0:
                        pe.wait_ge(w.lo_done, 2 * i + u + 3)
                    pe.wait_ge(acc_free, per * i + b + 1)
                    for k in range(n_k):
                        for j, (a, x) in enumerate(w.passes(u, k, src_hi[:, k, t0:t0 + n], src_lo[:, k, t0:t0 + n])):
                            last = nc.tensor.matmul(acc[:, u, c, 0:n], a, x, start=(k == 0 and j == 0),
                                                    stop=(k == n_k - 1 and j == 2))
                    last.then_inc(acc_done, 1)

                def head_sums(b):
                    n = chunks[b % n_c][1]
                    pe.wait_ge(sq_done, per * i + b + 1)
                    pe.wait_ge(root_done, per * i + b + 1)
                    nc.tensor.matmul(aux[:, 0, 0:n], g.head_ones[:, :], squares[:, b % 2, 0:n], start=True,
                                     stop=True).then_inc(ssq_done, 1)

                def turned(b):
                    n = chunks[b % n_c][1]
                    pe.wait_ge(base_done, per * i + b + 1 + per)
                    pe.wait_ge(sin_done, per * i + b + 1)
                    nc.tensor.matmul(aux[:, 1, 0:n], turn[:, :], base[:, b % 2, 0:n], start=True,
                                     stop=True).then_inc(turn_done, 1)

                for b in range(per + (2 if rotated else 0)):
                    if b < per:
                        main(b)
                    if normed and 1 <= b <= per:
                        head_sums(b - 1)
                    if rotated and b >= 2:
                        turned(b - 2)

        @block.scalar
        def _(act):
            if normed:
                act.sem_inc(root_done, 1)

            def split(i, u):
                act.wait_ge(w.loaded[u], 16 * i + 16)
                act.wait_ge(acc_done, per * i + n_c * (u + 1))
                w.high(u)

            def square(i, b):
                u, c = divmod(b, n_c)
                n = chunks[c][1]
                act.wait_ge(acc_done, per * i + b + 1 + per)
                nc.scalar.activation(squares[:, b % 2, 0:n], acc[:, u, c, 0:n], ACT.Square).then_inc(sq_done, 1)

            def take_root(i, b):
                n = chunks[b % n_c][1]
                act.wait_ge(ssq_done, per * i + b + 1)
                nc.scalar.activation(root[:, b % 2, 0:n], aux[:, 0, 0:n], ACT.Sqrt, bias=g.eps[:, 0:1],
                                     scale=1.0 / GQA_HD).then_inc(root_done, 1)

            def high(i, b):
                u, c = divmod(b, n_c)
                n = chunks[c][1]
                act.wait_ge(stored[b % 2], 32 * ((per // 2) * i + b // 2) + 16)
                if rotated:
                    act.wait_ge(whole_done, per * i + b + 1)
                    nc.scalar.copy(hi_out[:, b % 2, 0:n], whole[:, b % 2, 0:n]).then_inc(hi_done, 1)
                else:
                    act.wait_ge(acc_done, per * i + b + 1 + per)
                    nc.scalar.mul(hi_out[:, b % 2, 0:n], acc[:, u, c, 0:n], scale).then_inc(hi_done, 1)

            def body(i, more):
                for b in range(per + 2):
                    if more and b in (n_c, per):
                        split(i + 1, b // n_c - 1)
                    if normed and b < per:
                        square(i, b)
                    if normed and 1 <= b <= per:
                        take_root(i, b - 1)
                    if rotated and b >= 2:
                        high(i, b - 2)
                    if not rotated and b < per:
                        high(i, b)

            split(0, 0)
            split(0, 1)
            if n_bodies > 1:
                with act.Fori(0, n_bodies - 1) as i:
                    body(i, True)
            body(n_bodies - 1, False)

        @block.gpsimd
        def _(pool):
            pool.sem_inc(w.lo_done, 2)

            def split(i, u):
                pool.wait_ge(w.hi_done, 2 * i + u + 1)
                w.low(u)

            def cosine(i, b):
                t0, n = chunks[b % n_c]
                pool.wait_ge(base_done, per * i + b + 1 + per)
                nc.gpsimd.tensor_tensor(with_cos[:, b % 2, 0:n], base[:, b % 2, 0:n], cos[:, t0:t0 + n],
                                        ALU.mult).then_inc(cos_done, 1)

            def add(i, b):
                n = chunks[b % n_c][1]
                pool.wait_ge(cos_done, per * i + b + 1)
                pool.wait_ge(sin_done, per * i + b + 2)
                nc.gpsimd.tensor_tensor(whole[:, b % 2, 0:n], with_cos[:, b % 2, 0:n],
                                        with_sin[:, b % 2, 0:n], ALU.add).then_inc(whole_done, 1)

            def low(i, b):
                n = chunks[b % n_c][1]
                pool.wait_ge(hi_done, per * i + b + 1)
                nc.gpsimd.tensor_tensor(lo_out[:, b % 2, 0:n], whole[:, b % 2, 0:n],
                                        hi_out[:, b % 2, 0:n].bitcast(F32), ALU.subtract).then_inc(lo_done, 1)
                pool.wait_ge(lo_done, per * i + b + 1)

            def body(i, more):
                for b in range(per + 1):
                    if more and b in (n_c, per):
                        split(i + 1, b // n_c - 1)
                    if rotated:
                        if b < per:
                            cosine(i, b)
                        if b >= 1:
                            low(i, b - 1)
                        if b < per:
                            add(i, b)

            split(0, 0)
            split(0, 1)
            if n_bodies > 1:
                with pool.Fori(0, n_bodies - 1) as i:
                    body(i, True)
            if rotated:
                body(n_bodies - 1, False)

        @block.vector
        def _(dve):
            dve.sem_inc(acc_free, per)
            if rotated:
                dve.sem_inc(sin_done, 1)
            with dve.Fori(0, n_bodies) as i:
                def make_base(b):
                    u, c = divmod(b, n_c)
                    n = chunks[c][1]
                    if normed:
                        dve.wait_ge(root_done, per * i + b + 2)
                        nc.vector.reciprocal(rinv[:, b % 2, 0:n], root[:, b % 2, 0:n]).then_inc(rinv_done, 1)
                        dve.wait_ge(rinv_done, per * i + b + 1)
                        nc.vector.scalar_tensor_tensor(base[:, b % 2, 0:n], acc[:, u, c, 0:n],
                                                       gains[:, bass.ds(2 * i + u, 1)], rinv[:, b % 2, 0:n],
                                                       ALU.mult, ALU.mult).then_inc(base_done, 1)
                    else:
                        dve.wait_ge(acc_done, per * i + b + 1 + per)
                        nc.vector.tensor_scalar(base[:, b % 2, 0:n], acc[:, u, c, 0:n], scale, None,
                                                ALU.mult).then_inc(base_done, 1)

                def sine(b):
                    t0, n = chunks[b % n_c]
                    dve.wait_ge(cos_done, per * i + b + 1)
                    dve.wait_ge(turn_done, per * i + b + 1)
                    nc.vector.tensor_tensor(with_sin[:, b % 2, 0:n], aux[:, 1, 0:n], sin[:, t0:t0 + n],
                                            ALU.mult).then_inc(sin_done, 1)

                for b in range(per + (1 if rotated else 0)):
                    if rotated:
                        if b < per:
                            make_base(b)
                        if b >= 1:
                            sine(b - 1)
                    else:
                        u, c = divmod(b, n_c)
                        n = chunks[c][1]
                        dve.wait_ge(hi_done, per * i + b + 1)
                        nc.vector.scalar_tensor_tensor(lo_out[:, b % 2, 0:n], acc[:, u, c, 0:n], scale,
                                                       hi_out[:, b % 2, 0:n].bitcast(F32), ALU.mult,
                                                       ALU.subtract).then_inc(lo_done, 1)


def accumulate(nc, g, tag, w_dram, src_hi, src_lo, n_k, n_tiles, chunks, dst, gate=None):
    n_c = len(chunks)
    per = 2 * n_c
    n_bodies = n_tiles // 2
    with ExitStack() as ctx:
        sem = semaphores(nc, ctx, tag)
        w = Split(nc, ctx, tag, n_k, sem)
        acc = ctx.enter_context(nc.psum_tensor(tag + "acc", [P, 2, 3, BANK], F32))
        acc_done, added = sem("acc_done"), sem("added")
        block = ctx.enter_context(nc.Block(no_gpsimd_drain=True))

        @block.sync
        def _(sp):
            with sp.Fori(0, n_bodies) as i:
                for u in range(2):
                    sp.wait_ge(w.lo_done, 2 * i + u + 1)
                    sp.dma_start(w.raw[:, u, :], w_dram[bass.ds(2 * i + u, 1)].rearrange("a p n -> p (a n)")
                                 ).then_inc(w.loaded[u], 16)

        @block.scalar
        def _(act):
            with act.Fori(0, n_bodies) as i:
                for u in range(2):
                    act.wait_ge(w.loaded[u], 16 * i + 16)
                    act.wait_ge(acc_done, per * i + n_c * (u + 1))
                    w.high(u)

        @block.gpsimd
        def _(pool):
            pool.sem_inc(w.lo_done, 2)
            with pool.Fori(0, n_bodies) as i:
                for u in range(2):
                    pool.wait_ge(w.hi_done, 2 * i + u + 1)
                    w.low(u)

        @block.tensor
        def _(pe):
            pe.sem_inc(acc_done, per)
            with pe.Fori(0, n_bodies) as i:
                for u in range(2):
                    pe.wait_ge(w.lo_done, 2 * i + u + 3)
                    for c, (t0, n) in enumerate(chunks):
                        pe.wait_ge(added, per * i + n_c * u + c + 1)
                        for k in range(n_k):
                            for j, (a, x) in enumerate(
                                    w.passes(u, k, src_hi[:, k, t0:t0 + n], src_lo[:, k, t0:t0 + n])):
                                last = nc.tensor.matmul(acc[:, u, c, 0:n], a, x, start=(k == 0 and j == 0),
                                                        stop=(k == n_k - 1 and j == 2))
                        last.then_inc(acc_done, 1)

        @block.vector
        def _(dve):
            dve.sem_inc(added, per)
            with dve.Fori(0, n_bodies) as i:
                for u in range(2):
                    for c, (t0, n) in enumerate(chunks):
                        dve.wait_ge(acc_done, per * i + n_c * u + c + 1 + per)
                        out = dst[:, bass.ds(2 * i + u, 1), t0:t0 + n].rearrange("p a n -> p (a n)")
                        if gate:
                            nc.vector.scalar_tensor_tensor(out, acc[:, u, c, 0:n], gate(2 * i + u, stream_of(chunks[c])),
                                                           out, ALU.mult, ALU.add).then_inc(added, 1)
                        else:
                            nc.vector.tensor_copy(out, acc[:, u, c, 0:n]).then_inc(added, 1)


def values(nc, g, tag, w_dram, src_hi, src_lo, n_k, n_tiles, dst):
    n_c = len(ALL_CHUNKS)
    per = 2 * n_c
    n_bodies = n_tiles // 2
    groups = ((0, 4), (4, 4), (8, 2))
    n_g = len(groups)
    with ExitStack() as ctx:
        sb = lambda n, s, d=F32: ctx.enter_context(nc.sbuf_tensor(tag + n, s, d))
        sem = semaphores(nc, ctx, tag)
        w = Split(nc, ctx, tag, n_k, sem)
        v_t = sb("v_t", [P, 2, TOK])
        v_out = sb("v_out", [P, 2, 2, NKT, P], F32R)
        acc = ctx.enter_context(nc.psum_tensor(tag + "acc", [P, 2, 3, BANK], F32))
        turned_ps = ctx.enter_context(nc.psum_tensor(tag + "turned", [P, 2, BANK], F32))
        acc_done, copied, turned, v_hi, v_lo = (
            sem("acc_done"), sem("copied"), sem("turned"), sem("v_hi"), sem("v_lo"))
        stored = [sem("stored0"), sem("stored1")]
        block = ctx.enter_context(nc.Block(no_gpsimd_drain=True))

        @block.sync
        def _(sp):
            for u in range(2):
                sp.sem_inc(stored[u], 16)

            def load(i):
                for u in range(2):
                    sp.wait_ge(w.lo_done, 2 * i + u + 1)
                    sp.dma_start(w.raw[:, u, :], w_dram[bass.ds(2 * i + u, 1)].rearrange("a p n -> p (a n)")
                                 ).then_inc(w.loaded[u], 16)

            def store(i):
                for u in range(2):
                    sp.wait_ge(v_lo, 2 * n_g * i + n_g * (u + 1) + 2)
                    for h in range(2):
                        sp.dma_start(dst[bass.ds(4 * i + 2 * u + h, 1)].rearrange("a p n -> p (a n)"),
                                     v_out[:, u, h].rearrange("p k n -> p (k n)").bitcast(F32)).then_inc(stored[u], 16)

            load(0)
            if n_bodies > 1:
                with sp.Fori(0, n_bodies - 1) as i:
                    load(i + 1)
                    store(i)
            store(n_bodies - 1)
            for u in range(2):
                sp.wait_ge(stored[u], 16 + 32 * n_bodies)

        @block.gpsimd
        def _(pool):
            pool.sem_inc(w.lo_done, 2)
            with pool.Fori(0, n_bodies) as i:
                for u in range(2):
                    pool.wait_ge(w.hi_done, 2 * i + u + 1)
                    w.low(u)

        @block.tensor
        def _(pe):
            pe.sem_inc(acc_done, per)
            with pe.Fori(0, n_bodies) as i:
                for u in range(2):
                    pe.wait_ge(w.lo_done, 2 * i + u + 3)
                    for c, (t0, n) in enumerate(ALL_CHUNKS):
                        pe.wait_ge(copied, per * i + n_c * u + c + 1)
                        for k in range(n_k):
                            for j, (a, x) in enumerate(
                                    w.passes(u, k, src_hi[:, k, t0:t0 + n], src_lo[:, k, t0:t0 + n])):
                                last = nc.tensor.matmul(acc[:, u, c, 0:n], a, x, start=(k == 0 and j == 0),
                                                        stop=(k == n_k - 1 and j == 2))
                        last.then_inc(acc_done, 1)
                for u in range(2):
                    pe.wait_ge(copied, per * i + n_c * (u + 1) + per)
                    for q, (k0, m) in enumerate(groups):
                        pe.wait_ge(v_lo, 2 * n_g * i + n_g * u + q + 1)
                        for k in range(k0, k0 + m):
                            last = nc.tensor.transpose(turned_ps[:, (n_g * u + q) % 2, (k - k0) * P:(k - k0 + 1) * P],
                                                       v_t[:, u, k * P:(k + 1) * P], g.ident[:, :])
                        last.then_inc(turned, 1)

        def turned_view(u, q, m):
            return turned_ps[:, (n_g * u + q) % 2, 0:m * P].rearrange("p (k h f) -> p h k f", h=2, f=V_DIM)

        @block.scalar
        def _(act):
            def split(i, u):
                act.wait_ge(w.loaded[u], 16 * i + 16)
                act.wait_ge(acc_done, per * i + n_c * (u + 1))
                w.high(u)

            def body(i, more):
                if more:
                    split(i + 1, 0)
                    split(i + 1, 1)
                for u in range(2):
                    for q, (k0, m) in enumerate(groups):
                        if q == 0:
                            act.wait_ge(stored[u], 32 * i + 16)
                        act.wait_ge(turned, 2 * n_g * i + n_g * u + q + 1)
                        nc.scalar.copy(v_out[:, u, :, k0:k0 + m, 0:V_DIM], turned_view(u, q, m)).then_inc(v_hi, 1)

            split(0, 0)
            split(0, 1)
            if n_bodies > 1:
                with act.Fori(0, n_bodies - 1) as i:
                    body(i, True)
            body(n_bodies - 1, False)

        @block.vector
        def _(dve):
            dve.sem_inc(copied, per)
            dve.sem_inc(v_lo, 2)
            with dve.Fori(0, n_bodies) as i:
                for u in range(2):
                    for c, (t0, n) in enumerate(ALL_CHUNKS):
                        dve.wait_ge(acc_done, per * i + n_c * u + c + 1 + per)
                        nc.vector.tensor_copy(v_t[:, u, t0:t0 + n], acc[:, u, c, 0:n]).then_inc(copied, 1)
                for u in range(2):
                    for q, (k0, m) in enumerate(groups):
                        dve.wait_ge(v_hi, 2 * n_g * i + n_g * u + q + 1)
                        nc.vector.tensor_tensor(v_out[:, u, :, k0:k0 + m, V_DIM:2 * V_DIM], turned_view(u, q, m),
                                                v_out[:, u, :, k0:k0 + m, 0:V_DIM].bitcast(F32), ALU.subtract
                                                ).then_inc(v_lo, 1)


def attention(nc, g, tag, load_q, load_k, load_v, rows, passes, out_dram):
    n_bodies = HEADS // 2
    scores_at = {1: (1, 2), 4: (1, 3), 6: (2, 0), 9: (2, 1)}
    exp_at = {1: (1, 1), 4: (1, 2), 6: (1, 3), 9: (2, 0)}
    inverse_at = {2: (1, 1), 5: (1, 2), 7: (1, 3), 10: (2, 0)}
    early = [(0, 0), (0, 1), (0, 2), (0, 3), (1, 0), (1, 1)]
    with ExitStack() as ctx:
        sb = lambda n, s, d=F32: ctx.enter_context(nc.sbuf_tensor(tag + n, s, d))
        ps = lambda n, s, d=F32: ctx.enter_context(nc.psum_tensor(tag + n, s, d))
        sem = semaphores(nc, ctx, tag)
        n_qp = 1 + max(a for a, _ in passes)
        q_s = sb("q_s", [P, 2, n_qp, BANK], F32R)
        k_s = sb("k_s", [P, 2, 2, TOK], F32R)
        v_s = sb("v_s", [P, 2, NKT, P], F32R)
        prob = sb("prob", [P, 12, TOK])
        pt_hi = sb("pt_hi", [P, 2, BANK], F32R)
        pt_lo = sb("pt_lo", [P, 2, BANK], F32R)
        max_parts = sb("max_parts", [P, 2, 2])
        neg_max = sb("neg_max", [P, 2, 4])
        total_parts = sb("total_parts", [P, 2, 4, 2])
        total = sb("total", [P, 2, 4])
        r_total = sb("r_total", [P, 2, 4])
        o_a = sb("o_a", [V_DIM, 2, BANK])
        o_b = sb("o_b", [V_DIM, 2, BANK])
        o_sum = sb("o_sum", [V_DIM, 2, BANK])
        o_hi = sb("o_hi", [V_DIM, 2, BANK], F32R)
        o_lo = sb("o_lo", [V_DIM, 2, BANK], F32R)
        lat_ps = ps("lat_ps", [P, 2, 2, BANK])
        ctx_ps = ps("ctx_ps", [P, BANK])
        t_ps = ps("t_ps", [P, 2, BANK])
        o_ps = ps("o_ps", [P, BANK])
        q_loaded = [sem("q_loaded0"), sem("q_loaded1")]
        k_loaded = [sem("k_loaded0"), sem("k_loaded1")]
        v_loaded = [sem("v_loaded0"), sem("v_loaded1")]
        ctx_scored, lat_scored, max_part, max_done, ctx_exp, lat_exp, total_done, r_done, normed = (
            sem("ctx_scored"), sem("lat_scored"), sem("max_part"), sem("max_done"), sem("ctx_exp"),
            sem("lat_exp"), sem("total_done"), sem("r_done"), sem("normed"))
        turned, hi_done, lo_done, pv_step = sem("turned"), sem("hi_done"), sem("lo_done"), sem("pv_step")
        o_read, o_added, o_high, o_out = sem("o_read"), sem("o_added"), sem("o_high"), sem("o_out")
        stored = [sem("stored0"), sem("stored1")]
        n_q, n_k = len(load_q(0, 0, CTX)), len(load_k(0, 0))
        block = ctx.enter_context(nc.Block(no_gpsimd_drain=True))

        def prob_tile(un, q):
            return prob[:, (un % 4) * 2 + q if q < 2 else 8 + (un % 2) * 2 + q - 2, :]

        def steps(more, step):
            for un in range(4):
                for k in range(1, NKT + 1):
                    step(un, k, k < NKT or un < 3 or more)

        def tile_at(table, un, k, more):
            if k not in table:
                return None
            ahead, q = table[k]
            return (un + ahead, q) if un + ahead < 4 or more else None

        @block.sync
        def _(sp):
            for j in range(2):
                sp.sem_inc(stored[j], 16)

            def get_q(i, un):
                for src, part, r0, r in load_q(i, un // 2, CTX + BANK * (un % 2)):
                    sp.dma_start(q_s[r0:r0 + r, un % 2, part, :].bitcast(F32), src).then_inc(q_loaded[un % 2], 16)

            def get_k(i, h):
                for src, part, r0, r in load_k(i, h):
                    sp.dma_start(k_s[r0:r0 + r, h, part, :].bitcast(F32), src).then_inc(k_loaded[h], 16)

            def get_v(i, h):
                sp.dma_start(v_s[:, h].rearrange("p k n -> p (k n)").bitcast(F32), load_v(i, h)
                             ).then_inc(v_loaded[h], 16)

            def put(i, un):
                sp.wait_ge(o_out, 4 * i + un + 1 + 2)
                for part, tile in ((1, o_lo), (0, o_hi)):
                    sp.dma_start(out_dram(part, 2 * i + un // 2, CTX + BANK * (un % 2), BANK),
                                 tile[:, un % 2, :].bitcast(F32)).then_inc(stored[un % 2], 16)

            def scores_of(i, un):
                sp.wait_ge(ctx_scored, 16 * i + 4 * un + 4)

            def body(i, more):
                scores_of(i, 1)
                get_q(i, 3)
                if more:
                    get_k(i + 1, 0)
                put(i, 0)
                if more:
                    scores_of(i, 2)
                    get_q(i + 1, 0)
                put(i, 1)
                if more:
                    get_v(i + 1, 0)
                    scores_of(i, 3)
                    get_q(i + 1, 1)
                    get_k(i + 1, 1)
                put(i, 2)
                if more:
                    scores_of(i + 1, 0)
                    get_q(i + 1, 2)
                put(i, 3)
                if more:
                    get_v(i + 1, 1)

            get_q(0, 0)
            get_k(0, 0)
            get_q(0, 1)
            get_v(0, 0)
            get_k(0, 1)
            get_v(0, 1)
            scores_of(0, 0)
            get_q(0, 2)
            with sp.Fori(0, n_bodies - 1) as i:
                body(i, True)
            body(n_bodies - 1, False)
            for j in range(2):
                sp.wait_ge(stored[j], 16 + 32 * 2 * n_bodies)

        @block.tensor
        def _(pe):
            def score(out, un, q, lo, hi):
                for j, (a, b) in enumerate(passes):
                    last = nc.tensor.matmul(out, q_s[0:rows, un % 2, a, q * P:(q + 1) * P],
                                            k_s[0:rows, (un // 2) % 2, b, lo:hi], start=(j == 0),
                                            stop=(j == len(passes) - 1))
                return last

            def scores(i, un, q):
                m = 4 * un + q
                if q == 0:
                    pe.wait_ge(q_loaded[un % 2], 16 * n_q * (2 * i + un // 2 + 1))
                    pe.wait_ge(k_loaded[(un // 2) % 2], 16 * n_k * (i + un // 4 + 1))
                pe.wait_ge(lat_exp, 16 * i + m + 1)
                for c in range(2):
                    last = score(lat_ps[:, q % 2, c, :], un, q, CTX + c * BANK, CTX + (c + 1) * BANK)
                last.then_inc(lat_scored, 1)
                pe.wait_ge(ctx_exp, 16 * i + m + 1)
                score(ctx_ps[:, 0:CTX], un, q, 0, CTX).then_inc(ctx_scored, 1)

            def turn(i, un, k):
                if k == 0:
                    pe.wait_ge(normed, 16 * i + 4 * un + 4)
                pe.wait_ge(lo_done, 40 * i + 10 * un + k + 1)
                for q in range(4):
                    last = nc.tensor.transpose(t_ps[:, k % 2, q * P:(q + 1) * P],
                                               prob_tile(un, q)[:, k * P:(k + 1) * P], g.ident[:, :])
                last.then_inc(turned, 1)

            def weigh(i, un, k):
                if k == 0:
                    pe.wait_ge(v_loaded[un // 2], 16 * (i + 1))
                    pe.wait_ge(o_read, 4 * i + un + 1)
                pe.wait_ge(lo_done, 40 * i + 10 * un + k + 1 + 2)
                for j, pt in enumerate((pt_hi, pt_lo)):
                    last = nc.tensor.matmul(o_ps[:, :], v_s[:, un // 2, k, :], pt[:, k % 2, :],
                                            start=(k == 0 and j == 0), stop=(k == NKT - 1 and j == 1))
                last.then_inc(pv_step, 1)

            def body(i, more):
                def step(un, k, exists):
                    if exists:
                        turn(i, un + k // NKT, k % NKT)
                    if tile := tile_at(scores_at, un, k, more):
                        scores(i, *tile)
                    weigh(i, un, k - 1)

                steps(more, step)

            pe.sem_inc(pv_step, 2)
            for tile in early:
                scores(0, *tile)
            turn(0, 0, 0)
            with pe.Fori(0, n_bodies - 1) as i:
                body(i, True)
            body(n_bodies - 1, False)

        @block.vector
        def _(dve):
            def row_max(i, un, q):
                m = 16 * i + 4 * un + q
                dve.wait_ge(lat_scored, m + 1)
                nc.vector.tensor_reduce(max_parts[:, q % 2, 0:1], lat_ps[:, q % 2].rearrange("p c n -> p (c n)"),
                                        AX_X, ALU.max, negate=True).then_inc(max_part, 1)
                dve.wait_ge(ctx_scored, m + 1)
                nc.vector.tensor_reduce(max_parts[:, q % 2, 1:2], ctx_ps[:, 0:CTX], AX_X, ALU.max, negate=True
                                        ).then_inc(max_part, 1)
                dve.wait_ge(max_part, 2 * m + 2)
                nc.vector.tensor_tensor(neg_max[:, un % 2, q:q + 1], max_parts[:, q % 2, 0:1],
                                        max_parts[:, q % 2, 1:2], ALU.min).then_inc(max_done, 1)

            def inverse(i, un, q):
                m = 16 * i + 4 * un + q
                dve.wait_ge(lat_exp, m + 1 + 2)
                nc.vector.tensor_tensor(total[:, un % 2, q:q + 1], total_parts[:, un % 2, q, 0:1],
                                        total_parts[:, un % 2, q, 1:2], ALU.add).then_inc(total_done, 1)
                dve.wait_ge(total_done, m + 1)
                nc.vector.reciprocal(r_total[:, un % 2, q:q + 1], total[:, un % 2, q:q + 1]).then_inc(r_done, 1)

            def low(i, un, k):
                dve.wait_ge(hi_done, 40 * i + 10 * un + k + 1)
                nc.vector.tensor_tensor(pt_lo[:, k % 2, :], t_ps[:, k % 2, :], pt_hi[:, k % 2, :].bitcast(F32),
                                        ALU.subtract).then_inc(lo_done, 1)

            def body(i, more):
                def step(un, k, exists):
                    if exists:
                        low(i, un + k // NKT, k % NKT)
                    if tile := tile_at(scores_at, un, k, more):
                        row_max(i, *tile)
                    if tile := tile_at(inverse_at, un, k, more):
                        inverse(i, *tile)

                steps(more, step)

            dve.sem_inc(lo_done, 2)
            for m, tile in enumerate(early):
                row_max(0, *tile)
                if m:
                    inverse(0, *early[m - 1])
            low(0, 0, 0)
            with dve.Fori(0, n_bodies - 1) as i:
                body(i, True)
            body(n_bodies - 1, False)

        @block.scalar
        def _(act):
            def exponent(i, un, q):
                act.wait_ge(max_done, 16 * i + 4 * un + q + 1)
                nc.scalar.activation(prob_tile(un, q)[:, 0:CTX], ctx_ps[:, 0:CTX], ACT.Exp,
                                     bias=neg_max[:, un % 2, q:q + 1],
                                     accum_out=total_parts[:, un % 2, q, 1:2]).then_inc(ctx_exp, 1)
                nc.scalar.activation(prob_tile(un, q)[:, CTX:TOK], lat_ps[:, q % 2].rearrange("p c n -> p (c n)"),
                                     ACT.Exp, bias=neg_max[:, un % 2, q:q + 1],
                                     accum_out=total_parts[:, un % 2, q, 0:1]).then_inc(lat_exp, 1)

            def high(i, un, k):
                act.wait_ge(pv_step, 40 * i + 10 * un + k + 1)
                act.wait_ge(turned, 40 * i + 10 * un + k + 1)
                nc.scalar.copy(pt_hi[:, k % 2, :], t_ps[:, k % 2, :]).then_inc(hi_done, 1)

            def read_out(i, un):
                act.wait_ge(o_added, 4 * i + un + 1)
                act.wait_ge(pv_step, 40 * i + 10 * un + 10 + 2)
                nc.scalar.copy(o_a[:, un % 2, :], o_ps[0:V_DIM, :])
                nc.scalar.copy(o_b[:, un % 2, :], o_ps[V_DIM:2 * V_DIM, :]).then_inc(o_read, 1)

            def high_out(i, un):
                act.wait_ge(stored[un % 2], 32 * (2 * i + un // 2) + 16)
                act.wait_ge(o_added, 4 * i + un + 1 + 2)
                nc.scalar.copy(o_hi[:, un % 2, :], o_sum[:, un % 2, :]).then_inc(o_high, 1)

            def body(i, more, first=False):
                def step(un, k, exists):
                    if exists:
                        high(i, un + k // NKT, k % NKT)
                    if tile := tile_at(exp_at, un, k, more):
                        exponent(i, *tile)
                    if k == NKT:
                        read_out(i, un)
                    if k == 2 and un:
                        high_out(i, un - 1)
                    elif k == 2 and not first:
                        high_out(i - 1, 3)

                steps(more, step)

            act.sem_inc(ctx_exp, 1)
            act.sem_inc(lat_exp, 2)
            act.sem_inc(o_read, 1)
            for tile in early[:-1]:
                exponent(0, *tile)
            high(0, 0, 0)
            body(0, True, first=True)
            with act.Fori(1, n_bodies - 1) as i:
                body(i, True)
            body(n_bodies - 1, False)
            high_out(n_bodies - 1, 3)

        @block.gpsimd
        def _(pool):
            def normalise(i, un, q):
                pool.wait_ge(r_done, 16 * i + 4 * un + q + 1)
                nc.gpsimd.tensor_tensor(prob_tile(un, q), prob_tile(un, q),
                                        r_total[:, un % 2, q:q + 1].to_broadcast([P, TOK]), ALU.mult
                                        ).then_inc(normed, 1)

            def finish(i, un):
                pool.wait_ge(o_read, 4 * i + un + 1 + 1)
                nc.gpsimd.tensor_tensor(o_sum[:, un % 2, :], o_a[:, un % 2, :], o_b[:, un % 2, :], ALU.add
                                        ).then_inc(o_added, 1)

            def finish_low(i, un):
                pool.wait_ge(o_high, 4 * i + un + 1)
                nc.gpsimd.tensor_tensor(o_lo[:, un % 2, :], o_sum[:, un % 2, :], o_hi[:, un % 2, :].bitcast(F32),
                                        ALU.subtract).then_inc(o_out, 1)
                pool.wait_ge(o_out, 4 * i + un + 1 + 2)

            def body(i, more):
                def step(un, k, exists):
                    if tile := tile_at(inverse_at, un, k, more):
                        normalise(i, *tile)
                    if k == NKT:
                        finish(i, un)
                        finish_low(i, un)

                steps(more, step)

            pool.sem_inc(o_added, 2)
            pool.sem_inc(o_out, 2)
            for tile in early[:-1]:
                normalise(0, *tile)
            with pool.Fori(0, n_bodies - 1) as i:
                body(i, True)
            body(n_bodies - 1, False)


def context_attention(nc, g, tag, q_dram, k_dram, v_dram, out_dram):
    group = HEADS // GQA_KV
    n_t = 2 * group
    with ExitStack() as ctx:
        sb = lambda n, s, d=F32: ctx.enter_context(nc.sbuf_tensor(tag + n, s, d))
        ps = lambda n, s, d=F32: ctx.enter_context(nc.psum_tensor(tag + n, s, d))
        sem = semaphores(nc, ctx, tag)
        q_s = sb("q_s", [P, group, CTX], F32R)
        k_s = sb("k_s", [P, 2, CTX], F32R)
        v_s = sb("v_s", [P, 2, P], F32R)
        prob = sb("prob", [P, n_t, CTX])
        pt_hi = sb("pt_hi", [P, 2, 2, CTX], F32R)
        pt_lo = sb("pt_lo", [P, 2, 2, CTX], F32R)
        neg_max, total, r_total = sb("neg_max", [P, n_t]), sb("total", [P, n_t]), sb("r_total", [P, n_t])
        o_a, o_b, o_sum = sb("o_a", [V_DIM, group, CTX]), sb("o_b", [V_DIM, group, CTX]), sb("o_sum", [V_DIM, group, CTX])
        o_hi, o_lo = sb("o_hi", [V_DIM, group, CTX], F32R), sb("o_lo", [V_DIM, group, CTX], F32R)
        s_ps = ps("s_ps", [P, n_t, CTX])
        t_ps = ps("t_ps", [P, 2, BANK])
        o_ps = ps("o_ps", [P, group, CTX])
        loaded, scored, max_done, exp_done, r_done, normed = (
            sem("loaded"), sem("scored"), sem("max_done"), sem("exp_done"), sem("r_done"), sem("normed"))
        turned, hi_done, lo_done, weighed = sem("turned"), sem("hi_done"), sem("lo_done"), sem("weighed")
        o_read, o_added, o_high, o_out, stored = (
            sem("o_read"), sem("o_added"), sem("o_high"), sem("o_out"), sem("stored"))
        block = ctx.enter_context(nc.Block(no_gpsimd_drain=True))

        @block.sync
        def _(sp):
            n_out = 16 * 2 * group
            sp.sem_inc(stored, n_out)
            with sp.Fori(0, GQA_KV) as i:
                sp.wait_ge(stored, n_out * (i + 1))
                for j in range(group):
                    for part in range(2):
                        sp.dma_start(q_s[64 * part:64 * part + 64, j, :].bitcast(F32), q_dram(part, group * i + j)).then_inc(loaded, 16)
                for part in range(2):
                    for half in range(2):
                        sp.dma_start(k_s[64 * half:64 * half + 64, part, :].bitcast(F32), k_dram(part, i)).then_inc(loaded, 16)
                sp.dma_start(v_s[:, :, :].rearrange("p k n -> p (k n)").bitcast(F32), v_dram(i)).then_inc(loaded, 16)
                sp.wait_ge(o_out, i + 1)
                for j in range(group):
                    for part, tile in ((0, o_hi), (1, o_lo)):
                        sp.dma_start(out_dram(part, group * i + j, 0, CTX), tile[:, j, :].bitcast(F32)).then_inc(stored, 16)
            sp.wait_ge(stored, n_out * (GQA_KV + 1))

        @block.tensor
        def _(pe):
            with pe.Fori(0, GQA_KV) as i:
                pe.wait_ge(loaded, 16 * (2 * group + 5) * (i + 1))
                for q in range(n_t):
                    for j in range(2):
                        last = nc.tensor.matmul(s_ps[:, q, :], q_s[:, q // 2, (q % 2) * P:(q % 2 + 1) * P],
                                                k_s[:, j, :], start=(j == 0), stop=(j == 1))
                last.then_inc(scored, 1)
                for j in range(group):
                    pe.wait_ge(normed, n_t * i + 2 * j + 2)
                    pe.wait_ge(lo_done, group * i + j + 1)
                    for k in range(2):
                        for q in range(2):
                            last = nc.tensor.transpose(t_ps[:, j % 2, (2 * k + q) * P:(2 * k + q + 1) * P],
                                                       prob[:, 2 * j + q, k * P:(k + 1) * P], g.ident[:, :])
                    last.then_inc(turned, 1)
                    pe.wait_ge(lo_done, group * i + j + 3)
                    for k in range(2):
                        for m, pt in enumerate((pt_hi, pt_lo)):
                            last = nc.tensor.matmul(o_ps[:, j, :], v_s[:, k, :], pt[:, j % 2, k, :],
                                                    start=(k == 0 and m == 0), stop=(k == 1 and m == 1))
                    last.then_inc(weighed, 1)

        @block.vector
        def _(dve):
            dve.sem_inc(lo_done, 2)
            with dve.Fori(0, GQA_KV) as i:
                dve.wait_ge(scored, i + 1)
                nc.vector.tensor_reduce(neg_max[:, :], s_ps[:, :, :], AX_X, ALU.max, negate=True
                                        ).then_inc(max_done, 1)
                dve.wait_ge(exp_done, n_t * i + n_t)
                nc.vector.reciprocal(r_total[:, :], total[:, :]).then_inc(r_done, 1)
                for j in range(group):
                    dve.wait_ge(hi_done, group * i + j + 1)
                    nc.vector.tensor_tensor(pt_lo[:, j % 2].rearrange("p k n -> p (k n)"), t_ps[:, j % 2, :],
                                            pt_hi[:, j % 2].rearrange("p k n -> p (k n)").bitcast(F32), ALU.subtract
                                            ).then_inc(lo_done, 1)

        @block.scalar
        def _(act):
            with act.Fori(0, GQA_KV) as i:
                act.wait_ge(max_done, i + 1)
                for q in range(n_t):
                    nc.scalar.activation(prob[:, q, :], s_ps[:, q, :], ACT.Exp, bias=neg_max[:, q:q + 1],
                                         accum_out=total[:, q:q + 1]).then_inc(exp_done, 1)
                for j in range(group):
                    act.wait_ge(turned, group * i + j + 1)
                    nc.scalar.copy(pt_hi[:, j % 2].rearrange("p k n -> p (k n)"), t_ps[:, j % 2, :]
                                   ).then_inc(hi_done, 1)
                act.wait_ge(weighed, group * i + group)
                nc.scalar.copy(o_a[:, :, :], o_ps[0:V_DIM, :, :]).then_inc(o_read, 1)
                nc.scalar.copy(o_b[:, :, :], o_ps[V_DIM:2 * V_DIM, :, :]).then_inc(o_read, 1)

        @block.gpsimd
        def _(pool):
            with pool.Fori(0, GQA_KV) as i:
                pool.wait_ge(r_done, i + 1)
                for q in range(n_t):
                    nc.gpsimd.tensor_tensor(prob[:, q, :], prob[:, q, :],
                                            r_total[:, q:q + 1].to_broadcast([P, CTX]), ALU.mult).then_inc(normed, 1)
                pool.wait_ge(o_read, 2 * i + 2)
                nc.gpsimd.tensor_tensor(o_sum[:, :, :], o_a[:, :, :], o_b[:, :, :], ALU.add).then_inc(o_added, 1)
                pool.wait_ge(o_added, i + 1)
                nc.gpsimd.tensor_tensor(o_hi[:, :, :], o_sum[:, :, :], g.zeros_wide[0:V_DIM].rearrange(
                    "p (j n) -> p j n", n=CTX), ALU.add).then_inc(o_high, 1)
                pool.wait_ge(o_high, i + 1)
                nc.gpsimd.tensor_tensor(o_lo[:, :, :], o_sum[:, :, :], o_hi[:, :, :].bitcast(F32), ALU.subtract
                                        ).then_inc(o_out, 1)


def mlp(nc, g, tag, w_gu, w_down, src_hi, src_lo, chunks, dst, gate):
    n_c = len(chunks)
    n_bodies = NFF // 2
    n_w = 3
    n_gu = 2 * n_c
    n_dn = KD * n_c
    with ExitStack() as ctx:
        sb = lambda n, s, d=F32: ctx.enter_context(nc.sbuf_tensor(tag + n, s, d))
        ps = lambda n, s, d=F32: ctx.enter_context(nc.psum_tensor(tag + n, s, d))
        sem = semaphores(nc, ctx, tag)
        w = Split(nc, ctx, tag, KD, sem, slots=n_w)
        a_hi = sb("a_hi", [P, 2, TOK], F32R)
        a_lo = sb("a_lo", [P, 2, TOK], F32R)
        silu = sb("silu", [P, 3, BANK])
        prod = sb("prod", [P, 2, BANK])
        g_ps = ps("g_ps", [P, 3, BANK])
        u_ps = ps("u_ps", [P, 3, BANK])
        d_ps = ps("d_ps", [P, 2, BANK])
        g_done, u_done, d_done = sem("g_done"), sem("u_done"), sem("d_done")
        silu_done, prod_done, a_high, a_low, added = (
            sem("silu_done"), sem("prod_done"), sem("a_high"), sem("a_low"), sem("added"))
        block = ctx.enter_context(nc.Block(no_gpsimd_drain=True))

        @block.sync
        def _(sp):
            with sp.Fori(0, n_bodies) as i:
                for t in range(6):
                    sp.wait_ge(w.lo_done, 6 * i + t + 1)
                    src = w_gu[bass.ds(4 * i + t, 1)] if t < 4 else w_down[bass.ds(2 * i + t - 4, 1)]
                    sp.dma_start(w.raw[:, t % n_w, :], src.rearrange("a p n -> p (a n)")
                                 ).then_inc(w.loaded[t % n_w], 16)

        @block.gpsimd
        def _(pool):
            pool.sem_inc(w.lo_done, n_w)
            with pool.Fori(0, n_bodies) as i:
                for t in range(6):
                    pool.wait_ge(w.hi_done, 6 * i + t + 1)
                    w.low(t % n_w)

        @block.tensor
        def _(pe):
            pe.sem_inc(u_done, n_gu)
            pe.sem_inc(d_done, n_dn)
            with pe.Fori(0, n_bodies) as i:
                for t in range(4):
                    j, up = divmod(t, 2)
                    bank, done, free = (u_ps, u_done, prod_done) if up else (g_ps, g_done, silu_done)
                    pe.wait_ge(w.lo_done, 6 * i + t + 1 + n_w)
                    for c, (t0, n) in enumerate(chunks):
                        pe.wait_ge(free, n_gu * i + n_c * j + c + 1)
                        for k in range(KD):
                            for m, (a, x) in enumerate(
                                    w.passes(t % n_w, k, src_hi[:, k, t0:t0 + n], src_lo[:, k, t0:t0 + n])):
                                last = nc.tensor.matmul(bank[:, c, 0:n], a, x, start=(k == 0 and m == 0),
                                                        stop=(k == KD - 1 and m == 2))
                        last.then_inc(done, 1)
                pe.wait_ge(w.lo_done, 6 * i + 6 + n_w)
                for c, (t0, n) in enumerate(chunks):
                    pe.wait_ge(a_low, n_gu * i + n_c + c + 1 + 2)
                    for m in range(KD):
                        e = c * KD + m
                        pe.wait_ge(added, n_dn * i + e + 1)
                        for j in range(2):
                            for q, (a, x) in enumerate(
                                    w.passes(1 + j, m, a_hi[:, j, t0:t0 + n], a_lo[:, j, t0:t0 + n])):
                                last = nc.tensor.matmul(d_ps[:, e % 2, 0:n], a, x, start=(j == 0 and q == 0),
                                                        stop=(j == 1 and q == 2))
                        last.then_inc(d_done, 1)

        @block.scalar
        def _(act):
            with act.Fori(0, n_bodies) as i:
                last_use = ((u_done, n_gu * i + n_gu), (d_done, n_dn * i + n_dn), (d_done, n_dn * i + n_dn),
                            (g_done, n_gu * i + n_c), (u_done, n_gu * i + n_c + n_gu), (g_done, n_gu * i + n_gu))

                def split(t):
                    act.wait_ge(w.loaded[t % n_w], 32 * i + 16 * (t // n_w + 1))
                    act.wait_ge(*last_use[t])
                    w.high(t % n_w)

                def activate(j):
                    for c, (_, n) in enumerate(chunks):
                        act.wait_ge(prod_done, n_gu * i + n_c * j + c + 1)
                        act.wait_ge(g_done, n_gu * i + n_c * j + c + 1)
                        nc.scalar.activation(silu[:, c, 0:n], g_ps[:, c, 0:n], ACT.Silu).then_inc(silu_done, 1)

                def high(j):
                    for c, (t0, n) in enumerate(chunks):
                        act.wait_ge(prod_done, n_gu * i + n_c * j + c + 1 + n_c)
                        nc.scalar.copy(a_hi[:, j, t0:t0 + n], prod[:, (n_c * j + c) % 2, 0:n]).then_inc(a_high, 1)

                split(0)
                split(1)
                split(2)
                activate(0)
                split(3)
                high(0)
                split(4)
                activate(1)
                split(5)
                high(1)

        @block.vector
        def _(dve):
            dve.sem_inc(silu_done, n_c)
            dve.sem_inc(prod_done, n_c)
            dve.sem_inc(a_low, 2)
            dve.sem_inc(added, 2)
            with dve.Fori(0, n_bodies) as i:
                def multiply(e):
                    c = e % n_c
                    n = chunks[c][1]
                    dve.wait_ge(a_low, n_gu * i + e + 1)
                    dve.wait_ge(silu_done, n_gu * i + e + 1 + n_c)
                    dve.wait_ge(u_done, n_gu * i + e + 1 + n_gu)
                    nc.vector.tensor_tensor(prod[:, e % 2, 0:n], silu[:, c, 0:n], u_ps[:, c, 0:n], ALU.mult
                                            ).then_inc(prod_done, 1)

                def low(e):
                    j, c = divmod(e, n_c)
                    t0, n = chunks[c]
                    dve.wait_ge(a_high, n_gu * i + e + 1)
                    nc.vector.tensor_tensor(a_lo[:, j, t0:t0 + n], prod[:, e % 2, 0:n],
                                            a_hi[:, j, t0:t0 + n].bitcast(F32), ALU.subtract).then_inc(a_low, 1)

                for e in range(n_gu):
                    multiply(e)
                    low(e)
                for c, (t0, n) in enumerate(chunks):
                    for m in range(KD):
                        e = c * KD + m
                        dve.wait_ge(d_done, n_dn * i + e + 1 + n_dn)
                        nc.vector.scalar_tensor_tensor(dst[:, m, t0:t0 + n], d_ps[:, e % 2, 0:n],
                                                       gate(m, stream_of(chunks[c])), dst[:, m, t0:t0 + n],
                                                       ALU.mult, ALU.add).then_inc(added, 1)


def rotate_rows(nc, g, tag, src, turn, cos, sin, out_dram):
    n_c = len(ALL_CHUNKS)
    with ExitStack() as ctx:
        sb = lambda n, s, d=F32: ctx.enter_context(nc.sbuf_tensor(tag + n, s, d))
        sem = semaphores(nc, ctx, tag)
        with_cos, with_sin, whole = sb("with_cos", [P, TOK]), sb("with_sin", [P, TOK]), sb("whole", [P, TOK])
        hi, lo = sb("hi", [P, TOK], F32R), sb("lo", [P, TOK], F32R)
        turned_ps = ctx.enter_context(nc.psum_tensor(tag + "turned", [P, 3, BANK], F32))
        turned, cos_done, sin_done, whole_done, hi_done, lo_done, stored = (
            sem("turned"), sem("cos_done"), sem("sin_done"), sem("whole_done"), sem("hi_done"), sem("lo_done"),
            sem("stored"))
        block = ctx.enter_context(nc.Block(no_gpsimd_drain=True))

        @block.tensor
        def _(pe):
            for c, (t0, n) in enumerate(ALL_CHUNKS):
                nc.tensor.matmul(turned_ps[:, c, 0:n], turn[:, :], src[:, t0:t0 + n], start=True, stop=True
                                 ).then_inc(turned, 1)

        @block.gpsimd
        def _(pool):
            nc.gpsimd.tensor_tensor(with_cos[:, :], src, cos[:, :], ALU.mult).then_inc(cos_done, 1)

        @block.vector
        def _(dve):
            for c, (t0, n) in enumerate(ALL_CHUNKS):
                dve.wait_ge(turned, c + 1)
                nc.vector.tensor_tensor(with_sin[:, t0:t0 + n], turned_ps[:, c, 0:n], sin[:, t0:t0 + n],
                                        ALU.mult).then_inc(sin_done, 1)
            dve.wait_ge(sin_done, n_c)
            dve.wait_ge(cos_done, 1)
            nc.vector.tensor_tensor(whole[:, :], with_cos[:, :], with_sin[:, :], ALU.add).then_inc(whole_done, 1)
            dve.wait_ge(hi_done, 1)
            nc.vector.tensor_tensor(lo[:, :], whole[:, :], hi[:, :].bitcast(F32), ALU.subtract).then_inc(lo_done, 1)

        @block.scalar
        def _(act):
            act.wait_ge(whole_done, 1)
            nc.scalar.copy(hi[:, :], whole[:, :]).then_inc(hi_done, 1)

        @block.sync
        def _(sp):
            sp.wait_ge(lo_done, 1)
            for part, tile in ((0, hi), (1, lo)):
                sp.dma_start(out_dram[part], tile[0:ROPE, :].bitcast(F32)).then_inc(stored, 16)
            sp.wait_ge(stored, 32)


def fetch(nc, tag, pairs):
    with ExitStack() as ctx:
        loaded = semaphores(nc, ctx, tag)("loaded")
        block = ctx.enter_context(nc.Block(no_gpsimd_drain=True))

        @block.sync
        def _(sp):
            for dst, src in pairs:
                sp.dma_start(dst, src).then_inc(loaded, 16)
            sp.wait_ge(loaded, 16 * len(pairs))


class Globals:
    pass


def flat(ap):
    return ap.rearrange("a p n -> p (a n)")


def dit_kernel(nc, a, out):
    g = Globals()
    g.w_mod = [a["w_mod"][layer] for layer in range(2)]
    scratch = {}

    def dram(name, shape):
        scratch[name] = nc.dram_tensor(name, shape, F32, kind="Internal").ap()
        return scratch[name]

    with ExitStack() as ctx:
        sb = lambda n, s, d=F32: ctx.enter_context(nc.sbuf_tensor(n, s, d))
        x_t = sb("x_t", [P, KD, TOK])
        g.ident, g.ones, g.head_ones = sb("ident", [P, P]), sb("ones", [P, P]), sb("head_ones", [P, P])
        turn64, turn32 = sb("turn64", [P, P]), sb("turn32", [P, P])
        g.eps = sb("eps", [P, 1])
        g.zeros_wide = sb("zeros_wide", [P, 2 * BANK])
        g.zeros = g.zeros_wide[:, 0:BANK]
        g.mod_t = sb("mod_t", [P, MOD_COLS, 2])
        g.gain1, g.gain2 = sb("gain1", [P, KD, 2]), sb("gain2", [P, KD, 2])
        g.b_mod = sb("b_mod", [P, 2, MOD_COLS, 2])
        g.norms = sb("norms", [P, 2, 2, KD, 2])
        c_t = sb("c_t", [P, KD, 2])
        g.silu_c = sb("silu_c", [P, KD, 2])
        final_gain, qa_gain, kva_gain = sb("final_gain", [P, KD]), sb("qa_gain", [P, 3]), sb("kva_gain", [P, 2])
        qk_gain_in, qk_gains = sb("qk_gain_in", [P, 2]), sb("qk_gains", [P, 10])

        fetch(nc, "in_", [
            (x_t[:, :, CTX:TOK], a["x_t"].rearrange("(k p) n -> p k n", p=P)),
            (x_t[:, :, 0:CTX], a["ctx_t"].rearrange("(k p) n -> p k n", p=P)),
            (g.ident[:, :], a["ident"]), (g.ones[:, :], a["ones"]), (g.head_ones[:, :], a["head_ones"]),
            (turn64[:, :], a["turn64"]), (turn32[:, :], a["turn32"]),
            (g.b_mod[:, :, :, :], a["b_mod"]), (g.norms[:, :, :, :, :], a["norms"]), (c_t[:, :, :], a["c_t"]),
            (final_gain[:, :], a["final_gain"]), (qa_gain[:, :], a["qa_gain"]), (kva_gain[:, :], a["kva_gain"]),
            (qk_gain_in[:, :], a["qk_gain"]),
        ])
        setup_done = nc.alloc_semaphore("setup_done")
        with nc.Block(no_gpsimd_drain=True) as block:
            @block.vector
            def _(dve):
                nc.vector.memset(g.eps[:, :], EPS).then_inc(setup_done, 1)
                nc.vector.memset(g.zeros_wide[:, :], 0.0).then_inc(setup_done, 1)
                nc.vector.tensor_scalar(qk_gains[:, 0:8], qk_gain_in[:, 0:1].to_broadcast([P, 8]),
                                        GQA_HD ** -0.5, None, ALU.mult).then_inc(setup_done, 1)
                nc.vector.tensor_copy(qk_gains[:, 8:10], qk_gain_in[:, 1:2].to_broadcast([P, 2])
                                      ).then_inc(setup_done, 1)

            @block.scalar
            def _(act):
                nc.scalar.activation(g.silu_c[:, :, :], c_t[:, :, :], ACT.Silu)

        def mod(split):
            return lambda k, s: flat_column(g.mod_t, split * KD + k, s)

        def flat_column(table, col, s):
            return table[:, bass.ds(col, 1), s:s + 1].rearrange("p a b -> p (a b)")

        def attend_out(name):
            o = dram(name, (2, HEADS, V_DIM, TOK))
            return o, lambda part, h, t0, n: flat(o[part, bass.ds(h, 1), :, t0:t0 + n])

        modulation(nc, g, 0)
        o0, o0_at = attend_out("o0")
        qk0 = dram("qk0", (2, 10, P, TOK))
        qk0_heads = qk0.rearrange("s t (h p) n -> s (t h) p n", p=GQA_HD)
        v0 = dram("v0", (GQA_KV, P, NKT * P))

        with ExitStack() as hctx:
            h_hi = hctx.enter_context(nc.sbuf_tensor("h0_hi", [P, KD, TOK], F32R))
            h_lo = hctx.enter_context(nc.sbuf_tensor("h0_lo", [P, KD, TOK], F32R))
            norm(nc, g, "n01_", x_t, KD, lambda k, s: g.gain1[:, k, s:s + 1], mod(0), h_hi, h_lo, ALL_CHUNKS)
            values(nc, g, "v0_", a["w_v0"], h_hi, h_lo, KD, 2, v0)
            with ExitStack() as rctx:
                cos = rctx.enter_context(nc.sbuf_tensor("cos64", [P, TOK], F32))
                sin = rctx.enter_context(nc.sbuf_tensor("sin64", [P, TOK], F32))
                fetch(nc, "rope64_", [(cos[:, :], a["cos64"]), (sin[:, :], a["sin64"])])
                project(nc, g, "qk0_", a["w_qk0"], h_hi, h_lo, KD, 10, ALL_CHUNKS, "norm_rope",
                        lambda part, t, t0, n: flat(qk0[part, bass.ds(t, 1), :, t0:t0 + n]),
                        gains=qk_gains, turn=turn64, cos=cos, sin=sin)

        def q0(i, h, t0):
            return [(flat(qk0_heads[part, bass.ds(2 * i + h, 1), :, t0:t0 + BANK]), 0, 64 * part, 64)
                    for part in range(2)]

        def k0(i, h):
            return [(flat(qk0_heads[part, bass.ds(HEADS + i // 2, 1), :, :]), part, 64 * half, 64)
                    for part in range(2) for half in range(2)]

        attention(nc, g, "at0_", q0, k0, lambda i, h: flat(v0[bass.ds(i // 2, 1)]), P, ((0, 0), (0, 1)), o0_at)
        context_attention(
            nc, g, "ca0_", lambda part, h: flat(qk0_heads[part, bass.ds(h, 1), :, 0:CTX]),
            lambda part, i: flat(qk0_heads[part, bass.ds(HEADS + i, 1), :, 0:CTX]),
            lambda i: flat(v0[bass.ds(i, 1), :, 0:CTX]), o0_at)

        def out_and_mlp(layer, o_dram, w_o, w_gu, w_down, chunks):
            t_first = min(t0 for t0, _ in chunks)
            with ExitStack() as hctx:
                h_hi = hctx.enter_context(nc.sbuf_tensor(f"m{layer}_hi", [P, KD, TOK], F32R))
                h_lo = hctx.enter_context(nc.sbuf_tensor(f"m{layer}_lo", [P, KD, TOK], F32R))
                fetch(nc, f"o{layer}_", [(h[64 * half:64 * half + 64, k, t_first:TOK].bitcast(F32),
                                          o_dram[part, 2 * k + half, :, t_first:TOK])
                                         for part, h in ((0, h_hi), (1, h_lo)) for k in range(KD)
                                         for half in range(2)])
                accumulate(nc, g, f"wo{layer}_", w_o, h_hi, h_lo, KD, KD, chunks, x_t, mod(2))
                norm(nc, g, f"n{layer}2_", x_t, KD, lambda k, s: g.gain2[:, k, s:s + 1], mod(3), h_hi, h_lo, chunks)
                mlp(nc, g, f"mlp{layer}_", w_gu, w_down, h_hi, h_lo, chunks, x_t, mod(5))

        out_and_mlp(0, o0, a["w_o0"], a["w_gu0"], a["w_down0"], ALL_CHUNKS)

        modulation(nc, g, 1)
        o1, o1_at = attend_out("o1")
        q_nope, q_rope = dram("q_nope", (2, 8, P, TOK)), dram("q_rope", (2, 4, P, TOK))
        k_nope, k_rope, v1 = dram("k_nope", (2, 8, P, TOK)), dram("k_rope", (2, ROPE, TOK)), dram(
            "v1", (HEADS, P, NKT * P))
        q_nope_heads = q_nope.rearrange("s t (h p) n -> s (t h) p n", p=NOPE)
        q_rope_heads = q_rope.rearrange("s t (h p) n -> s (t h) p n", p=ROPE)
        k_nope_heads = k_nope.rearrange("s t (h p) n -> s (t h) p n", p=NOPE)
        mla_scale = float(np.float32(QK_MLA ** -0.5))

        with ExitStack() as lctx:
            low_rank = lctx.enter_context(nc.sbuf_tensor("low_rank", [P, W_IN_TILES, TOK], F32))
            with ExitStack() as hctx:
                h_hi = hctx.enter_context(nc.sbuf_tensor("h1_hi", [P, KD, TOK], F32R))
                h_lo = hctx.enter_context(nc.sbuf_tensor("h1_lo", [P, KD, TOK], F32R))
                norm(nc, g, "n11_", x_t, KD, lambda k, s: g.gain1[:, k, s:s + 1], mod(0), h_hi, h_lo, ALL_CHUNKS)
                accumulate(nc, g, "win_", a["w_in"], h_hi, h_lo, KD, W_IN_TILES, ALL_CHUNKS, low_rank)
            q_hi = lctx.enter_context(nc.sbuf_tensor("q_hi", [P, 3, TOK], F32R))
            q_lo = lctx.enter_context(nc.sbuf_tensor("q_lo", [P, 3, TOK], F32R))
            kv_hi = lctx.enter_context(nc.sbuf_tensor("kv_hi", [P, 2, TOK], F32R))
            kv_lo = lctx.enter_context(nc.sbuf_tensor("kv_lo", [P, 2, TOK], F32R))
            cos = lctx.enter_context(nc.sbuf_tensor("cos32", [P, TOK], F32))
            sin = lctx.enter_context(nc.sbuf_tensor("sin32", [P, TOK], F32))
            fetch(nc, "rope32_", [(cos[:, :], a["cos32"]), (sin[:, :], a["sin32"])])
            norm(nc, g, "nqa_", low_rank[:, 0:3], 3, lambda k, s: qa_gain[:, k:k + 1], None, q_hi, q_lo, LAT_CHUNKS)
            norm(nc, g, "nkv_", low_rank[:, 3:5], 2, lambda k, s: kva_gain[:, k:k + 1], None, kv_hi, kv_lo, ALL_CHUNKS)
            rotate_rows(nc, g, "kr_", low_rank[:, 5, :], turn32, cos, sin, k_rope)
            project(nc, g, "qn_", a["w_q_nope"], q_hi, q_lo, 3, 8, LAT_CHUNKS, "plain",
                    lambda part, t, t0, n: flat(q_nope[part, bass.ds(t, 1), :, t0:t0 + n]), scale=mla_scale)
            project(nc, g, "qr_", a["w_q_rope"], q_hi, q_lo, 3, 4, LAT_CHUNKS, "rope",
                    lambda part, t, t0, n: flat(q_rope[part, bass.ds(t, 1), :, t0:t0 + n]), scale=mla_scale,
                    turn=turn32, cos=cos, sin=sin)
            project(nc, g, "kn_", a["w_k_nope"], kv_hi, kv_lo, 2, 8, ALL_CHUNKS, "plain",
                    lambda part, t, t0, n: flat(k_nope[part, bass.ds(t, 1), :, t0:t0 + n]))
            values(nc, g, "v1_", a["w_v1"], kv_hi, kv_lo, 2, 8, v1)

        def q1(i, h, t0):
            return ([(flat(q_nope_heads[part, bass.ds(2 * i + h, 1), :, t0:t0 + BANK]), part, 0, NOPE)
                     for part in range(2)]
                    + [(flat(q_rope_heads[part, bass.ds(2 * i + h, 1), :, t0:t0 + BANK]), part, NOPE, ROPE)
                       for part in range(2)])

        def k1(i, h):
            return ([(flat(k_nope_heads[part, bass.ds(2 * i + h, 1), :, :]), part, 0, NOPE) for part in range(2)]
                    + [(k_rope[part], part, NOPE, ROPE) for part in range(2)])

        attention(nc, g, "at1_", q1, k1, lambda i, h: flat(v1[bass.ds(2 * i + h, 1)]), QK_MLA,
                  ((0, 0), (1, 0), (0, 1)), o1_at)
        out_and_mlp(1, o1, a["w_o1"], a["w_gu1"], a["w_down1"], LAT_CHUNKS)

        norm(nc, g, "fin_", x_t, KD, lambda k, s: final_gain[:, k:k + 1], None, None, None, LAT_CHUNKS, out_dram=out)




def tiles(w):
    k, n = w.shape
    return np.ascontiguousarray(w.reshape(k // P, P, n // P, P).transpose(2, 1, 0, 3).reshape(n // P, P, k))


def per_feature(v):
    return np.ascontiguousarray(v.reshape(-1, P).T)


def rope_tables(rot_dim):
    n = rot_dim // 4
    inv = np.power(np.float32(10000.0), -np.arange(n, dtype=np.float32) / np.float32(n))
    rows = SEQ // GRID_W
    row = np.repeat(np.arange(rows, dtype=np.float32), GRID_W)
    col = np.tile(np.arange(GRID_W, dtype=np.float32), rows)
    ang = np.concatenate([row[:, None] * inv, col[:, None] * inv], axis=-1).astype(np.float64)
    cos = np.ones((rot_dim // 2, TOK), np.float32)
    sin = np.zeros((rot_dim // 2, TOK), np.float32)
    cos[:, CTX:], sin[:, CTX:] = np.cos(ang).T, np.sin(ang).T
    return np.tile(cos, (2 * P // rot_dim, 1)), np.tile(sin, (2 * P // rot_dim, 1))


def turn_matrix(rot_dim):
    half = rot_dim // 2
    m = np.zeros((P, P), np.float32)
    for g0 in range(0, P, rot_dim):
        for j in range(half):
            m[g0 + half + j, g0 + j] = -1.0
            m[g0 + j, g0 + half + j] = 1.0
    return m


def kernel(**inputs):
    import concourse.bacc as bacc
    from concourse.bass_utils import run_bass_kernel_spmd

    v = {name: np.asarray(x) for name, x in inputs.items()}
    arrays = {
        "x_t": v["x"][0].T,
        "ctx_t": v["ctx"][0].T,
        "c_t": np.stack([v["c"][0], v["c_ctx"]], axis=-1).reshape(KD, P, 2).transpose(1, 0, 2),
        "w_mod": v["w_mod"].reshape(2, KD, P, 12, BANK).transpose(0, 3, 2, 1, 4).reshape(2, 12, P, KD * BANK),
        "b_mod": np.repeat(v["b_mod"].reshape(2, MOD_COLS, P).transpose(2, 0, 1)[..., None], 2, axis=-1),
        "norms": np.repeat(np.stack([v["norm1"], v["norm2"]], axis=1).reshape(2, 2, KD, P).transpose(3, 0, 1, 2)
                           [..., None], 2, axis=-1),
        "final_gain": per_feature(v["final_norm"]),
        "qa_gain": per_feature(v["mla_q_a_norm"][0]),
        "kva_gain": per_feature(v["mla_kv_a_norm"][0]),
        "qk_gain": np.stack([np.tile(v["gqa_q_norm"][0], 2), np.tile(v["gqa_k_norm"][0], 2)], axis=-1),
    }
    qkv = v["gqa_w_qkv"][0]
    n_qk = (HEADS + GQA_KV) * GQA_HD
    arrays["w_qk0"] = tiles(qkv[:, :n_qk])
    arrays["w_v0"] = tiles(qkv[:, n_qk:])
    w_in = v["mla_w_in"][0]
    padded = np.zeros((D, W_IN_TILES * P), w_in.dtype)
    padded[:, :w_in.shape[1]] = w_in
    arrays["w_in"] = tiles(padded)
    q_b = v["mla_q_b"][0].reshape(Q_RANK, HEADS, QK_MLA)
    arrays["w_q_nope"] = tiles(q_b[:, :, :NOPE].reshape(Q_RANK, HEADS * NOPE))
    arrays["w_q_rope"] = tiles(q_b[:, :, NOPE:].reshape(Q_RANK, HEADS * ROPE))
    kv_b = v["mla_kv_b"][0].reshape(KV_RANK, HEADS, NOPE + V_DIM)
    arrays["w_k_nope"] = tiles(kv_b[:, :, :NOPE].reshape(KV_RANK, HEADS * NOPE))
    arrays["w_v1"] = tiles(kv_b[:, :, NOPE:].reshape(KV_RANK, HEADS * V_DIM))
    for layer, w_o in enumerate((v["gqa_w_o"][0], v["mla_w_o"][0])):
        arrays[f"w_o{layer}"] = tiles(w_o)
        gu = v["w_gate_up"][layer]
        arrays[f"w_gu{layer}"] = np.stack([tiles(gu[:, :DFF]), tiles(gu[:, DFF:])], axis=1).reshape(2 * NFF, P, D)
        arrays[f"w_down{layer}"] = v["w_down"][layer].reshape(NFF, P, D)
    arrays["ident"] = np.eye(P, dtype=np.float32)
    arrays["ones"] = np.ones((P, P), np.float32)
    arrays["head_ones"] = np.kron(np.eye(2, dtype=np.float32), np.ones((64, 64), np.float32))
    arrays["turn64"], arrays["turn32"] = turn_matrix(64), turn_matrix(32)
    arrays["cos64"], arrays["sin64"] = rope_tables(64)
    arrays["cos32"], arrays["sin32"] = rope_tables(32)
    arrays = {name: np.ascontiguousarray(x) for name, x in arrays.items()}

    nc = bacc.Bacc("TRN2", target_bir_lowering=False, num_devices=1)
    aps = {name: nc.dram_tensor(f"in_{name}", x.shape, mybir.dt.from_np(x.dtype), kind="ExternalInput").ap()
           for name, x in arrays.items()}
    out = nc.dram_tensor("out_t", (D, SEQ), F32, kind="ExternalOutput").ap()
    dit_kernel(nc, aps, out)
    r = run_bass_kernel_spmd(nc, [{f"in_{name}": x for name, x in arrays.items()}], core_ids=[0])
    return np.ascontiguousarray(r.results[0]["out_t"].T)[None]
```

```python
from contextlib import ExitStack

import concourse.bass as bass
import numpy as np
from concourse import mybir

F32 = mybir.dt.float32
F32R = mybir.dt.float32r
ALU = mybir.AluOpType
ACT = mybir.ActivationFunctionType
AX_X = mybir.AxisListType.X

P = 128
D = 1024
KD = D // P
CTX = 256
SEQ = 1024
TOK = CTX + SEQ
NKT = TOK // P
DFF = 2816
NFF = DFF // P
HEADS = 16
GQA_HD = 64
GQA_KV = 4
NOPE = 64
ROPE = 32
QK_MLA = NOPE + ROPE
V_DIM = 64
Q_RANK = 384
KV_RANK = 256
W_IN_TILES = 6
GRID_W = 64
EPS = 1e-6
BANK = 512
MOD_COLS = 6 * KD

LAT_CHUNKS = ((256, 512), (768, 512))
ALL_CHUNKS = LAT_CHUNKS + ((0, 256),)


def stream_of(chunk):
    return 0 if chunk[0] >= CTX else 1


def semaphores(nc, ctx, tag):
    taken = []

    def sem(name):
        taken.append(nc.alloc_semaphore(tag + name))
        return taken[-1]

    def give_back():
        nc.clear_and_free_semaphores(taken)
        nc.all_engine_barrier(sem_only=True)

    ctx.callback(give_back)
    return sem


def modulation(nc, g, layer):
    n_chunks = 12
    n_raw = 4
    n_bodies = n_chunks // n_raw
    with ExitStack() as ctx:
        tag = f"mod{layer}_"
        sb = lambda n, s, d=F32: ctx.enter_context(nc.sbuf_tensor(tag + n, s, d))
        ps = lambda n, s, d=F32: ctx.enter_context(nc.psum_tensor(tag + n, s, d))
        sem = semaphores(nc, ctx, tag)
        w_raw = sb("w_raw", [P, n_raw, KD * BANK])
        w_hi = sb("w_hi", [P, 2, KD * BANK], F32R)
        w_lo = sb("w_lo", [P, 2, KD * BANK], F32R)
        rows = sb("rows", [4, 2, BANK])
        row_ps = ps("row_ps", [4, 2, BANK])
        col_ps = ps("col_ps", [P, 2, BANK])
        w_loaded = [sem(f"w_loaded{j}") for j in range(n_raw)]
        w_high, w_low, rows_done, row_copied, turned, mod_added = (
            sem("w_high"), sem("w_low"), sem("rows_done"), sem("row_copied"), sem("turned"), sem("mod_added"))
        affine = sem("affine")
        block = ctx.enter_context(nc.Block(no_gpsimd_drain=True))

        @block.sync
        def _(sp):
            with sp.Fori(0, n_bodies) as i:
                for u in range(n_raw):
                    sp.wait_ge(w_low, n_raw * i + u + 1)
                    sp.dma_start(w_raw[:, u, :], flat(g.w_mod[layer][bass.ds(n_raw * i + u, 1)])
                                 ).then_inc(w_loaded[u], 16)

        @block.scalar
        def _(act):
            with act.Fori(0, n_bodies) as i:
                for u in range(n_raw):
                    act.wait_ge(rows_done, n_raw * i + u + 1)
                    act.wait_ge(w_loaded[u], 16 * i + 16)
                    nc.scalar.copy(w_hi[:, u % 2, :], w_raw[:, u, :]).then_inc(w_high, 1)

        @block.tensor
        def _(pe):
            def products(i, u):
                pe.wait_ge(row_copied, n_raw * i + u + 1)
                pe.wait_ge(w_low, n_raw * i + u + 1 + n_raw)
                for k in range(KD):
                    for j, w in enumerate((w_hi, w_lo)):
                        last = nc.tensor.matmul(row_ps[:, u % 2, :], g.silu_parts[:, k, :],
                                                w[:, u % 2, k * BANK:(k + 1) * BANK],
                                                start=(k == 0 and j == 0), stop=(k == KD - 1 and j == 1))
                last.then_inc(rows_done, 1)

            def turn(i, u):
                pe.wait_ge(row_copied, n_raw * i + u + 3)
                pe.wait_ge(mod_added, n_raw * i + u + 1)
                for j in range(4):
                    last = nc.tensor.matmul(col_ps[:, u % 2, 2 * j:2 * j + 2], rows[:, u % 2, j * P:(j + 1) * P],
                                            g.pair_sum[:, :], start=True, stop=True)
                last.then_inc(turned, 1)

            def body(i, more):
                for u in range(n_raw):
                    if u + 1 < n_raw:
                        products(i, u + 1)
                    elif more:
                        products(i + 1, 0)
                    turn(i, u)

            pe.sem_inc(rows_done, 2)
            products(0, 0)
            with pe.Fori(0, n_bodies - 1) as i:
                body(i, True)
            body(n_bodies - 1, False)

        @block.vector
        def _(dve):
            dve.sem_inc(w_low, n_raw)
            dve.sem_inc(row_copied, 2)
            dve.sem_inc(mod_added, 2)

            def low(i, u):
                dve.wait_ge(w_high, n_raw * i + u + 1)
                nc.vector.tensor_tensor(w_lo[:, u % 2, :], w_raw[:, u % n_raw, :], w_hi[:, u % 2, :].bitcast(F32),
                                        ALU.subtract).then_inc(w_low, 1)

            def copy_rows(i, u):
                dve.wait_ge(rows_done, n_raw * i + u + 3)
                nc.vector.tensor_copy(rows[:, u % 2, :], row_ps[:, u % 2, :]).then_inc(row_copied, 1)

            def add(i, u):
                dve.wait_ge(turned, n_raw * i + u + 1)
                nc.vector.tensor_tensor(
                    g.mod_t[:, bass.ds(4 * n_raw * i + 4 * u, 4), :],
                    col_ps[:, u % 2, 0:8].rearrange("p (j s) -> p j s", s=2),
                    g.b_mod[:, layer, bass.ds(4 * n_raw * i + 4 * u, 4), :], ALU.add,
                ).then_inc(mod_added, 1)

            def body(i, more):
                for u in range(n_raw):
                    if u + 2 < n_raw or more:
                        low(i, u + 2)
                    if u + 1 < n_raw or more:
                        copy_rows(i, u + 1)
                    add(i, u)

            low(0, 0)
            low(0, 1)
            copy_rows(0, 0)
            with dve.Fori(0, n_bodies - 1) as i:
                body(i, True)
            body(n_bodies - 1, False)
            dve.wait_ge(mod_added, 2 + n_chunks)
            for j, gain in ((0, g.gain1), (1, g.gain2)):
                scale = g.mod_t[:, (3 * j + 1) * KD:(3 * j + 2) * KD, :]
                nc.vector.tensor_scalar(gain[:, :, :], scale, 1.0, None, ALU.add).then_inc(affine, 1)
            dve.wait_ge(affine, 2)
            for j, gain in ((0, g.gain1), (1, g.gain2)):
                nc.vector.tensor_tensor(gain[:, :, :], gain[:, :, :], g.norms[:, layer, j, :, :],
                                        ALU.mult).then_inc(affine, 1)


def norm(nc, g, tag, src, n_k, gain, shift, out_hi, out_lo, chunks, out_dram=None):
    width = n_k * P
    with ExitStack() as ctx:
        sb = lambda n, s, d=F32: ctx.enter_context(nc.sbuf_tensor(tag + n, s, d))
        sem = semaphores(nc, ctx, tag)
        squares = sb("squares", [P, 2, BANK])
        root = sb("root", [P, 2, BANK])
        rinv = sb("rinv", [P, 2, BANK])
        n_t = 4
        scaled = sb("scaled", [P, n_t, BANK])
        ssq = ctx.enter_context(nc.psum_tensor(tag + "ssq", [P, 2, BANK], F32))
        sq_ready, ssq_added, root_ready, rinv_ready = (
            sem("sq_ready"), sem("ssq_added"), sem("root_ready"), sem("rinv_ready"))
        t_ready, hi_ready, lo_ready = sem("t_ready"), sem("hi_ready"), sem("lo_ready")
        stored = [sem(f"stored{j}") for j in range(n_t)] if out_dram is not None else None
        n_c = len(chunks)
        block = ctx.enter_context(nc.Block(no_gpsimd_drain=True))

        @block.scalar
        def _(act):
            def square_chunk(ci):
                t0, n = chunks[ci]
                for k in range(n_k):
                    s = ci * n_k + k
                    if s >= 2:
                        act.wait_ge(ssq_added, s - 1)
                    nc.scalar.activation(squares[:, s % 2, 0:n], src[:, k, t0:t0 + n],
                                         ACT.Square).then_inc(sq_ready, 1)

            def root_chunk(ci):
                n = chunks[ci][1]
                act.wait_ge(ssq_added, (ci + 1) * n_k)
                if ci >= 2:
                    act.wait_ge(rinv_ready, ci - 1)
                nc.scalar.activation(root[:, ci % 2, 0:n], ssq[:, ci % 2, 0:n], ACT.Sqrt,
                                     bias=g.eps[:, 0:1], scale=1.0 / width).then_inc(root_ready, 1)

            def hi_chunk(ci):
                if out_dram is not None:
                    return
                t0, n = chunks[ci]
                for k in range(n_k):
                    s = ci * n_k + k
                    act.wait_ge(t_ready, s + 1)
                    bias = shift(k, stream_of(chunks[ci])) if shift else 0.0
                    nc.scalar.activation(out_hi[:, k, t0:t0 + n], scaled[:, s % n_t, 0:n], ACT.Identity,
                                         bias=bias).then_inc(hi_ready, 1)

            for ci in range(n_c):
                square_chunk(ci)
                if ci:
                    hi_chunk(ci - 1)
                root_chunk(ci)
            hi_chunk(n_c - 1)

        @block.tensor
        def _(pe):
            for ci, (_, n) in enumerate(chunks):
                if ci >= 2:
                    pe.wait_ge(root_ready, ci - 1)
                for k in range(n_k):
                    pe.wait_ge(sq_ready, ci * n_k + k + 1)
                    nc.tensor.matmul(ssq[:, ci % 2, 0:n], g.ones[:, :], squares[:, (ci * n_k + k) % 2, 0:n],
                                     start=(k == 0), stop=(k == n_k - 1)).then_inc(ssq_added, 1)

        @block.vector
        def _(dve):
            def lo_of(s):
                ci, k = divmod(s, n_k)
                t0, n = chunks[ci]
                dve.wait_ge(hi_ready, s + 1)
                hi = out_hi[:, k, t0:t0 + n].bitcast(F32)
                lo = out_lo[:, k, t0:t0 + n]
                t = scaled[:, s % n_t, 0:n]
                if shift:
                    nc.vector.scalar_tensor_tensor(lo, t, shift(k, stream_of(chunks[ci])), hi,
                                                   ALU.add, ALU.subtract).then_inc(lo_ready, 1)
                else:
                    nc.vector.tensor_tensor(lo, t, hi, ALU.subtract).then_inc(lo_ready, 1)

            for ci, (t0, n) in enumerate(chunks):
                dve.wait_ge(root_ready, ci + 1)
                if ci >= 2:
                    dve.wait_ge(t_ready, (ci - 1) * n_k)
                nc.vector.reciprocal(rinv[:, ci % 2, 0:n], root[:, ci % 2, 0:n]).then_inc(rinv_ready, 1)
                dve.wait_ge(rinv_ready, ci + 1)
                for k in range(n_k):
                    s = ci * n_k + k
                    if out_dram is not None and s >= n_t:
                        dve.wait_ge(stored[s % n_t], 16 * (s // n_t))
                    if out_dram is None and s >= n_t:
                        dve.wait_ge(lo_ready, s - n_t + 1)
                    nc.vector.scalar_tensor_tensor(
                        scaled[:, s % n_t, 0:n], src[:, k, t0:t0 + n], gain(k, stream_of(chunks[ci])),
                        rinv[:, ci % 2, 0:n], ALU.mult, ALU.mult).then_inc(t_ready, 1)
                    if out_dram is None and s >= 2:
                        lo_of(s - 2)
            if out_dram is None:
                for s in range(max(0, n_c * n_k - 2), n_c * n_k):
                    lo_of(s)

        if out_dram is not None:
            @block.sync
            def _(sp):
                for s in range(n_c * n_k):
                    ci, k = divmod(s, n_k)
                    t0, n = chunks[ci]
                    sp.wait_ge(t_ready, s + 1)
                    sp.dma_start(out_dram[k * P:(k + 1) * P, t0 - CTX:t0 - CTX + n],
                                 scaled[:, s % n_t, 0:n]).then_inc(stored[s % n_t], 16)
                for j in range(n_t):
                    sp.wait_ge(stored[j], 16 * len(range(j, n_c * n_k, n_t)))


class Split:

    def __init__(self, nc, ctx, tag, n_k, sem, slots=2):
        self.nc, self.n_k, self.slots = nc, n_k, slots
        width = n_k * P
        self.raw = ctx.enter_context(nc.sbuf_tensor(tag + "w_raw", [P, slots, width], F32))
        self.hi = ctx.enter_context(nc.sbuf_tensor(tag + "w_hi", [P, slots, width], F32R))
        self.lo = ctx.enter_context(nc.sbuf_tensor(tag + "w_lo", [P, slots, width], F32R))
        self.loaded = [sem(f"w_loaded{j}") for j in range(slots)]
        self.hi_done = sem("w_hi_done")
        self.lo_done = sem("w_lo_done")

    def passes(self, slot, k, x_hi, x_lo):
        w_hi, w_lo = (x[:, slot, k * P:(k + 1) * P] for x in (self.hi, self.lo))
        return ((w_hi, x_hi), (w_hi, x_lo), (w_lo, x_hi))

    def high(self, slot):
        return self.nc.scalar.copy(self.hi[:, slot, :], self.raw[:, slot, :]).then_inc(self.hi_done, 1)

    def low(self, slot):
        return self.nc.gpsimd.tensor_tensor(self.lo[:, slot, :], self.raw[:, slot, :],
                                            self.hi[:, slot, :].bitcast(F32), ALU.subtract
                                            ).then_inc(self.lo_done, 1)


def project(nc, g, tag, w_dram, src_hi, src_lo, n_k, n_tiles, chunks, mode, dst, scale=1.0, gains=None,
            turn=None, cos=None, sin=None):
    n_c = len(chunks)
    per = 2 * n_c
    n_bodies = n_tiles // 2
    assert n_tiles % 2 == 0
    rotated = mode != "plain"
    normed = mode == "norm_rope"
    with ExitStack() as ctx:
        sb = lambda n, s, d=F32: ctx.enter_context(nc.sbuf_tensor(tag + n, s, d))
        ps = lambda n, s, d=F32: ctx.enter_context(nc.psum_tensor(tag + n, s, d))
        sem = semaphores(nc, ctx, tag)
        w = Split(nc, ctx, tag, n_k, sem)
        hi_out = sb("hi_out", [P, 2, BANK], F32R)
        lo_out = sb("lo_out", [P, 2, BANK], F32R)
        acc = ps("acc", [P, 2, 3, BANK])
        acc_done = sem("acc_done")
        hi_done, lo_done = sem("hi_done"), sem("lo_done")
        lo_start = 0 if rotated else per
        stored = [sem("stored0"), sem("stored1")]
        if rotated:
            aux = ps("aux", [P, 2, BANK])
            base = sb("base", [P, 2, BANK])
            with_cos = sb("with_cos", [P, 2, BANK])
            with_sin = sb("with_sin", [P, 2, BANK])
            whole = sb("whole", [P, 2, BANK])
            base_done, cos_done, turn_done, sin_done, whole_done = (
                sem("base_done"), sem("cos_done"), sem("turn_done"), sem("sin_done"), sem("whole_done"))
        if normed:
            squares = sb("squares", [P, 2, BANK])
            root = sb("root", [P, 2, BANK])
            rinv = sb("rinv", [P, 2, BANK])
            sq_done, ssq_done, root_done, rinv_done = (
                sem("sq_done"), sem("ssq_done"), sem("root_done"), sem("rinv_done"))
        acc_free = base_done if rotated else lo_done
        block = ctx.enter_context(nc.Block(no_gpsimd_drain=True))

        @block.sync
        def _(sp):
            sp.sem_inc(stored[0], 16)
            sp.sem_inc(stored[1], 16)

            def load(i):
                for u in range(2):
                    sp.wait_ge(w.lo_done, 2 * i + u + 1)
                    sp.dma_start(w.raw[:, u, :], w_dram[bass.ds(2 * i + u, 1)].rearrange("a p n -> p (a n)")
                                 ).then_inc(w.loaded[u], 16)

            def store(i):
                for b in range(per):
                    u, c = divmod(b, n_c)
                    t0, n = chunks[c]
                    sp.wait_ge(lo_done, per * i + b + 1 + lo_start)
                    for part, tile in ((1, lo_out), (0, hi_out)):
                        sp.dma_start(dst(part, 2 * i + u, t0, n), tile[:, b % 2, 0:n].bitcast(F32)).then_inc(stored[b % 2], 16)

            load(0)
            if n_bodies > 1:
                with sp.Fori(0, n_bodies - 1) as i:
                    load(i + 1)
                    store(i)
            store(n_bodies - 1)
            for j in range(2):
                sp.wait_ge(stored[j], 16 + 32 * (per // 2) * n_bodies)

        @block.tensor
        def _(pe):
            pe.sem_inc(acc_done, per)
            with pe.Fori(0, n_bodies) as i:
                def main(b):
                    u, c = divmod(b, n_c)
                    t0, n = chunks[c]
                    if c == 0:
                        pe.wait_ge(w.lo_done, 2 * i + u + 3)
                    pe.wait_ge(acc_free, per * i + b + 1)
                    for k in range(n_k):
                        for j, (a, x) in enumerate(w.passes(u, k, src_hi[:, k, t0:t0 + n], src_lo[:, k, t0:t0 + n])):
                            last = nc.tensor.matmul(acc[:, u, c, 0:n], a, x, start=(k == 0 and j == 0),
                                                    stop=(k == n_k - 1 and j == 2))
                    last.then_inc(acc_done, 1)

                def head_sums(b):
                    n = chunks[b % n_c][1]
                    pe.wait_ge(sq_done, per * i + b + 1)
                    pe.wait_ge(root_done, per * i + b + 1)
                    nc.tensor.matmul(aux[:, 0, 0:n], g.head_ones[:, :], squares[:, b % 2, 0:n], start=True,
                                     stop=True).then_inc(ssq_done, 1)

                def turned(b):
                    n = chunks[b % n_c][1]
                    pe.wait_ge(base_done, per * i + b + 1 + per)
                    pe.wait_ge(sin_done, per * i + b + 1)
                    nc.tensor.matmul(aux[:, 1, 0:n], turn[:, :], base[:, b % 2, 0:n], start=True,
                                     stop=True).then_inc(turn_done, 1)

                for b in range(per + (2 if rotated else 0)):
                    if b < per:
                        main(b)
                    if normed and 1 <= b <= per:
                        head_sums(b - 1)
                    if rotated and b >= 2:
                        turned(b - 2)

        @block.scalar
        def _(act):
            if normed:
                act.sem_inc(root_done, 1)

            def split(i, u):
                act.wait_ge(w.loaded[u], 16 * i + 16)
                act.wait_ge(acc_done, per * i + n_c * (u + 1))
                w.high(u)

            def square(i, b):
                u, c = divmod(b, n_c)
                n = chunks[c][1]
                act.wait_ge(acc_done, per * i + b + 1 + per)
                nc.scalar.activation(squares[:, b % 2, 0:n], acc[:, u, c, 0:n], ACT.Square).then_inc(sq_done, 1)

            def take_root(i, b):
                n = chunks[b % n_c][1]
                act.wait_ge(ssq_done, per * i + b + 1)
                nc.scalar.activation(root[:, b % 2, 0:n], aux[:, 0, 0:n], ACT.Sqrt, bias=g.eps[:, 0:1],
                                     scale=1.0 / GQA_HD).then_inc(root_done, 1)

            def high(i, b):
                u, c = divmod(b, n_c)
                n = chunks[c][1]
                act.wait_ge(stored[b % 2], 32 * ((per // 2) * i + b // 2) + 16)
                if rotated:
                    act.wait_ge(whole_done, per * i + b + 1)
                    nc.scalar.copy(hi_out[:, b % 2, 0:n], whole[:, b % 2, 0:n]).then_inc(hi_done, 1)
                else:
                    act.wait_ge(acc_done, per * i + b + 1 + per)
                    nc.scalar.mul(hi_out[:, b % 2, 0:n], acc[:, u, c, 0:n], scale).then_inc(hi_done, 1)

            def body(i, more):
                for b in range(per + 2):
                    if more and b in (n_c, per):
                        split(i + 1, b // n_c - 1)
                    if normed and b < per:
                        square(i, b)
                    if normed and 1 <= b <= per:
                        take_root(i, b - 1)
                    if rotated and b >= 2:
                        high(i, b - 2)
                    if not rotated and b < per:
                        high(i, b)

            split(0, 0)
            split(0, 1)
            if n_bodies > 1:
                with act.Fori(0, n_bodies - 1) as i:
                    body(i, True)
            body(n_bodies - 1, False)

        @block.gpsimd
        def _(pool):
            pool.sem_inc(w.lo_done, 2)

            def split(i, u):
                pool.wait_ge(w.hi_done, 2 * i + u + 1)
                w.low(u)

            def cosine(i, b):
                t0, n = chunks[b % n_c]
                pool.wait_ge(base_done, per * i + b + 1 + per)
                nc.gpsimd.tensor_tensor(with_cos[:, b % 2, 0:n], base[:, b % 2, 0:n], cos[:, t0:t0 + n],
                                        ALU.mult).then_inc(cos_done, 1)

            def add(i, b):
                n = chunks[b % n_c][1]
                pool.wait_ge(cos_done, per * i + b + 1)
                pool.wait_ge(sin_done, per * i + b + 2)
                nc.gpsimd.tensor_tensor(whole[:, b % 2, 0:n], with_cos[:, b % 2, 0:n],
                                        with_sin[:, b % 2, 0:n], ALU.add).then_inc(whole_done, 1)

            def low(i, b):
                n = chunks[b % n_c][1]
                pool.wait_ge(hi_done, per * i + b + 1)
                nc.gpsimd.tensor_tensor(lo_out[:, b % 2, 0:n], whole[:, b % 2, 0:n],
                                        hi_out[:, b % 2, 0:n].bitcast(F32), ALU.subtract).then_inc(lo_done, 1)
                pool.wait_ge(lo_done, per * i + b + 1)

            def body(i, more):
                for b in range(per + 1):
                    if more and b in (n_c, per):
                        split(i + 1, b // n_c - 1)
                    if rotated:
                        if b < per:
                            cosine(i, b)
                        if b >= 1:
                            low(i, b - 1)
                        if b < per:
                            add(i, b)

            split(0, 0)
            split(0, 1)
            if n_bodies > 1:
                with pool.Fori(0, n_bodies - 1) as i:
                    body(i, True)
            if rotated:
                body(n_bodies - 1, False)

        @block.vector
        def _(dve):
            dve.sem_inc(acc_free, per)
            if rotated:
                dve.sem_inc(sin_done, 1)
            with dve.Fori(0, n_bodies) as i:
                def make_base(b):
                    u, c = divmod(b, n_c)
                    n = chunks[c][1]
                    if normed:
                        dve.wait_ge(root_done, per * i + b + 2)
                        nc.vector.reciprocal(rinv[:, b % 2, 0:n], root[:, b % 2, 0:n]).then_inc(rinv_done, 1)
                        dve.wait_ge(rinv_done, per * i + b + 1)
                        nc.vector.scalar_tensor_tensor(base[:, b % 2, 0:n], acc[:, u, c, 0:n],
                                                       gains[:, bass.ds(2 * i + u, 1)], rinv[:, b % 2, 0:n],
                                                       ALU.mult, ALU.mult).then_inc(base_done, 1)
                    else:
                        dve.wait_ge(acc_done, per * i + b + 1 + per)
                        nc.vector.tensor_scalar(base[:, b % 2, 0:n], acc[:, u, c, 0:n], scale, None,
                                                ALU.mult).then_inc(base_done, 1)

                def sine(b):
                    t0, n = chunks[b % n_c]
                    dve.wait_ge(cos_done, per * i + b + 1)
                    dve.wait_ge(turn_done, per * i + b + 1)
                    nc.vector.tensor_tensor(with_sin[:, b % 2, 0:n], aux[:, 1, 0:n], sin[:, t0:t0 + n],
                                            ALU.mult).then_inc(sin_done, 1)

                for b in range(per + (1 if rotated else 0)):
                    if rotated:
                        if b < per:
                            make_base(b)
                        if b >= 1:
                            sine(b - 1)
                    else:
                        u, c = divmod(b, n_c)
                        n = chunks[c][1]
                        dve.wait_ge(hi_done, per * i + b + 1)
                        nc.vector.scalar_tensor_tensor(lo_out[:, b % 2, 0:n], acc[:, u, c, 0:n], scale,
                                                       hi_out[:, b % 2, 0:n].bitcast(F32), ALU.mult,
                                                       ALU.subtract).then_inc(lo_done, 1)


def accumulate(nc, g, tag, w_dram, src_hi, src_lo, n_k, n_tiles, chunks, dst, gate=None, whole=None):
    n_c = len(chunks)
    per = 2 * n_c
    n_bodies = n_tiles // 2
    with ExitStack() as ctx:
        sem = semaphores(nc, ctx, tag)
        w = Split(nc, ctx, tag, n_k, sem)
        acc = ctx.enter_context(nc.psum_tensor(tag + "acc", [P, 2, 3, BANK], F32))
        acc_done, added = sem("acc_done"), sem("added")
        src_high, src_low = sem("src_high"), sem("src_low")
        t_first = min(t0 for t0, _ in chunks)
        n_bodies_first = 1 if whole is not None else 0
        block = ctx.enter_context(nc.Block(no_gpsimd_drain=True))

        @block.sync
        def _(sp):
            with sp.Fori(0, n_bodies) as i:
                for u in range(2):
                    sp.wait_ge(w.lo_done, 2 * i + u + 1)
                    sp.dma_start(w.raw[:, u, :], w_dram[bass.ds(2 * i + u, 1)].rearrange("a p n -> p (a n)")
                                 ).then_inc(w.loaded[u], 16)

        @block.scalar
        def _(act):
            def split(i, u):
                act.wait_ge(w.loaded[u], 16 * i + 16)
                act.wait_ge(acc_done, per * i + n_c * (u + 1))
                w.high(u)

            if whole is not None:
                for k in range(n_k):
                    nc.scalar.copy(src_hi[:, k, t_first:TOK], whole[:, k, t_first:TOK]).then_inc(src_high, 1)
                    if k < 2:
                        split(0, k)
            with act.Fori(n_bodies_first, n_bodies) as i:
                for u in range(2):
                    split(i, u)

        @block.gpsimd
        def _(pool):
            pool.sem_inc(w.lo_done, 2)
            with pool.Fori(0, n_bodies) as i:
                for u in range(2):
                    pool.wait_ge(w.hi_done, 2 * i + u + 1)
                    w.low(u)

        @block.tensor
        def _(pe):
            pe.sem_inc(acc_done, per)

            def body(i, first=False):
                for u in range(2):
                    pe.wait_ge(w.lo_done, 2 * i + u + 3)
                    k_groups = [[k] for k in range(n_k)] if first and u == 0 else [range(n_k)]
                    for ks in k_groups:
                        if first and u == 0:
                            pe.wait_ge(src_low, ks[0] + 1)
                        for c, (t0, n) in enumerate(chunks):
                            if ks[0] == 0:
                                pe.wait_ge(added, per * i + n_c * u + c + 1)
                            for k in ks:
                                for j, (a, x) in enumerate(
                                        w.passes(u, k, src_hi[:, k, t0:t0 + n], src_lo[:, k, t0:t0 + n])):
                                    last = nc.tensor.matmul(acc[:, u, c, 0:n], a, x, start=(k == 0 and j == 0),
                                                            stop=(k == n_k - 1 and j == 2))
                            if ks[-1] == n_k - 1:
                                last.then_inc(acc_done, 1)

            if whole is not None:
                body(0, first=True)
            with pe.Fori(n_bodies_first, n_bodies) as i:
                body(i)

        @block.vector
        def _(dve):
            dve.sem_inc(added, per)
            if whole is not None:
                for k in range(n_k):
                    dve.wait_ge(src_high, k + 1)
                    nc.vector.tensor_tensor(src_lo[:, k, t_first:TOK], whole[:, k, t_first:TOK],
                                            src_hi[:, k, t_first:TOK].bitcast(F32), ALU.subtract
                                            ).then_inc(src_low, 1)
            with dve.Fori(0, n_bodies) as i:
                for u in range(2):
                    for c, (t0, n) in enumerate(chunks):
                        dve.wait_ge(acc_done, per * i + n_c * u + c + 1 + per)
                        out = dst[:, bass.ds(2 * i + u, 1), t0:t0 + n].rearrange("p a n -> p (a n)")
                        if gate:
                            nc.vector.scalar_tensor_tensor(out, acc[:, u, c, 0:n], gate(2 * i + u, stream_of(chunks[c])),
                                                           out, ALU.mult, ALU.add).then_inc(added, 1)
                        else:
                            nc.vector.tensor_copy(out, acc[:, u, c, 0:n]).then_inc(added, 1)


def values(nc, g, tag, w_dram, src_hi, src_lo, n_k, n_tiles, dst):
    n_c = len(ALL_CHUNKS)
    per = 2 * n_c
    n_bodies = n_tiles // 2
    groups = ((0, 4), (4, 4), (8, 2))
    n_g = len(groups)
    with ExitStack() as ctx:
        sb = lambda n, s, d=F32: ctx.enter_context(nc.sbuf_tensor(tag + n, s, d))
        sem = semaphores(nc, ctx, tag)
        w = Split(nc, ctx, tag, n_k, sem)
        v_t = sb("v_t", [P, 2, TOK])
        v_out = sb("v_out", [P, 2, 2, NKT, P], F32R)
        acc = ctx.enter_context(nc.psum_tensor(tag + "acc", [P, 2, 3, BANK], F32))
        turned_ps = ctx.enter_context(nc.psum_tensor(tag + "turned", [P, 2, BANK], F32))
        acc_done, copied, turned, v_hi, v_lo = (
            sem("acc_done"), sem("copied"), sem("turned"), sem("v_hi"), sem("v_lo"))
        stored = [sem("stored0"), sem("stored1")]
        block = ctx.enter_context(nc.Block(no_gpsimd_drain=True))

        @block.sync
        def _(sp):
            for u in range(2):
                sp.sem_inc(stored[u], 16)

            def load(i):
                for u in range(2):
                    sp.wait_ge(w.lo_done, 2 * i + u + 1)
                    sp.dma_start(w.raw[:, u, :], w_dram[bass.ds(2 * i + u, 1)].rearrange("a p n -> p (a n)")
                                 ).then_inc(w.loaded[u], 16)

            def store(i):
                for u in range(2):
                    sp.wait_ge(v_lo, 2 * n_g * i + n_g * (u + 1) + 2)
                    for h in range(2):
                        sp.dma_start(dst[bass.ds(4 * i + 2 * u + h, 1)].rearrange("a p n -> p (a n)"),
                                     v_out[:, u, h].rearrange("p k n -> p (k n)").bitcast(F32)).then_inc(stored[u], 16)

            load(0)
            if n_bodies > 1:
                with sp.Fori(0, n_bodies - 1) as i:
                    load(i + 1)
                    store(i)
            store(n_bodies - 1)
            for u in range(2):
                sp.wait_ge(stored[u], 16 + 32 * n_bodies)

        @block.gpsimd
        def _(pool):
            pool.sem_inc(w.lo_done, 2)
            with pool.Fori(0, n_bodies) as i:
                for u in range(2):
                    pool.wait_ge(w.hi_done, 2 * i + u + 1)
                    w.low(u)

        @block.tensor
        def _(pe):
            pe.sem_inc(acc_done, per)
            with pe.Fori(0, n_bodies) as i:
                for u in range(2):
                    pe.wait_ge(w.lo_done, 2 * i + u + 3)
                    for c, (t0, n) in enumerate(ALL_CHUNKS):
                        pe.wait_ge(copied, per * i + n_c * u + c + 1)
                        for k in range(n_k):
                            for j, (a, x) in enumerate(
                                    w.passes(u, k, src_hi[:, k, t0:t0 + n], src_lo[:, k, t0:t0 + n])):
                                last = nc.tensor.matmul(acc[:, u, c, 0:n], a, x, start=(k == 0 and j == 0),
                                                        stop=(k == n_k - 1 and j == 2))
                        last.then_inc(acc_done, 1)
                for u in range(2):
                    pe.wait_ge(copied, per * i + n_c * (u + 1) + per)
                    for q, (k0, m) in enumerate(groups):
                        pe.wait_ge(v_lo, 2 * n_g * i + n_g * u + q + 1)
                        for k in range(k0, k0 + m):
                            last = nc.tensor.transpose(turned_ps[:, (n_g * u + q) % 2, (k - k0) * P:(k - k0 + 1) * P],
                                                       v_t[:, u, k * P:(k + 1) * P], g.ident[:, :])
                        last.then_inc(turned, 1)

        def turned_view(u, q, m):
            return turned_ps[:, (n_g * u + q) % 2, 0:m * P].rearrange("p (k h f) -> p h k f", h=2, f=V_DIM)

        @block.scalar
        def _(act):
            def split(i, u):
                act.wait_ge(w.loaded[u], 16 * i + 16)
                act.wait_ge(acc_done, per * i + n_c * (u + 1))
                w.high(u)

            def body(i, more):
                if more:
                    split(i + 1, 0)
                    split(i + 1, 1)
                for u in range(2):
                    for q, (k0, m) in enumerate(groups):
                        if q == 0:
                            act.wait_ge(stored[u], 32 * i + 16)
                        act.wait_ge(turned, 2 * n_g * i + n_g * u + q + 1)
                        nc.scalar.copy(v_out[:, u, :, k0:k0 + m, 0:V_DIM], turned_view(u, q, m)).then_inc(v_hi, 1)

            split(0, 0)
            split(0, 1)
            if n_bodies > 1:
                with act.Fori(0, n_bodies - 1) as i:
                    body(i, True)
            body(n_bodies - 1, False)

        @block.vector
        def _(dve):
            dve.sem_inc(copied, per)
            dve.sem_inc(v_lo, 2)
            with dve.Fori(0, n_bodies) as i:
                for u in range(2):
                    for c, (t0, n) in enumerate(ALL_CHUNKS):
                        dve.wait_ge(acc_done, per * i + n_c * u + c + 1 + per)
                        nc.vector.tensor_copy(v_t[:, u, t0:t0 + n], acc[:, u, c, 0:n]).then_inc(copied, 1)
                for u in range(2):
                    for q, (k0, m) in enumerate(groups):
                        dve.wait_ge(v_hi, 2 * n_g * i + n_g * u + q + 1)
                        nc.vector.tensor_tensor(v_out[:, u, :, k0:k0 + m, V_DIM:2 * V_DIM], turned_view(u, q, m),
                                                v_out[:, u, :, k0:k0 + m, 0:V_DIM].bitcast(F32), ALU.subtract
                                                ).then_inc(v_lo, 1)


def attention(nc, g, tag, load_q, load_k, load_v, rows, passes, o_t):
    n_bodies = HEADS // 2
    CTX_PIECE = 2
    starts = (4, 6, 9, 11)
    ways = ((0, 1, 1, 2, 3, 4), (0, 1, 2, 3, 4, 5))
    scores_at, ctx_exp_at, lat_exp_at, inverse_at = {}, {}, {}, {}
    for q, start in enumerate(starts):
        *pieces, ctx_exp_step, lat_exp_step, inverse_step = (start + d for d in ways[q % 2])
        for c, s in enumerate(pieces):
            scores_at.setdefault((s - 1) % NKT + 1, []).append(((2 - (s - 1) // NKT, q), c))
        for table, s in ((ctx_exp_at, ctx_exp_step), (lat_exp_at, lat_exp_step), (inverse_at, inverse_step)):
            table[(s - 1) % NKT + 1] = (2 - (s - 1) // NKT, q)
    with ExitStack() as ctx:
        sb = lambda n, s, d=F32: ctx.enter_context(nc.sbuf_tensor(tag + n, s, d))
        ps = lambda n, s, d=F32: ctx.enter_context(nc.psum_tensor(tag + n, s, d))
        sem = semaphores(nc, ctx, tag)
        n_qp = 1 + max(a for a, _ in passes)
        q_s = sb("q_s", [P, 2, n_qp, BANK], F32R)
        k_s = sb("k_s", [P, 2, 2, TOK], F32R)
        v_s = sb("v_s", [P, 2, NKT, P], F32R)
        prob = sb("prob", [P, 12, TOK])
        pt_hi = sb("pt_hi", [P, 2, BANK], F32R)
        pt_lo = sb("pt_lo", [P, 2, BANK], F32R)
        max_parts = sb("max_parts", [P, 2, 3])
        neg_max = sb("neg_max", [P, 2, 4])
        total_parts = sb("total_parts", [P, 2, 4, 2])
        total = sb("total", [P, 2, 4])
        r_total = sb("r_total", [P, 2, 4])
        o_a = sb("o_a", [P, 2, BANK])
        o_b = sb("o_b", [P, 2, BANK])
        lat_ps = ps("lat_ps", [P, 2, 2, BANK])
        ctx_ps = ps("ctx_ps", [P, BANK])
        t_ps = ps("t_ps", [P, 2, BANK])
        o_ps = ps("o_ps", [P, BANK])
        q_loaded = [sem("q_loaded0"), sem("q_loaded1")]
        k_loaded = [sem("k_loaded0"), sem("k_loaded1")]
        v_loaded = [sem("v_loaded0"), sem("v_loaded1")]
        ctx_scored, lat_scored, max_part, max_done, ctx_exp, lat_exp, total_done, r_done, normed = (
            sem("ctx_scored"), sem("lat_scored"), sem("max_part"), sem("max_done"), sem("ctx_exp"),
            sem("lat_exp"), sem("total_done"), sem("r_done"), sem("normed"))
        turned, hi_done, lo_done, pv_step = sem("turned"), sem("hi_done"), sem("lo_done"), sem("pv_step")
        o_read, o_added = sem("o_read"), sem("o_added")
        n_q, n_k = len(load_q(0, 0, CTX)), len(load_k(0, 0))
        block = ctx.enter_context(nc.Block(no_gpsimd_drain=True))

        def prob_tile(un, q):
            return prob[:, (un % 4) * 2 + q if q < 2 else 8 + (un % 2) * 2 + q - 2, :]

        def steps(units, more, step):
            for un in units:
                for k in range(1, NKT + 1):
                    step(un, k, k < NKT and un >= 0 or k == NKT and -1 <= un and (un < 3 or more))

        def exists(un, more):
            return 0 <= un and (un < 4 or more)

        def pieces_at(table, un, k, more):
            return [(un + ahead, q, c) for (ahead, q), c in table.get(k, []) if exists(un + ahead, more)]

        def tile_at(table, un, k, more):
            if k not in table:
                return None
            ahead, q = table[k]
            return (un + ahead, q) if exists(un + ahead, more) else None

        def o_rows(tile, un):
            r0 = V_DIM * (un // 2)
            return tile[r0:r0 + V_DIM, un % 2, :]

        way_in, whole_body = (-2, -1), range(4)

        @block.sync
        def _(sp):
            def get_q(i, un):
                for src, part, r0, r in load_q(i, un // 2, CTX + BANK * (un % 2)):
                    sp.dma_start(q_s[r0:r0 + r, un % 2, part, :].bitcast(F32), src).then_inc(q_loaded[un % 2], 16)

            def get_k(i, h):
                for src, part, r0, r in load_k(i, h):
                    sp.dma_start(k_s[r0:r0 + r, h, part, :].bitcast(F32), src).then_inc(k_loaded[h], 16)

            def get_v(i, h):
                sp.dma_start(v_s[:, h].rearrange("p k n -> p (k n)").bitcast(F32), load_v(i, h)
                             ).then_inc(v_loaded[h], 16)

            def output_of(i, un):
                sp.wait_ge(pv_step, 40 * i + 10 * un + 10 + 2)

            def scores_of(i, un):
                sp.wait_ge(ctx_scored, 16 * i + 4 * un + 4)

            def body(i, more):
                scores_of(i, 1)
                get_q(i, 3)
                if more:
                    get_k(i + 1, 0)
                    scores_of(i, 2)
                    get_q(i + 1, 0)
                    output_of(i, 1)
                    get_v(i + 1, 0)
                    scores_of(i, 3)
                    get_q(i + 1, 1)
                    get_k(i + 1, 1)
                    scores_of(i + 1, 0)
                    get_q(i + 1, 2)
                    output_of(i, 3)
                    get_v(i + 1, 1)

            get_q(0, 0)
            get_k(0, 0)
            get_q(0, 1)
            get_v(0, 0)
            get_k(0, 1)
            get_v(0, 1)
            scores_of(0, 0)
            get_q(0, 2)
            with sp.Fori(0, n_bodies - 1) as i:
                body(i, True)
            body(n_bodies - 1, False)

        @block.tensor
        def _(pe):
            def score(out, un, q, lo, hi):
                for j, (a, b) in enumerate(passes):
                    last = nc.tensor.matmul(out, q_s[0:rows, un % 2, a, q * P:(q + 1) * P],
                                            k_s[0:rows, (un // 2) % 2, b, lo:hi], start=(j == 0),
                                            stop=(j == len(passes) - 1))
                return last

            def scores(i, un, q, c):
                m = 16 * i + 4 * un + q
                if q == 0 and c == 0:
                    pe.wait_ge(q_loaded[un % 2], 16 * n_q * (2 * i + un // 2 + 1))
                    pe.wait_ge(k_loaded[(un // 2) % 2], 16 * n_k * (i + un // 4 + 1))
                if c == CTX_PIECE:
                    pe.wait_ge(ctx_exp, m + 1)
                    score(ctx_ps[:, 0:CTX], un, q, 0, CTX).then_inc(ctx_scored, 1)
                else:
                    if c == 0:
                        pe.wait_ge(lat_exp, m + 1)
                    score(lat_ps[:, q % 2, c, :], un, q, CTX + c * BANK, CTX + (c + 1) * BANK
                          ).then_inc(lat_scored, 1)

            def turn(i, un, k):
                if k == 0:
                    pe.wait_ge(normed, 16 * i + 4 * un + 4)
                pe.wait_ge(lo_done, 40 * i + 10 * un + k + 1)
                for q in range(4):
                    last = nc.tensor.transpose(t_ps[:, k % 2, q * P:(q + 1) * P],
                                               prob_tile(un, q)[:, k * P:(k + 1) * P], g.ident[:, :])
                last.then_inc(turned, 1)

            def weigh(i, un, k):
                if k == 0:
                    pe.wait_ge(v_loaded[un // 2], 16 * (i + 1))
                    pe.wait_ge(o_read, 4 * i + un + 1)
                pe.wait_ge(lo_done, 40 * i + 10 * un + k + 1 + 2)
                for j, pt in enumerate((pt_hi, pt_lo)):
                    last = nc.tensor.matmul(o_ps[:, :], v_s[:, un // 2, k, :], pt[:, k % 2, :],
                                            start=(k == 0 and j == 0), stop=(k == NKT - 1 and j == 1))
                last.then_inc(pv_step, 1)

            def body(i, more, units=whole_body):
                def step(un, k, turns):
                    if turns:
                        turn(i, un + k // NKT, k % NKT)
                    for piece in pieces_at(scores_at, un, k, more):
                        scores(i, *piece)
                    if un >= 0:
                        weigh(i, un, k - 1)

                steps(units, more, step)

            pe.sem_inc(pv_step, 2)
            body(0, True, way_in)
            with pe.Fori(0, n_bodies - 1) as i:
                body(i, True)
            body(n_bodies - 1, False)

        @block.vector
        def _(dve):
            def row_max(i, un, q, c):
                m = 16 * i + 4 * un + q
                if c == CTX_PIECE:
                    dve.wait_ge(ctx_scored, m + 1)
                    scores = ctx_ps[:, 0:CTX]
                else:
                    dve.wait_ge(lat_scored, 2 * m + c + 1)
                    scores = lat_ps[:, q % 2, c, :]
                nc.vector.tensor_reduce(max_parts[:, q % 2, c:c + 1], scores, AX_X, ALU.max).then_inc(max_part, 1)
                if c == CTX_PIECE:
                    dve.wait_ge(max_part, 3 * m + 3)
                    nc.vector.tensor_reduce(neg_max[:, un % 2, q:q + 1], max_parts[:, q % 2, :], AX_X, ALU.max,
                                            negate=True).then_inc(max_done, 1)

            def inverse(i, un, q):
                m = 16 * i + 4 * un + q
                dve.wait_ge(lat_exp, m + 1 + 2)
                nc.vector.tensor_tensor(total[:, un % 2, q:q + 1], total_parts[:, un % 2, q, 0:1],
                                        total_parts[:, un % 2, q, 1:2], ALU.add).then_inc(total_done, 1)
                dve.wait_ge(total_done, m + 1)
                nc.vector.reciprocal(r_total[:, un % 2, q:q + 1], total[:, un % 2, q:q + 1]).then_inc(r_done, 1)

            def low(i, un, k):
                dve.wait_ge(hi_done, 40 * i + 10 * un + k + 1)
                nc.vector.tensor_tensor(pt_lo[:, k % 2, :], t_ps[:, k % 2, :], pt_hi[:, k % 2, :].bitcast(F32),
                                        ALU.subtract).then_inc(lo_done, 1)

            def body(i, more, units=whole_body):
                def step(un, k, turns):
                    if turns:
                        low(i, un + k // NKT, k % NKT)
                    for piece in pieces_at(scores_at, un, k, more):
                        row_max(i, *piece)
                    if tile := tile_at(inverse_at, un, k, more):
                        inverse(i, *tile)

                steps(units, more, step)

            dve.sem_inc(lo_done, 2)
            body(0, True, way_in)
            with dve.Fori(0, n_bodies - 1) as i:
                body(i, True)
            body(n_bodies - 1, False)

        @block.scalar
        def _(act):
            def ctx_exponent(i, un, q):
                act.wait_ge(max_done, 16 * i + 4 * un + q + 1)
                nc.scalar.activation(prob_tile(un, q)[:, 0:CTX], ctx_ps[:, 0:CTX], ACT.Exp,
                                     bias=neg_max[:, un % 2, q:q + 1],
                                     accum_out=total_parts[:, un % 2, q, 1:2]).then_inc(ctx_exp, 1)

            def lat_exponent(i, un, q):
                act.wait_ge(max_done, 16 * i + 4 * un + q + 1)
                nc.scalar.activation(prob_tile(un, q)[:, CTX:TOK], lat_ps[:, q % 2].rearrange("p c n -> p (c n)"),
                                     ACT.Exp, bias=neg_max[:, un % 2, q:q + 1],
                                     accum_out=total_parts[:, un % 2, q, 0:1]).then_inc(lat_exp, 1)

            def high(i, un, k):
                act.wait_ge(pv_step, 40 * i + 10 * un + k + 1)
                act.wait_ge(turned, 40 * i + 10 * un + k + 1)
                nc.scalar.copy(pt_hi[:, k % 2, :], t_ps[:, k % 2, :]).then_inc(hi_done, 1)

            def read_out(i, un):
                act.wait_ge(o_added, 2 * i + un % 2 + 1)
                act.wait_ge(pv_step, 40 * i + 10 * un + 10 + 2)
                nc.scalar.copy(o_rows(o_a, un), o_ps[0:V_DIM, :])
                nc.scalar.copy(o_rows(o_b, un), o_ps[V_DIM:2 * V_DIM, :]).then_inc(o_read, 1)

            def body(i, more, units=whole_body):
                def step(un, k, turns):
                    if turns:
                        high(i, un + k // NKT, k % NKT)
                    if tile := tile_at(ctx_exp_at, un, k, more):
                        ctx_exponent(i, *tile)
                    if tile := tile_at(lat_exp_at, un, k, more):
                        lat_exponent(i, *tile)
                    if k == NKT and un >= 0:
                        read_out(i, un)

                steps(units, more, step)

            act.sem_inc(ctx_exp, 1)
            act.sem_inc(lat_exp, 2)
            act.sem_inc(o_read, 1)
            body(0, True, way_in)
            with act.Fori(0, n_bodies - 1) as i:
                body(i, True)
            body(n_bodies - 1, False)

        @block.gpsimd
        def _(pool):
            def normalise(i, un, q):
                pool.wait_ge(r_done, 16 * i + 4 * un + q + 1)
                nc.gpsimd.tensor_tensor(prob_tile(un, q), prob_tile(un, q),
                                        r_total[:, un % 2, q:q + 1].to_broadcast([P, TOK]), ALU.mult
                                        ).then_inc(normed, 1)

            def finish(i, un):
                t0 = CTX + BANK * (un % 2)
                pool.wait_ge(o_read, 4 * i + un + 1 + 1)
                out = o_t[:, bass.ds(i, 1), t0:t0 + BANK].rearrange("p a n -> p (a n)")
                nc.gpsimd.tensor_tensor(out, o_a[:, un % 2, :], o_b[:, un % 2, :], ALU.add).then_inc(o_added, 1)

            def body(i, more, units=whole_body):
                def step(un, k, turns):
                    if tile := tile_at(inverse_at, un, k, more):
                        normalise(i, *tile)
                    if k == NKT and un >= 2:
                        finish(i, un)

                steps(units, more, step)

            pool.sem_inc(o_added, 2)
            body(0, True, way_in)
            with pool.Fori(0, n_bodies - 1) as i:
                body(i, True)
            body(n_bodies - 1, False)


def context_attention(nc, g, tag, load_q, load_k, load_v, o_t):
    group = HEADS // GQA_KV
    n_t = 2 * group
    with ExitStack() as ctx:
        sb = lambda n, s, d=F32: ctx.enter_context(nc.sbuf_tensor(tag + n, s, d))
        ps = lambda n, s, d=F32: ctx.enter_context(nc.psum_tensor(tag + n, s, d))
        sem = semaphores(nc, ctx, tag)
        q_s = sb("q_s", [P, HEADS, CTX], F32R)
        k_s = sb("k_s", [P, GQA_KV, 2, CTX], F32R)
        v_s = sb("v_s", [P, GQA_KV, 2, P], F32R)
        prob = sb("prob", [P, 2, n_t, CTX])
        pt_hi = sb("pt_hi", [P, 2, 2, CTX], F32R)
        pt_lo = sb("pt_lo", [P, 2, 2, CTX], F32R)
        neg_max, total, r_total = sb("neg_max", [P, 2, n_t]), sb("total", [P, 2, n_t]), sb("r_total", [P, 2, n_t])
        o_a, o_b = (sb(n, [P, 2, CTX]) for n in ("o_a", "o_b"))
        s_ps = ps("s_ps", [P, n_t, CTX])
        t_ps = ps("t_ps", [P, 2, BANK])
        o_ps = ps("o_ps", [P, 2, 2 * CTX])
        scored, max_done, exp_done, r_done, normed = (
            sem("scored"), sem("max_done"), sem("exp_done"), sem("r_done"), sem("normed"))
        turned, hi_done, lo_done, weighed = sem("turned"), sem("hi_done"), sem("lo_done"), sem("weighed")
        o_read, o_added = sem("o_read"), sem("o_added")
        loaded = [sem(f"loaded{r}") for r in range(GQA_KV)]
        rounds = range(GQA_KV)
        block = ctx.enter_context(nc.Block(no_gpsimd_drain=True))

        def wide(tile):
            return tile.rearrange("p k n -> p (k n)")

        @block.sync
        def _(sp):
            for r in rounds:
                for part in range(2):
                    rows = slice(64 * part, 64 * part + 64)
                    sp.dma_start(q_s[rows, group * r:group * (r + 1), :].bitcast(F32), load_q(part, group * r, group)
                                 ).then_inc(loaded[r], 16)
                    for half in range(2):
                        sp.dma_start(k_s[64 * half:64 * half + 64, r, part, :].bitcast(F32), load_k(part, r)
                                     ).then_inc(loaded[r], 16)
                sp.dma_start(wide(v_s[:, r]).bitcast(F32), load_v(r)).then_inc(loaded[r], 16)

        @block.tensor
        def _(pe):
            def scores(r):
                if r:
                    pe.wait_ge(exp_done, n_t * r)
                pe.wait_ge(loaded[r], 16 * 7)
                for q in range(n_t):
                    for j in range(2):
                        last = nc.tensor.matmul(s_ps[:, q, :], q_s[:, group * r + q // 2, (q % 2) * P:(q % 2 + 1) * P],
                                                k_s[:, r, j, :], start=(j == 0), stop=(j == 1))
                last.then_inc(scored, 1)

            def turn(e):
                r, j = divmod(e, group)
                pe.wait_ge(normed, n_t * r + 2 * j + 2)
                if e >= 2:
                    pe.wait_ge(lo_done, e - 1)
                for k in range(2):
                    for q in range(2):
                        last = nc.tensor.transpose(t_ps[:, e % 2, (2 * k + q) * P:(2 * k + q + 1) * P],
                                                   prob[:, r % 2, 2 * j + q, k * P:(k + 1) * P], g.ident[:, :])
                last.then_inc(turned, 1)

            def weigh(e):
                r, j = divmod(e, group)
                b = j // 2
                pe.wait_ge(lo_done, e + 1)
                if j % 2 == 0 and r:
                    pe.wait_ge(o_read, 4 * (2 * (r - 1) + b) + 4)
                for k in range(2):
                    for m, pt in enumerate((pt_hi, pt_lo)):
                        last = nc.tensor.matmul(o_ps[:, b, (j % 2) * CTX:(j % 2 + 1) * CTX], v_s[:, r, k, :],
                                                pt[:, e % 2, k, :], start=(k == 0 and m == 0),
                                                stop=(k == 1 and m == 1))
                last.then_inc(weighed, 1)

            scores(0)
            for r in rounds:
                if r + 1 < GQA_KV:
                    scores(r + 1)
                for e in range(group * r, group * (r + 1)):
                    turn(e)
                    if e:
                        weigh(e - 1)
            weigh(group * GQA_KV - 1)

        @block.vector
        def _(dve):
            def low(e):
                dve.wait_ge(hi_done, e + 1)
                nc.vector.tensor_tensor(wide(pt_lo[:, e % 2]), t_ps[:, e % 2, :], wide(pt_hi[:, e % 2]).bitcast(F32),
                                        ALU.subtract).then_inc(lo_done, 1)

            def row_max(r):
                dve.wait_ge(scored, r + 1)
                nc.vector.tensor_reduce(neg_max[:, r % 2, :], s_ps[:, :, :], AX_X, ALU.max, negate=True
                                        ).then_inc(max_done, 1)

            def inverse(r):
                dve.wait_ge(exp_done, n_t * (r + 1))
                nc.vector.reciprocal(r_total[:, r % 2, :], total[:, r % 2, :]).then_inc(r_done, 1)

            row_max(0)
            inverse(0)
            for r in rounds:
                if r + 1 < GQA_KV:
                    row_max(r + 1)
                for e in range(group * r, group * (r + 1)):
                    low(e)
                if r + 1 < GQA_KV:
                    inverse(r + 1)

        @block.scalar
        def _(act):
            def exponents(r):
                act.wait_ge(max_done, r + 1)
                for q in range(n_t):
                    nc.scalar.activation(prob[:, r % 2, q, :], s_ps[:, q, :], ACT.Exp, bias=neg_max[:, r % 2, q:q + 1],
                                         accum_out=total[:, r % 2, q:q + 1]).then_inc(exp_done, 1)

            def high(e):
                if e >= 2:
                    act.wait_ge(weighed, e - 1)
                act.wait_ge(turned, e + 1)
                nc.scalar.copy(wide(pt_hi[:, e % 2]), t_ps[:, e % 2, :]).then_inc(hi_done, 1)

            def read_out(b):
                act.wait_ge(weighed, 2 * b + 2)
                if b >= 2:
                    act.wait_ge(o_added, b - 1)
                for half in range(2):
                    for tile, r0 in ((o_a, 0), (o_b, V_DIM)):
                        nc.scalar.copy(tile[V_DIM * half:V_DIM * (half + 1), b % 2, :],
                                       o_ps[r0:r0 + V_DIM, b % 2, CTX * half:CTX * (half + 1)]).then_inc(o_read, 1)

            exponents(0)
            for r in rounds:
                if r + 1 < GQA_KV:
                    exponents(r + 1)
                for e in range(group * r, group * (r + 1)):
                    high(e)
                    if e % 2 == 0 and e >= 2:
                        read_out(e // 2 - 1)
            read_out(2 * GQA_KV - 1)

        @block.gpsimd
        def _(pool):
            def normalise(r):
                pool.wait_ge(r_done, r + 1)
                for q in range(n_t):
                    nc.gpsimd.tensor_tensor(prob[:, r % 2, q, :], prob[:, r % 2, q, :],
                                            r_total[:, r % 2, q:q + 1].to_broadcast([P, CTX]), ALU.mult
                                            ).then_inc(normed, 1)

            def add_out(b):
                pool.wait_ge(o_read, 4 * b + 4)
                nc.gpsimd.tensor_tensor(o_t[:, b, 0:CTX], o_a[:, b % 2, :], o_b[:, b % 2, :], ALU.add
                                        ).then_inc(o_added, 1)

            normalise(0)
            for r in rounds:
                if r:
                    add_out(2 * r - 1)
                add_out(2 * r)
                if r + 1 < GQA_KV:
                    normalise(r + 1)
            add_out(2 * GQA_KV - 1)


def mlp(nc, g, tag, w_gu, w_down, src_hi, src_lo, chunks, dst, gate):
    n_c = len(chunks)
    n_bodies = NFF // 2
    n_w = 3
    n_gu = 2 * n_c
    n_dn = KD * n_c
    with ExitStack() as ctx:
        sb = lambda n, s, d=F32: ctx.enter_context(nc.sbuf_tensor(tag + n, s, d))
        ps = lambda n, s, d=F32: ctx.enter_context(nc.psum_tensor(tag + n, s, d))
        sem = semaphores(nc, ctx, tag)
        w = Split(nc, ctx, tag, KD, sem, slots=n_w)
        a_hi = sb("a_hi", [P, 2, TOK], F32R)
        a_lo = sb("a_lo", [P, 2, TOK], F32R)
        silu = sb("silu", [P, 3, BANK])
        prod = sb("prod", [P, 2, BANK])
        g_ps = ps("g_ps", [P, 3, BANK])
        u_ps = ps("u_ps", [P, 3, BANK])
        d_ps = ps("d_ps", [P, 2, BANK])
        g_done, u_done, d_done = sem("g_done"), sem("u_done"), sem("d_done")
        silu_done, prod_done, a_high, a_low, added = (
            sem("silu_done"), sem("prod_done"), sem("a_high"), sem("a_low"), sem("added"))
        block = ctx.enter_context(nc.Block(no_gpsimd_drain=True))

        @block.sync
        def _(sp):
            with sp.Fori(0, n_bodies) as i:
                for t in range(6):
                    sp.wait_ge(w.lo_done, 6 * i + t + 1)
                    src = w_gu[bass.ds(4 * i + t, 1)] if t < 4 else w_down[bass.ds(2 * i + t - 4, 1)]
                    sp.dma_start(w.raw[:, t % n_w, :], src.rearrange("a p n -> p (a n)")
                                 ).then_inc(w.loaded[t % n_w], 16)

        @block.gpsimd
        def _(pool):
            pool.sem_inc(w.lo_done, n_w)
            with pool.Fori(0, n_bodies) as i:
                for t in range(6):
                    pool.wait_ge(w.hi_done, 6 * i + t + 1)
                    w.low(t % n_w)

        @block.tensor
        def _(pe):
            pe.sem_inc(u_done, n_gu)
            pe.sem_inc(d_done, n_dn)
            with pe.Fori(0, n_bodies) as i:
                for t in range(4):
                    j, up = divmod(t, 2)
                    bank, done, free = (u_ps, u_done, prod_done) if up else (g_ps, g_done, silu_done)
                    pe.wait_ge(w.lo_done, 6 * i + t + 1 + n_w)
                    for c, (t0, n) in enumerate(chunks):
                        pe.wait_ge(free, n_gu * i + n_c * j + c + 1)
                        for k in range(KD):
                            for m, (a, x) in enumerate(
                                    w.passes(t % n_w, k, src_hi[:, k, t0:t0 + n], src_lo[:, k, t0:t0 + n])):
                                last = nc.tensor.matmul(bank[:, c, 0:n], a, x, start=(k == 0 and m == 0),
                                                        stop=(k == KD - 1 and m == 2))
                        last.then_inc(done, 1)
                pe.wait_ge(w.lo_done, 6 * i + 6 + n_w)
                for c, (t0, n) in enumerate(chunks):
                    pe.wait_ge(a_low, n_gu * i + n_c + c + 1 + 2)
                    for m in range(KD):
                        e = c * KD + m
                        pe.wait_ge(added, n_dn * i + e + 1)
                        for j in range(2):
                            for q, (a, x) in enumerate(
                                    w.passes(1 + j, m, a_hi[:, j, t0:t0 + n], a_lo[:, j, t0:t0 + n])):
                                last = nc.tensor.matmul(d_ps[:, e % 2, 0:n], a, x, start=(j == 0 and q == 0),
                                                        stop=(j == 1 and q == 2))
                        last.then_inc(d_done, 1)

        @block.scalar
        def _(act):
            with act.Fori(0, n_bodies) as i:
                last_use = ((u_done, n_gu * i + n_gu), (d_done, n_dn * i + n_dn), (d_done, n_dn * i + n_dn),
                            (g_done, n_gu * i + n_c), (u_done, n_gu * i + n_c + n_gu), (g_done, n_gu * i + n_gu))

                def split(t):
                    act.wait_ge(w.loaded[t % n_w], 32 * i + 16 * (t // n_w + 1))
                    act.wait_ge(*last_use[t])
                    w.high(t % n_w)

                def activate(j):
                    for c, (_, n) in enumerate(chunks):
                        act.wait_ge(prod_done, n_gu * i + n_c * j + c + 1)
                        act.wait_ge(g_done, n_gu * i + n_c * j + c + 1)
                        nc.scalar.activation(silu[:, c, 0:n], g_ps[:, c, 0:n], ACT.Silu).then_inc(silu_done, 1)

                def high(j):
                    for c, (t0, n) in enumerate(chunks):
                        act.wait_ge(prod_done, n_gu * i + n_c * j + c + 1 + n_c)
                        nc.scalar.copy(a_hi[:, j, t0:t0 + n], prod[:, (n_c * j + c) % 2, 0:n]).then_inc(a_high, 1)

                split(0)
                split(1)
                split(2)
                activate(0)
                split(3)
                high(0)
                split(4)
                activate(1)
                split(5)
                high(1)

        @block.vector
        def _(dve):
            dve.sem_inc(silu_done, n_c)
            dve.sem_inc(prod_done, n_c)
            dve.sem_inc(a_low, 2)
            dve.sem_inc(added, 2)
            with dve.Fori(0, n_bodies) as i:
                def multiply(e):
                    c = e % n_c
                    n = chunks[c][1]
                    dve.wait_ge(a_low, n_gu * i + e + 1)
                    dve.wait_ge(silu_done, n_gu * i + e + 1 + n_c)
                    dve.wait_ge(u_done, n_gu * i + e + 1 + n_gu)
                    nc.vector.tensor_tensor(prod[:, e % 2, 0:n], silu[:, c, 0:n], u_ps[:, c, 0:n], ALU.mult
                                            ).then_inc(prod_done, 1)

                def low(e):
                    j, c = divmod(e, n_c)
                    t0, n = chunks[c]
                    dve.wait_ge(a_high, n_gu * i + e + 1)
                    nc.vector.tensor_tensor(a_lo[:, j, t0:t0 + n], prod[:, e % 2, 0:n],
                                            a_hi[:, j, t0:t0 + n].bitcast(F32), ALU.subtract).then_inc(a_low, 1)

                for e in range(n_gu):
                    multiply(e)
                    low(e)
                for c, (t0, n) in enumerate(chunks):
                    for m in range(KD):
                        e = c * KD + m
                        dve.wait_ge(d_done, n_dn * i + e + 1 + n_dn)
                        nc.vector.scalar_tensor_tensor(dst[:, m, t0:t0 + n], d_ps[:, e % 2, 0:n],
                                                       gate(m, stream_of(chunks[c])), dst[:, m, t0:t0 + n],
                                                       ALU.mult, ALU.add).then_inc(added, 1)


def rotate_rows(nc, g, tag, src, turn, cos, sin, out_dram):
    n_c = len(ALL_CHUNKS)
    with ExitStack() as ctx:
        sb = lambda n, s, d=F32: ctx.enter_context(nc.sbuf_tensor(tag + n, s, d))
        sem = semaphores(nc, ctx, tag)
        with_cos, with_sin, whole = sb("with_cos", [P, TOK]), sb("with_sin", [P, TOK]), sb("whole", [P, TOK])
        hi, lo = sb("hi", [P, TOK], F32R), sb("lo", [P, TOK], F32R)
        turned_ps = ctx.enter_context(nc.psum_tensor(tag + "turned", [P, 3, BANK], F32))
        turned, cos_done, sin_done, whole_done, hi_done, lo_done, stored = (
            sem("turned"), sem("cos_done"), sem("sin_done"), sem("whole_done"), sem("hi_done"), sem("lo_done"),
            sem("stored"))
        block = ctx.enter_context(nc.Block(no_gpsimd_drain=True))

        @block.tensor
        def _(pe):
            for c, (t0, n) in enumerate(ALL_CHUNKS):
                nc.tensor.matmul(turned_ps[:, c, 0:n], turn[:, :], src[:, t0:t0 + n], start=True, stop=True
                                 ).then_inc(turned, 1)

        @block.gpsimd
        def _(pool):
            nc.gpsimd.tensor_tensor(with_cos[:, :], src, cos[:, :], ALU.mult).then_inc(cos_done, 1)

        @block.vector
        def _(dve):
            for c, (t0, n) in enumerate(ALL_CHUNKS):
                dve.wait_ge(turned, c + 1)
                nc.vector.tensor_tensor(with_sin[:, t0:t0 + n], turned_ps[:, c, 0:n], sin[:, t0:t0 + n],
                                        ALU.mult).then_inc(sin_done, 1)
            dve.wait_ge(sin_done, n_c)
            dve.wait_ge(cos_done, 1)
            nc.vector.tensor_tensor(whole[:, :], with_cos[:, :], with_sin[:, :], ALU.add).then_inc(whole_done, 1)
            dve.wait_ge(hi_done, 1)
            nc.vector.tensor_tensor(lo[:, :], whole[:, :], hi[:, :].bitcast(F32), ALU.subtract).then_inc(lo_done, 1)

        @block.scalar
        def _(act):
            act.wait_ge(whole_done, 1)
            nc.scalar.copy(hi[:, :], whole[:, :]).then_inc(hi_done, 1)

        @block.sync
        def _(sp):
            sp.wait_ge(lo_done, 1)
            for part, tile in ((0, hi), (1, lo)):
                sp.dma_start(out_dram[part], tile[0:ROPE, :].bitcast(F32)).then_inc(stored, 16)
            sp.wait_ge(stored, 32)


def fetch(nc, tag, pairs):
    with ExitStack() as ctx:
        loaded = semaphores(nc, ctx, tag)("loaded")
        block = ctx.enter_context(nc.Block(no_gpsimd_drain=True))

        @block.sync
        def _(sp):
            for dst, src in pairs:
                sp.dma_start(dst, src).then_inc(loaded, 16)
            sp.wait_ge(loaded, 16 * len(pairs))


class Globals:
    pass


def flat(ap):
    return ap.rearrange("a p n -> p (a n)")


def dit_kernel(nc, a, out):
    g = Globals()
    g.w_mod = [a["w_mod"][layer] for layer in range(2)]
    scratch = {}

    def dram(name, shape):
        scratch[name] = nc.dram_tensor(name, shape, F32, kind="Internal").ap()
        return scratch[name]

    with ExitStack() as ctx:
        sb = lambda n, s, d=F32: ctx.enter_context(nc.sbuf_tensor(n, s, d))
        x_t = sb("x_t", [P, KD, TOK])
        g.ident, g.ones, g.head_ones = sb("ident", [P, P]), sb("ones", [P, P]), sb("head_ones", [P, P])
        turn64, turn32 = sb("turn64", [P, P]), sb("turn32", [P, P])
        g.eps = sb("eps", [P, 1])
        g.mod_t = sb("mod_t", [P, MOD_COLS, 2])
        g.gain1, g.gain2 = sb("gain1", [P, KD, 2]), sb("gain2", [P, KD, 2])
        g.b_mod = sb("b_mod", [P, 2, MOD_COLS, 2])
        g.norms = sb("norms", [P, 2, 2, KD, 2])
        c_t = sb("c_t", [P, KD, 2])
        silu_c = sb("silu_c", [P, KD, 2])
        g.silu_parts = sb("silu_parts", [P, KD, 4], F32R)
        g.pair_sum = sb("pair_sum", [4, 2])
        final_gain, qa_gain, kva_gain = sb("final_gain", [P, KD]), sb("qa_gain", [P, 3]), sb("kva_gain", [P, 2])
        qk_gain_in, qk_gains = sb("qk_gain_in", [P, 2]), sb("qk_gains", [P, 10])

        fetch(nc, "in_", [
            (x_t[:, :, CTX:TOK], a["x_t"].rearrange("(k p) n -> p k n", p=P)),
            (x_t[:, :, 0:CTX], a["ctx_t"].rearrange("(k p) n -> p k n", p=P)),
            (g.ident[:, :], a["ident"]), (g.ones[:, :], a["ones"]), (g.head_ones[:, :], a["head_ones"]),
            (turn64[:, :], a["turn64"]), (turn32[:, :], a["turn32"]), (g.pair_sum[:, :], a["pair_sum"]),
            (g.b_mod[:, :, :, :], a["b_mod"]), (g.norms[:, :, :, :, :], a["norms"]), (c_t[:, :, :], a["c_t"]),
            (final_gain[:, :], a["final_gain"]), (qa_gain[:, :], a["qa_gain"]), (kva_gain[:, :], a["kva_gain"]),
            (qk_gain_in[:, :], a["qk_gain"]),
        ])
        setup_done, silu_done, silu_high = (
            nc.alloc_semaphore(n) for n in ("setup_done", "silu_done", "silu_high"))
        with nc.Block(no_gpsimd_drain=True) as block:
            @block.vector
            def _(dve):
                nc.vector.memset(g.eps[:, :], EPS).then_inc(setup_done, 1)
                nc.vector.tensor_scalar(qk_gains[:, 0:8], qk_gain_in[:, 0:1].to_broadcast([P, 8]),
                                        GQA_HD ** -0.5, None, ALU.mult).then_inc(setup_done, 1)
                nc.vector.tensor_copy(qk_gains[:, 8:10], qk_gain_in[:, 1:2].to_broadcast([P, 2])
                                      ).then_inc(setup_done, 1)
                dve.wait_ge(silu_high, 1)
                nc.vector.tensor_tensor(g.silu_parts[:, :, 2:4], silu_c[:, :, :],
                                        g.silu_parts[:, :, 0:2].bitcast(F32), ALU.subtract).then_inc(setup_done, 1)

            @block.scalar
            def _(act):
                nc.scalar.activation(silu_c[:, :, :], c_t[:, :, :], ACT.Silu).then_inc(silu_done, 1)
                act.wait_ge(silu_done, 1)
                nc.scalar.copy(g.silu_parts[:, :, 0:2], silu_c[:, :, :]).then_inc(silu_high, 1)

        def mod(split):
            return lambda k, s: flat_column(g.mod_t, split * KD + k, s)

        def flat_column(table, col, s):
            return table[:, bass.ds(col, 1), s:s + 1].rearrange("p a b -> p (a b)")

        def attention_output(layer):
            octx = ExitStack()
            return octx.enter_context(nc.sbuf_tensor(f"o{layer}", [P, KD, TOK], F32)), octx

        modulation(nc, g, 0)
        qk0 = dram("qk0", (2, 10, P, TOK))
        qk0_heads = qk0.rearrange("s t (h p) n -> s (t h) p n", p=GQA_HD)
        v0 = dram("v0", (GQA_KV, P, NKT * P))

        with ExitStack() as hctx:
            h_hi = hctx.enter_context(nc.sbuf_tensor("h0_hi", [P, KD, TOK], F32R))
            h_lo = hctx.enter_context(nc.sbuf_tensor("h0_lo", [P, KD, TOK], F32R))
            norm(nc, g, "n01_", x_t, KD, lambda k, s: g.gain1[:, k, s:s + 1], mod(0), h_hi, h_lo, ALL_CHUNKS)
            values(nc, g, "v0_", a["w_v0"], h_hi, h_lo, KD, 2, v0)
            with ExitStack() as rctx:
                cos = rctx.enter_context(nc.sbuf_tensor("cos64", [P, TOK], F32))
                sin = rctx.enter_context(nc.sbuf_tensor("sin64", [P, TOK], F32))
                fetch(nc, "rope64_", [(cos[:, :], a["cos64"]), (sin[:, :], a["sin64"])])
                project(nc, g, "qk0_", a["w_qk0"], h_hi, h_lo, KD, 10, ALL_CHUNKS, "norm_rope",
                        lambda part, t, t0, n: flat(qk0[part, bass.ds(t, 1), :, t0:t0 + n]),
                        gains=qk_gains, turn=turn64, cos=cos, sin=sin)

        def q0(i, h, t0):
            return [(flat(qk0_heads[part, bass.ds(2 * i + h, 1), :, t0:t0 + BANK]), 0, 64 * part, 64)
                    for part in range(2)]

        def k0(i, h):
            return [(flat(qk0_heads[part, bass.ds(HEADS + i // 2, 1), :, :]), part, 64 * half, 64)
                    for part in range(2) for half in range(2)]

        o_t, o_ctx = attention_output(0)
        attention(nc, g, "at0_", q0, k0, lambda i, h: flat(v0[bass.ds(i // 2, 1)]), P, ((0, 0), (0, 1)), o_t)
        context_attention(
            nc, g, "ca0_", lambda part, h, n: qk0_heads[part, h:h + n, :, 0:CTX].rearrange("h p n -> p h n"),
            lambda part, r: qk0_heads[part, HEADS + r, :, 0:CTX], lambda r: v0[r, :, 0:CTX], o_t)

        def out_and_mlp(layer, o_t, o_ctx, w_o, w_gu, w_down, chunks):
            with o_ctx:
                o_hi = o_ctx.enter_context(nc.sbuf_tensor(f"o{layer}_hi", [P, KD, TOK], F32R))
                o_lo = o_ctx.enter_context(nc.sbuf_tensor(f"o{layer}_lo", [P, KD, TOK], F32R))
                accumulate(nc, g, f"wo{layer}_", w_o, o_hi, o_lo, KD, KD, chunks, x_t, mod(2), whole=o_t)
            with ExitStack() as hctx:
                h_hi = hctx.enter_context(nc.sbuf_tensor(f"m{layer}_hi", [P, KD, TOK], F32R))
                h_lo = hctx.enter_context(nc.sbuf_tensor(f"m{layer}_lo", [P, KD, TOK], F32R))
                norm(nc, g, f"n{layer}2_", x_t, KD, lambda k, s: g.gain2[:, k, s:s + 1], mod(3), h_hi, h_lo, chunks)
                mlp(nc, g, f"mlp{layer}_", w_gu, w_down, h_hi, h_lo, chunks, x_t, mod(5))

        out_and_mlp(0, o_t, o_ctx, a["w_o0"], a["w_gu0"], a["w_down0"], ALL_CHUNKS)

        modulation(nc, g, 1)
        q_nope, q_rope = dram("q_nope", (2, 8, P, TOK)), dram("q_rope", (2, 4, P, TOK))
        k_nope, k_rope, v1 = dram("k_nope", (2, 8, P, TOK)), dram("k_rope", (2, ROPE, TOK)), dram(
            "v1", (HEADS, P, NKT * P))
        q_nope_heads = q_nope.rearrange("s t (h p) n -> s (t h) p n", p=NOPE)
        q_rope_heads = q_rope.rearrange("s t (h p) n -> s (t h) p n", p=ROPE)
        k_nope_heads = k_nope.rearrange("s t (h p) n -> s (t h) p n", p=NOPE)
        mla_scale = float(np.float32(QK_MLA ** -0.5))

        with ExitStack() as lctx:
            low_rank = lctx.enter_context(nc.sbuf_tensor("low_rank", [P, W_IN_TILES, TOK], F32))
            with ExitStack() as hctx:
                h_hi = hctx.enter_context(nc.sbuf_tensor("h1_hi", [P, KD, TOK], F32R))
                h_lo = hctx.enter_context(nc.sbuf_tensor("h1_lo", [P, KD, TOK], F32R))
                norm(nc, g, "n11_", x_t, KD, lambda k, s: g.gain1[:, k, s:s + 1], mod(0), h_hi, h_lo, ALL_CHUNKS)
                accumulate(nc, g, "win_", a["w_in"], h_hi, h_lo, KD, W_IN_TILES, ALL_CHUNKS, low_rank)
            q_hi = lctx.enter_context(nc.sbuf_tensor("q_hi", [P, 3, TOK], F32R))
            q_lo = lctx.enter_context(nc.sbuf_tensor("q_lo", [P, 3, TOK], F32R))
            kv_hi = lctx.enter_context(nc.sbuf_tensor("kv_hi", [P, 2, TOK], F32R))
            kv_lo = lctx.enter_context(nc.sbuf_tensor("kv_lo", [P, 2, TOK], F32R))
            cos = lctx.enter_context(nc.sbuf_tensor("cos32", [P, TOK], F32))
            sin = lctx.enter_context(nc.sbuf_tensor("sin32", [P, TOK], F32))
            fetch(nc, "rope32_", [(cos[:, :], a["cos32"]), (sin[:, :], a["sin32"])])
            norm(nc, g, "nqa_", low_rank[:, 0:3], 3, lambda k, s: qa_gain[:, k:k + 1], None, q_hi, q_lo, LAT_CHUNKS)
            norm(nc, g, "nkv_", low_rank[:, 3:5], 2, lambda k, s: kva_gain[:, k:k + 1], None, kv_hi, kv_lo, ALL_CHUNKS)
            rotate_rows(nc, g, "kr_", low_rank[:, 5, :], turn32, cos, sin, k_rope)
            project(nc, g, "qn_", a["w_q_nope"], q_hi, q_lo, 3, 8, LAT_CHUNKS, "plain",
                    lambda part, t, t0, n: flat(q_nope[part, bass.ds(t, 1), :, t0:t0 + n]), scale=mla_scale)
            project(nc, g, "qr_", a["w_q_rope"], q_hi, q_lo, 3, 4, LAT_CHUNKS, "rope",
                    lambda part, t, t0, n: flat(q_rope[part, bass.ds(t, 1), :, t0:t0 + n]), scale=mla_scale,
                    turn=turn32, cos=cos, sin=sin)
            project(nc, g, "kn_", a["w_k_nope"], kv_hi, kv_lo, 2, 8, ALL_CHUNKS, "plain",
                    lambda part, t, t0, n: flat(k_nope[part, bass.ds(t, 1), :, t0:t0 + n]))
            values(nc, g, "v1_", a["w_v1"], kv_hi, kv_lo, 2, 8, v1)

        def q1(i, h, t0):
            return ([(flat(q_nope_heads[part, bass.ds(2 * i + h, 1), :, t0:t0 + BANK]), part, 0, NOPE)
                     for part in range(2)]
                    + [(flat(q_rope_heads[part, bass.ds(2 * i + h, 1), :, t0:t0 + BANK]), part, NOPE, ROPE)
                       for part in range(2)])

        def k1(i, h):
            return ([(flat(k_nope_heads[part, bass.ds(2 * i + h, 1), :, :]), part, 0, NOPE) for part in range(2)]
                    + [(k_rope[part], part, NOPE, ROPE) for part in range(2)])

        o_t, o_ctx = attention_output(1)
        attention(nc, g, "at1_", q1, k1, lambda i, h: flat(v1[bass.ds(2 * i + h, 1)]), QK_MLA,
                  ((0, 0), (1, 0), (0, 1)), o_t)
        out_and_mlp(1, o_t, o_ctx, a["w_o1"], a["w_gu1"], a["w_down1"], LAT_CHUNKS)

        norm(nc, g, "fin_", x_t, KD, lambda k, s: final_gain[:, k:k + 1], None, None, None, LAT_CHUNKS, out_dram=out)




def tiles(w):
    k, n = w.shape
    return np.ascontiguousarray(w.reshape(k // P, P, n // P, P).transpose(2, 1, 0, 3).reshape(n // P, P, k))


def per_feature(v):
    return np.ascontiguousarray(v.reshape(-1, P).T)


def rope_tables(rot_dim):
    n = rot_dim // 4
    inv = np.power(np.float32(10000.0), -np.arange(n, dtype=np.float32) / np.float32(n))
    rows = SEQ // GRID_W
    row = np.repeat(np.arange(rows, dtype=np.float32), GRID_W)
    col = np.tile(np.arange(GRID_W, dtype=np.float32), rows)
    ang = np.concatenate([row[:, None] * inv, col[:, None] * inv], axis=-1).astype(np.float64)
    cos = np.ones((rot_dim // 2, TOK), np.float32)
    sin = np.zeros((rot_dim // 2, TOK), np.float32)
    cos[:, CTX:], sin[:, CTX:] = np.cos(ang).T, np.sin(ang).T
    return np.tile(cos, (2 * P // rot_dim, 1)), np.tile(sin, (2 * P // rot_dim, 1))


def turn_matrix(rot_dim):
    half = rot_dim // 2
    m = np.zeros((P, P), np.float32)
    for g0 in range(0, P, rot_dim):
        for j in range(half):
            m[g0 + half + j, g0 + j] = -1.0
            m[g0 + j, g0 + half + j] = 1.0
    return m


def kernel(**inputs):
    import concourse.bacc as bacc
    from concourse.bass_utils import run_bass_kernel_spmd

    v = {name: np.asarray(x) for name, x in inputs.items()}
    arrays = {
        "x_t": v["x"][0].T,
        "ctx_t": v["ctx"][0].T,
        "c_t": np.stack([v["c"][0], v["c_ctx"]], axis=-1).reshape(KD, P, 2).transpose(1, 0, 2),
        "w_mod": v["w_mod"].reshape(2, KD, P, 12, BANK).transpose(0, 3, 2, 1, 4).reshape(2, 12, P, KD * BANK),
        "b_mod": np.repeat(v["b_mod"].reshape(2, MOD_COLS, P).transpose(2, 0, 1)[..., None], 2, axis=-1),
        "norms": np.repeat(np.stack([v["norm1"], v["norm2"]], axis=1).reshape(2, 2, KD, P).transpose(3, 0, 1, 2)
                           [..., None], 2, axis=-1),
        "final_gain": per_feature(v["final_norm"]),
        "qa_gain": per_feature(v["mla_q_a_norm"][0]),
        "kva_gain": per_feature(v["mla_kv_a_norm"][0]),
        "qk_gain": np.stack([np.tile(v["gqa_q_norm"][0], 2), np.tile(v["gqa_k_norm"][0], 2)], axis=-1),
    }
    qkv = v["gqa_w_qkv"][0]
    n_qk = (HEADS + GQA_KV) * GQA_HD
    arrays["w_qk0"] = tiles(qkv[:, :n_qk])
    arrays["w_v0"] = tiles(qkv[:, n_qk:])
    w_in = v["mla_w_in"][0]
    padded = np.zeros((D, W_IN_TILES * P), w_in.dtype)
    padded[:, :w_in.shape[1]] = w_in
    arrays["w_in"] = tiles(padded)
    q_b = v["mla_q_b"][0].reshape(Q_RANK, HEADS, QK_MLA)
    arrays["w_q_nope"] = tiles(q_b[:, :, :NOPE].reshape(Q_RANK, HEADS * NOPE))
    arrays["w_q_rope"] = tiles(q_b[:, :, NOPE:].reshape(Q_RANK, HEADS * ROPE))
    kv_b = v["mla_kv_b"][0].reshape(KV_RANK, HEADS, NOPE + V_DIM)
    arrays["w_k_nope"] = tiles(kv_b[:, :, :NOPE].reshape(KV_RANK, HEADS * NOPE))
    arrays["w_v1"] = tiles(kv_b[:, :, NOPE:].reshape(KV_RANK, HEADS * V_DIM))
    for layer, w_o in enumerate((v["gqa_w_o"][0], v["mla_w_o"][0])):
        arrays[f"w_o{layer}"] = tiles(w_o)
        gu = v["w_gate_up"][layer]
        arrays[f"w_gu{layer}"] = np.stack([tiles(gu[:, :DFF]), tiles(gu[:, DFF:])], axis=1).reshape(2 * NFF, P, D)
        arrays[f"w_down{layer}"] = v["w_down"][layer].reshape(NFF, P, D)
    arrays["ident"] = np.eye(P, dtype=np.float32)
    arrays["pair_sum"] = np.tile(np.eye(2, dtype=np.float32), (2, 1))
    arrays["ones"] = np.ones((P, P), np.float32)
    arrays["head_ones"] = np.kron(np.eye(2, dtype=np.float32), np.ones((64, 64), np.float32))
    arrays["turn64"], arrays["turn32"] = turn_matrix(64), turn_matrix(32)
    arrays["cos64"], arrays["sin64"] = rope_tables(64)
    arrays["cos32"], arrays["sin32"] = rope_tables(32)
    arrays = {name: np.ascontiguousarray(x) for name, x in arrays.items()}

    nc = bacc.Bacc("TRN2", target_bir_lowering=False, num_devices=1)
    aps = {name: nc.dram_tensor(f"in_{name}", x.shape, mybir.dt.from_np(x.dtype), kind="ExternalInput").ap()
           for name, x in arrays.items()}
    out = nc.dram_tensor("out_t", (D, SEQ), F32, kind="ExternalOutput").ap()
    dit_kernel(nc, aps, out)
    r = run_bass_kernel_spmd(nc, [{f"in_{name}": x for name, x in arrays.items()}], core_ids=[0])
    return np.ascontiguousarray(r.results[0]["out_t"].T)[None]
```

```python
from contextlib import ExitStack

import concourse.bass as bass
import numpy as np
from concourse import mybir

F32 = mybir.dt.float32
F32R = mybir.dt.float32r
ALU = mybir.AluOpType
ACT = mybir.ActivationFunctionType
AX_X = mybir.AxisListType.X

P = 128
D = 1024
KD = D // P
CTX = 256
SEQ = 1024
TOK = CTX + SEQ
NKT = TOK // P
DFF = 2816
NFF = DFF // P
HEADS = 16
GQA_HD = 64
GQA_KV = 4
NOPE = 64
ROPE = 32
QK_MLA = NOPE + ROPE
V_DIM = 64
Q_RANK = 384
KV_RANK = 256
W_IN_TILES = 6
GRID_W = 64
EPS = 1e-6
BANK = 512
MOD_COLS = 6 * KD

LAT_CHUNKS = ((256, 512), (768, 512))
ALL_CHUNKS = LAT_CHUNKS + ((0, 256),)


def stream_of(chunk):
    return 0 if chunk[0] >= CTX else 1


def semaphores(nc, ctx, tag):
    taken = []

    def sem(name):
        taken.append(nc.alloc_semaphore(tag + name))
        return taken[-1]

    def give_back():
        nc.clear_and_free_semaphores(taken)
        nc.all_engine_barrier(sem_only=True)

    ctx.callback(give_back)
    return sem


def modulation(nc, g, layer):
    n_chunks = 12
    n_raw = 4
    n_bodies = n_chunks // n_raw
    with ExitStack() as ctx:
        tag = f"mod{layer}_"
        sb = lambda n, s, d=F32: ctx.enter_context(nc.sbuf_tensor(tag + n, s, d))
        ps = lambda n, s, d=F32: ctx.enter_context(nc.psum_tensor(tag + n, s, d))
        sem = semaphores(nc, ctx, tag)
        w_raw = sb("w_raw", [P, n_raw, KD * BANK])
        w_hi = sb("w_hi", [P, 2, KD * BANK], F32R)
        w_lo = sb("w_lo", [P, 2, KD * BANK], F32R)
        rows = sb("rows", [4, 2, BANK])
        row_ps = ps("row_ps", [4, 2, BANK])
        col_ps = ps("col_ps", [P, 2, BANK])
        w_loaded = [sem(f"w_loaded{j}") for j in range(n_raw)]
        w_high, w_low, rows_done, row_copied, turned, mod_added = (
            sem("w_high"), sem("w_low"), sem("rows_done"), sem("row_copied"), sem("turned"), sem("mod_added"))
        affine = sem("affine")
        block = ctx.enter_context(nc.Block(no_gpsimd_drain=True))

        @block.sync
        def _(sp):
            with sp.Fori(0, n_bodies) as i:
                for u in range(n_raw):
                    sp.wait_ge(w_low, n_raw * i + u + 1)
                    sp.dma_start(w_raw[:, u, :], flat(g.w_mod[layer][bass.ds(n_raw * i + u, 1)])
                                 ).then_inc(w_loaded[u], 16)

        @block.scalar
        def _(act):
            with act.Fori(0, n_bodies) as i:
                for u in range(n_raw):
                    act.wait_ge(rows_done, n_raw * i + u + 1)
                    act.wait_ge(w_loaded[u], 16 * i + 16)
                    nc.scalar.copy(w_hi[:, u % 2, :], w_raw[:, u, :]).then_inc(w_high, 1)

        @block.tensor
        def _(pe):
            def products(i, u):
                pe.wait_ge(row_copied, n_raw * i + u + 1)
                pe.wait_ge(w_low, n_raw * i + u + 1 + n_raw)
                for k in range(KD):
                    for j, w in enumerate((w_hi, w_lo)):
                        last = nc.tensor.matmul(row_ps[:, u % 2, :], g.silu_parts[:, k, :],
                                                w[:, u % 2, k * BANK:(k + 1) * BANK],
                                                start=(k == 0 and j == 0), stop=(k == KD - 1 and j == 1))
                last.then_inc(rows_done, 1)

            def turn(i, u):
                pe.wait_ge(row_copied, n_raw * i + u + 3)
                pe.wait_ge(mod_added, n_raw * i + u + 1)
                for j in range(4):
                    last = nc.tensor.matmul(col_ps[:, u % 2, 2 * j:2 * j + 2], rows[:, u % 2, j * P:(j + 1) * P],
                                            g.pair_sum[:, :], start=True, stop=True)
                last.then_inc(turned, 1)

            def body(i, more):
                for u in range(n_raw):
                    if u + 1 < n_raw:
                        products(i, u + 1)
                    elif more:
                        products(i + 1, 0)
                    turn(i, u)

            pe.sem_inc(rows_done, 2)
            products(0, 0)
            with pe.Fori(0, n_bodies - 1) as i:
                body(i, True)
            body(n_bodies - 1, False)

        @block.vector
        def _(dve):
            dve.sem_inc(w_low, n_raw)
            dve.sem_inc(row_copied, 2)
            dve.sem_inc(mod_added, 2)

            def low(i, u):
                dve.wait_ge(w_high, n_raw * i + u + 1)
                nc.vector.tensor_tensor(w_lo[:, u % 2, :], w_raw[:, u % n_raw, :], w_hi[:, u % 2, :].bitcast(F32),
                                        ALU.subtract).then_inc(w_low, 1)

            def copy_rows(i, u):
                dve.wait_ge(rows_done, n_raw * i + u + 3)
                nc.vector.tensor_copy(rows[:, u % 2, :], row_ps[:, u % 2, :]).then_inc(row_copied, 1)

            def add(i, u):
                dve.wait_ge(turned, n_raw * i + u + 1)
                nc.vector.tensor_tensor(
                    g.mod_t[:, bass.ds(4 * n_raw * i + 4 * u, 4), :],
                    col_ps[:, u % 2, 0:8].rearrange("p (j s) -> p j s", s=2),
                    g.b_mod[:, layer, bass.ds(4 * n_raw * i + 4 * u, 4), :], ALU.add,
                ).then_inc(mod_added, 1)

            def body(i, more):
                for u in range(n_raw):
                    if u + 2 < n_raw or more:
                        low(i, u + 2)
                    if u + 1 < n_raw or more:
                        copy_rows(i, u + 1)
                    add(i, u)

            low(0, 0)
            low(0, 1)
            copy_rows(0, 0)
            with dve.Fori(0, n_bodies - 1) as i:
                body(i, True)
            body(n_bodies - 1, False)
            dve.wait_ge(mod_added, 2 + n_chunks)
            for j, gain in ((0, g.gain1), (1, g.gain2)):
                scale = g.mod_t[:, (3 * j + 1) * KD:(3 * j + 2) * KD, :]
                nc.vector.tensor_scalar(gain[:, :, :], scale, 1.0, None, ALU.add).then_inc(affine, 1)
            dve.wait_ge(affine, 2)
            for j, gain in ((0, g.gain1), (1, g.gain2)):
                nc.vector.tensor_tensor(gain[:, :, :], gain[:, :, :], g.norms[:, layer, j, :, :],
                                        ALU.mult).then_inc(affine, 1)


class Norm:

    def __init__(self, nc, g, ctx, sem, tag, src, n_k, gain, shift, out_hi, out_lo, chunks, ssq, out_dram=None):
        sb = lambda n, s, d=F32: ctx.enter_context(nc.sbuf_tensor(tag + n, s, d))
        self.nc, self.g, self.src, self.n_k, self.gain, self.shift = nc, g, src, n_k, gain, shift
        self.out_hi, self.out_lo, self.chunks, self.ssq, self.out_dram = out_hi, out_lo, chunks, ssq, out_dram
        self.n_t = 4
        self.squares = sb("squares", [P, 2, BANK])
        self.root = sb("root", [P, 2, BANK])
        self.scaled = sb("scaled", [P, self.n_t, BANK])
        self.sq_ready, self.ssq_added, self.root_ready, self.rinv_ready = (
            sem("norm_sq_ready"), sem("norm_ssq_added"), sem("norm_root_ready"), sem("norm_rinv_ready"))
        self.t_ready, self.hi_ready, self.lo_ready = sem("norm_t_ready"), sem("norm_hi_ready"), sem("norm_lo_ready")
        if out_dram is not None:
            self.stored = [sem(f"norm_stored{j}") for j in range(self.n_t)]

    def wait_ready(self, engine, t0):
        ci = [c[0] for c in self.chunks].index(t0)
        engine.wait_ge(self.lo_ready, (ci + 1) * self.n_k)

    def scalar(self, act):
        nc, n_k, chunks = self.nc, self.n_k, self.chunks

        def square_chunk(ci):
            t0, n = chunks[ci]
            for k in range(n_k):
                s = ci * n_k + k
                if s >= 2:
                    act.wait_ge(self.ssq_added, s - 1)
                nc.scalar.activation(self.squares[:, s % 2, 0:n], self.src[:, k, t0:t0 + n],
                                     ACT.Square).then_inc(self.sq_ready, 1)

        def root_chunk(ci):
            n = chunks[ci][1]
            act.wait_ge(self.ssq_added, (ci + 1) * n_k)
            if ci >= 2:
                act.wait_ge(self.t_ready, (ci - 1) * n_k)
            nc.scalar.activation(self.root[:, ci % 2, 0:n], self.ssq[:, ci % 2, 0:n], ACT.Sqrt,
                                 bias=self.g.eps[:, 0:1], scale=1.0 / (n_k * P)).then_inc(self.root_ready, 1)

        def hi_chunk(ci):
            if self.out_dram is not None:
                return
            t0, n = chunks[ci]
            for k in range(n_k):
                s = ci * n_k + k
                act.wait_ge(self.t_ready, s + 1)
                bias = self.shift(k, stream_of(chunks[ci])) if self.shift else 0.0
                nc.scalar.activation(self.out_hi[:, k, t0:t0 + n], self.scaled[:, s % self.n_t, 0:n], ACT.Identity,
                                     bias=bias).then_inc(self.hi_ready, 1)

        for ci in range(len(chunks)):
            square_chunk(ci)
            if ci:
                hi_chunk(ci - 1)
            root_chunk(ci)
        hi_chunk(len(chunks) - 1)

    def tensor(self, pe):
        nc, n_k = self.nc, self.n_k
        for ci, (_, n) in enumerate(self.chunks):
            if ci >= 2:
                pe.wait_ge(self.root_ready, ci - 1)
            for k in range(n_k):
                pe.wait_ge(self.sq_ready, ci * n_k + k + 1)
                nc.tensor.matmul(self.ssq[:, ci % 2, 0:n], self.g.ones[:, :],
                                 self.squares[:, (ci * n_k + k) % 2, 0:n],
                                 start=(k == 0), stop=(k == n_k - 1)).then_inc(self.ssq_added, 1)

    def vector(self, dve):
        nc, n_k, n_t, chunks = self.nc, self.n_k, self.n_t, self.chunks

        def lo_of(s):
            ci, k = divmod(s, n_k)
            t0, n = chunks[ci]
            dve.wait_ge(self.hi_ready, s + 1)
            hi = self.out_hi[:, k, t0:t0 + n].bitcast(F32)
            lo = self.out_lo[:, k, t0:t0 + n]
            t = self.scaled[:, s % n_t, 0:n]
            if self.shift:
                nc.vector.scalar_tensor_tensor(lo, t, self.shift(k, stream_of(chunks[ci])), hi,
                                               ALU.add, ALU.subtract).then_inc(self.lo_ready, 1)
            else:
                nc.vector.tensor_tensor(lo, t, hi, ALU.subtract).then_inc(self.lo_ready, 1)

        for ci, (t0, n) in enumerate(chunks):
            dve.wait_ge(self.root_ready, ci + 1)
            nc.vector.reciprocal(self.root[:, ci % 2, 0:n], self.root[:, ci % 2, 0:n]).then_inc(self.rinv_ready, 1)
            dve.wait_ge(self.rinv_ready, ci + 1)
            for k in range(n_k):
                s = ci * n_k + k
                if self.out_dram is not None and s >= n_t:
                    dve.wait_ge(self.stored[s % n_t], 16 * (s // n_t))
                if self.out_dram is None and s >= n_t:
                    dve.wait_ge(self.lo_ready, s - n_t + 1)
                nc.vector.scalar_tensor_tensor(
                    self.scaled[:, s % n_t, 0:n], self.src[:, k, t0:t0 + n], self.gain(k, stream_of(chunks[ci])),
                    self.root[:, ci % 2, 0:n], ALU.mult, ALU.mult).then_inc(self.t_ready, 1)
                if self.out_dram is None and s >= 2:
                    lo_of(s - 2)
        if self.out_dram is None:
            for s in range(max(0, len(chunks) * n_k - 2), len(chunks) * n_k):
                lo_of(s)

    def sync(self, sp):
        n_k, n_t, chunks = self.n_k, self.n_t, self.chunks
        for s in range(len(chunks) * n_k):
            ci, k = divmod(s, n_k)
            t0, n = chunks[ci]
            sp.wait_ge(self.t_ready, s + 1)
            sp.dma_start(self.out_dram[k * P:(k + 1) * P, t0 - CTX:t0 - CTX + n],
                         self.scaled[:, s % n_t, 0:n]).then_inc(self.stored[s % n_t], 16)
        for j in range(n_t):
            sp.wait_ge(self.stored[j], 16 * len(range(j, len(chunks) * n_k, n_t)))


def final_norm(nc, g, tag, src, n_k, gain, chunks, out_dram):
    with ExitStack() as ctx:
        sem = semaphores(nc, ctx, tag)
        ssq = ctx.enter_context(nc.psum_tensor(tag + "ssq", [P, 2, BANK], F32))
        norm = Norm(nc, g, ctx, sem, tag, src, n_k, gain, None, None, None, chunks, ssq, out_dram)
        block = ctx.enter_context(nc.Block(no_gpsimd_drain=True))

        @block.scalar
        def _(act):
            norm.scalar(act)

        @block.tensor
        def _(pe):
            norm.tensor(pe)

        @block.vector
        def _(dve):
            norm.vector(dve)

        @block.sync
        def _(sp):
            norm.sync(sp)


class Split:

    def __init__(self, nc, ctx, tag, n_k, sem, slots=2):
        self.nc, self.n_k, self.slots = nc, n_k, slots
        width = n_k * P
        self.raw = ctx.enter_context(nc.sbuf_tensor(tag + "w_raw", [P, slots, width], F32))
        self.hi = ctx.enter_context(nc.sbuf_tensor(tag + "w_hi", [P, slots, width], F32R))
        self.lo = ctx.enter_context(nc.sbuf_tensor(tag + "w_lo", [P, slots, width], F32R))
        self.loaded = [sem(f"w_loaded{j}") for j in range(slots)]
        self.hi_done = sem("w_hi_done")
        self.lo_done = sem("w_lo_done")

    def passes(self, slot, k, x_hi, x_lo):
        w_hi, w_lo = (x[:, slot, k * P:(k + 1) * P] for x in (self.hi, self.lo))
        return ((w_hi, x_hi), (w_hi, x_lo), (w_lo, x_hi))

    def high(self, slot):
        return self.nc.scalar.copy(self.hi[:, slot, :], self.raw[:, slot, :]).then_inc(self.hi_done, 1)

    def low(self, slot):
        return self.nc.gpsimd.tensor_tensor(self.lo[:, slot, :], self.raw[:, slot, :],
                                            self.hi[:, slot, :].bitcast(F32), ALU.subtract
                                            ).then_inc(self.lo_done, 1)


def project(nc, g, tag, w_dram, src_hi, src_lo, n_k, n_tiles, chunks, mode, dst, scale=1.0, gains=None,
            turn=None, cos=None, sin=None, make_norm=None):
    n_c = len(chunks)
    per = 2 * n_c
    n_bodies = n_tiles // 2
    assert n_tiles % 2 == 0
    rotated = mode != "plain"
    normed = mode == "norm_rope"
    with ExitStack() as ctx:
        sb = lambda n, s, d=F32: ctx.enter_context(nc.sbuf_tensor(tag + n, s, d))
        ps = lambda n, s, d=F32: ctx.enter_context(nc.psum_tensor(tag + n, s, d))
        sem = semaphores(nc, ctx, tag)
        w = Split(nc, ctx, tag, n_k, sem)
        n_out = 2 if rotated else per
        hi_out = sb("hi_out", [P, n_out, BANK], F32R)
        lo_out = sb("lo_out", [P, n_out, BANK], F32R)
        acc = ps("acc", [P, 2, 3, BANK])
        acc_done = sem("acc_done")
        hi_done, lo_done = sem("hi_done"), sem("lo_done")
        lo_start = 0 if rotated else per
        stored = [sem(f"stored{j}") for j in range(n_out)]
        if rotated:
            aux = ps("aux", [P, 2, BANK])
            base = sb("base", [P, 2, BANK])
            with_cos = sb("with_cos", [P, 2, BANK])
            with_sin = sb("with_sin", [P, 2, BANK])
            whole = sb("whole", [P, 2, BANK])
            base_done, cos_done, turn_done, sin_done, whole_done = (
                sem("base_done"), sem("cos_done"), sem("turn_done"), sem("sin_done"), sem("whole_done"))
        if normed:
            squares = sb("squares", [P, 2, BANK])
            root = sb("root", [P, 2, BANK])
            rinv = sb("rinv", [P, 2, BANK])
            sq_done, ssq_done, root_done, rinv_done = (
                sem("sq_done"), sem("ssq_done"), sem("root_done"), sem("rinv_done"))
        acc_free = base_done if rotated else lo_done
        if make_norm:
            ssq = ps("ssq", [P, 2, BANK])
        norm = make_norm(ctx, sem, ssq) if make_norm else None
        block = ctx.enter_context(nc.Block(no_gpsimd_drain=True))

        def run(engine, stages, before=None):
            top = max(lag for _, lag in stages)

            def body(i, first=False, last=False):
                for b in range(per):
                    if before:
                        before(i, b, first, last)
                    for stage, lag in stages:
                        if b >= lag:
                            stage(i, b - lag)
                        elif not first:
                            stage(i - 1, b - lag + per)

            body(0, first=True)
            if n_bodies > 2:
                with engine.Fori(1, n_bodies - 1) as i:
                    body(i)
            body(n_bodies - 1, last=True)
            for b in range(per, per + top):
                for stage, lag in stages:
                    if b - lag < per:
                        stage(n_bodies - 1, b - lag)

        @block.sync
        def _(sp):
            for buffer_stored in stored:
                sp.sem_inc(buffer_stored, 16)

            def load(i):
                for u in range(2):
                    sp.wait_ge(w.lo_done, 2 * i + u + 1)
                    sp.dma_start(w.raw[:, u, :], w_dram[bass.ds(2 * i + u, 1)].rearrange("a p n -> p (a n)")
                                 ).then_inc(w.loaded[u], 16)

            def store(i):
                for b in range(per):
                    u, c = divmod(b, n_c)
                    t0, n = chunks[c]
                    sp.wait_ge(lo_done, per * i + b + 1 + lo_start)
                    for part, tile in ((1, lo_out), (0, hi_out)):
                        sp.dma_start(dst(part, 2 * i + u, t0, n), tile[:, b % n_out, 0:n].bitcast(F32)
                                     ).then_inc(stored[b % n_out], 16)

            load(0)
            if n_bodies > 1:
                with sp.Fori(0, n_bodies - 1) as i:
                    load(i + 1)
                    store(i)
            store(n_bodies - 1)
            for buffer_stored in stored:
                sp.wait_ge(buffer_stored, 16 + 32 * (per // n_out) * n_bodies)

        @block.tensor
        def _(pe):
            pe.sem_inc(acc_done, per)

            def main(i, b):
                u, c = divmod(b, n_c)
                t0, n = chunks[c]
                if c == 0:
                    pe.wait_ge(w.lo_done, 2 * i + u + 3)
                pe.wait_ge(acc_free, per * i + b + 1)
                if norm:
                    norm.wait_ready(pe, t0)
                for k in range(n_k):
                    for j, (a, x) in enumerate(w.passes(u, k, src_hi[:, k, t0:t0 + n], src_lo[:, k, t0:t0 + n])):
                        last = nc.tensor.matmul(acc[:, u, c, 0:n], a, x, start=(k == 0 and j == 0),
                                                stop=(k == n_k - 1 and j == 2))
                last.then_inc(acc_done, 1)

            def head_sums(i, b):
                n = chunks[b % n_c][1]
                pe.wait_ge(sq_done, per * i + b + 1)
                pe.wait_ge(root_done, per * i + b + 1)
                nc.tensor.matmul(aux[:, 0, 0:n], g.head_ones[:, :], squares[:, b % 2, 0:n], start=True,
                                 stop=True).then_inc(ssq_done, 1)

            def turned(i, b):
                n = chunks[b % n_c][1]
                pe.wait_ge(base_done, per * i + b + 1 + per)
                pe.wait_ge(sin_done, per * i + b + 1)
                nc.tensor.matmul(aux[:, 1, 0:n], turn[:, :], base[:, b % 2, 0:n], start=True,
                                 stop=True).then_inc(turn_done, 1)

            if norm:
                norm.tensor(pe)
            run(pe, [(main, 0)] + [(head_sums, 1)] * normed + [(turned, 2)] * rotated)

        @block.scalar
        def _(act):
            if normed:
                act.sem_inc(root_done, 1)

            def split(i, u):
                act.wait_ge(w.loaded[u], 16 * i + 16)
                act.wait_ge(acc_done, per * i + n_c * (u + 1))
                w.high(u)

            def square(i, b):
                u, c = divmod(b, n_c)
                n = chunks[c][1]
                act.wait_ge(acc_done, per * i + b + 1 + per)
                nc.scalar.activation(squares[:, b % 2, 0:n], acc[:, u, c, 0:n], ACT.Square).then_inc(sq_done, 1)

            def take_root(i, b):
                n = chunks[b % n_c][1]
                act.wait_ge(ssq_done, per * i + b + 1)
                nc.scalar.activation(root[:, b % 2, 0:n], aux[:, 0, 0:n], ACT.Sqrt, bias=g.eps[:, 0:1],
                                     scale=1.0 / GQA_HD).then_inc(root_done, 1)

            def high(i, b):
                u, c = divmod(b, n_c)
                n = chunks[c][1]
                act.wait_ge(stored[b % n_out], 32 * ((per // n_out) * i + b // n_out) + 16)
                if rotated:
                    act.wait_ge(whole_done, per * i + b + 1)
                    nc.scalar.copy(hi_out[:, b % n_out, 0:n], whole[:, b % 2, 0:n]).then_inc(hi_done, 1)
                else:
                    act.wait_ge(acc_done, per * i + b + 1 + per)
                    nc.scalar.mul(hi_out[:, b % n_out, 0:n], acc[:, u, c, 0:n], scale).then_inc(hi_done, 1)

            split(0, 0)
            split(0, 1)
            def before(i, b, first, last):
                if b == 0 and not first:
                    split(i, 1)
                if b == n_c and not last:
                    split(i + 1, 0)

            if norm:
                norm.scalar(act)
            run(act, [(square, 0), (take_root, 1)] * normed + [(high, 2 if rotated else 0)], before)

        @block.gpsimd
        def _(pool):
            pool.sem_inc(w.lo_done, 2)

            def split(i, u):
                pool.wait_ge(w.hi_done, 2 * i + u + 1)
                w.low(u)

            def cosine(i, b):
                t0, n = chunks[b % n_c]
                pool.wait_ge(base_done, per * i + b + 1 + per)
                nc.gpsimd.tensor_tensor(with_cos[:, b % 2, 0:n], base[:, b % 2, 0:n], cos[:, t0:t0 + n],
                                        ALU.mult).then_inc(cos_done, 1)

            def add(i, b):
                n = chunks[b % n_c][1]
                pool.wait_ge(cos_done, per * i + b + 1)
                pool.wait_ge(sin_done, per * i + b + 2)
                nc.gpsimd.tensor_tensor(whole[:, b % 2, 0:n], with_cos[:, b % 2, 0:n],
                                        with_sin[:, b % 2, 0:n], ALU.add).then_inc(whole_done, 1)

            def low(i, b):
                n = chunks[b % n_c][1]
                pool.wait_ge(hi_done, per * i + b + 1)
                nc.gpsimd.tensor_tensor(lo_out[:, b % n_out, 0:n], whole[:, b % 2, 0:n],
                                        hi_out[:, b % n_out, 0:n].bitcast(F32), ALU.subtract).then_inc(lo_done, 1)
                pool.wait_ge(lo_done, per * i + b + 1)

            split(0, 0)
            split(0, 1)
            def before(i, b, first, last):
                if b in (n_c - 1, per - 1) and not last:
                    split(i + 1, b // n_c)

            run(pool, [(cosine, 0), (low, 1), (add, 0)] * rotated or [(lambda i, b: None, 0)], before)

        @block.vector
        def _(dve):
            dve.sem_inc(acc_free, per)
            if rotated:
                dve.sem_inc(sin_done, 1)

            def make_base(i, b):
                u, c = divmod(b, n_c)
                n = chunks[c][1]
                if normed:
                    dve.wait_ge(root_done, per * i + b + 2)
                    nc.vector.reciprocal(rinv[:, b % 2, 0:n], root[:, b % 2, 0:n]).then_inc(rinv_done, 1)
                    dve.wait_ge(rinv_done, per * i + b + 1)
                    nc.vector.scalar_tensor_tensor(base[:, b % 2, 0:n], acc[:, u, c, 0:n],
                                                   gains[:, bass.ds(2 * i + u, 1)], rinv[:, b % 2, 0:n],
                                                   ALU.mult, ALU.mult).then_inc(base_done, 1)
                else:
                    dve.wait_ge(acc_done, per * i + b + 1 + per)
                    nc.vector.tensor_scalar(base[:, b % 2, 0:n], acc[:, u, c, 0:n], scale, None,
                                            ALU.mult).then_inc(base_done, 1)

            def sine(i, b):
                t0, n = chunks[b % n_c]
                dve.wait_ge(cos_done, per * i + b + 1)
                dve.wait_ge(turn_done, per * i + b + 1)
                nc.vector.tensor_tensor(with_sin[:, b % 2, 0:n], aux[:, 1, 0:n], sin[:, t0:t0 + n],
                                        ALU.mult).then_inc(sin_done, 1)

            def low_plain(i, b):
                u, c = divmod(b, n_c)
                n = chunks[c][1]
                dve.wait_ge(hi_done, per * i + b + 1)
                nc.vector.scalar_tensor_tensor(lo_out[:, b % n_out, 0:n], acc[:, u, c, 0:n], scale,
                                               hi_out[:, b % n_out, 0:n].bitcast(F32), ALU.mult,
                                               ALU.subtract).then_inc(lo_done, 1)

            if norm:
                norm.vector(dve)
            run(dve, [(make_base, 0), (sine, 1)] if rotated else [(low_plain, 0)])


def accumulate(nc, g, tag, w_dram, src_hi, src_lo, n_k, n_tiles, chunks, dst, gate=None, whole=None,
               make_norm=None):
    n_c = len(chunks)
    per = 2 * n_c
    n_bodies = n_tiles // 2
    with ExitStack() as ctx:
        sem = semaphores(nc, ctx, tag)
        w = Split(nc, ctx, tag, n_k, sem)
        acc = ctx.enter_context(nc.psum_tensor(tag + "acc", [P, 2, 3, BANK], F32))
        acc_done, added = sem("acc_done"), sem("added")
        src_high, src_low = sem("src_high"), sem("src_low")
        t_first = min(t0 for t0, _ in chunks)
        n_bodies_first = 1 if whole is not None or make_norm else 0
        if make_norm:
            ssq = ctx.enter_context(nc.psum_tensor(tag + "ssq", [P, 2, BANK], F32))
        norm = make_norm(ctx, sem, ssq) if make_norm else None
        block = ctx.enter_context(nc.Block(no_gpsimd_drain=True))

        @block.sync
        def _(sp):
            with sp.Fori(0, n_bodies) as i:
                for u in range(2):
                    sp.wait_ge(w.lo_done, 2 * i + u + 1)
                    sp.dma_start(w.raw[:, u, :], w_dram[bass.ds(2 * i + u, 1)].rearrange("a p n -> p (a n)")
                                 ).then_inc(w.loaded[u], 16)

        @block.scalar
        def _(act):
            def split(i, u):
                act.wait_ge(w.loaded[u], 16 * i + 16)
                act.wait_ge(acc_done, per * i + n_c * (u + 1))
                w.high(u)

            if whole is not None:
                for k in range(n_k):
                    nc.scalar.copy(src_hi[:, k, t_first:TOK], whole[:, k, t_first:TOK]).then_inc(src_high, 1)
                    if k < 2:
                        split(0, k)
            if norm:
                split(0, 0)
                split(0, 1)
                norm.scalar(act)
            with act.Fori(n_bodies_first, n_bodies) as i:
                for u in range(2):
                    split(i, u)

        @block.gpsimd
        def _(pool):
            pool.sem_inc(w.lo_done, 2)
            with pool.Fori(0, n_bodies) as i:
                for u in range(2):
                    pool.wait_ge(w.hi_done, 2 * i + u + 1)
                    w.low(u)

        @block.tensor
        def _(pe):
            pe.sem_inc(acc_done, per)

            def body(i, first=False):
                for u in range(2):
                    pe.wait_ge(w.lo_done, 2 * i + u + 3)
                    k_groups = [[k] for k in range(n_k)] if first and u == 0 else [range(n_k)]
                    for ks in k_groups:
                        if first and u == 0:
                            pe.wait_ge(src_low, ks[0] + 1)
                        for c, (t0, n) in enumerate(chunks):
                            if norm:
                                norm.wait_ready(pe, t0)
                            if ks[0] == 0:
                                pe.wait_ge(added, per * i + n_c * u + c + 1)
                            for k in ks:
                                for j, (a, x) in enumerate(
                                        w.passes(u, k, src_hi[:, k, t0:t0 + n], src_lo[:, k, t0:t0 + n])):
                                    last = nc.tensor.matmul(acc[:, u, c, 0:n], a, x, start=(k == 0 and j == 0),
                                                            stop=(k == n_k - 1 and j == 2))
                            if ks[-1] == n_k - 1:
                                last.then_inc(acc_done, 1)

            if norm:
                norm.tensor(pe)
            if whole is not None:
                body(0, first=True)
            with pe.Fori(1 if whole is not None else 0, n_bodies) as i:
                body(i)

        @block.vector
        def _(dve):
            dve.sem_inc(added, per)
            if norm:
                norm.vector(dve)
            if whole is not None:
                for k in range(n_k):
                    dve.wait_ge(src_high, k + 1)
                    nc.vector.tensor_tensor(src_lo[:, k, t_first:TOK], whole[:, k, t_first:TOK],
                                            src_hi[:, k, t_first:TOK].bitcast(F32), ALU.subtract
                                            ).then_inc(src_low, 1)
            with dve.Fori(0, n_bodies) as i:
                for u in range(2):
                    for c, (t0, n) in enumerate(chunks):
                        dve.wait_ge(acc_done, per * i + n_c * u + c + 1 + per)
                        out = dst[:, bass.ds(2 * i + u, 1), t0:t0 + n].rearrange("p a n -> p (a n)")
                        if gate:
                            nc.vector.scalar_tensor_tensor(out, acc[:, u, c, 0:n], gate(2 * i + u, stream_of(chunks[c])),
                                                           out, ALU.mult, ALU.add).then_inc(added, 1)
                        else:
                            nc.vector.tensor_copy(out, acc[:, u, c, 0:n]).then_inc(added, 1)


def values(nc, g, tag, w_dram, src_hi, src_lo, n_k, n_tiles, dst, make_norm=None):
    n_c = len(ALL_CHUNKS)
    per = 2 * n_c
    n_bodies = n_tiles // 2
    groups = ((0, 4), (4, 4), (8, 2))
    n_g = len(groups)
    with ExitStack() as ctx:
        sb = lambda n, s, d=F32: ctx.enter_context(nc.sbuf_tensor(tag + n, s, d))
        sem = semaphores(nc, ctx, tag)
        w = Split(nc, ctx, tag, n_k, sem)
        v_t = sb("v_t", [P, 2, TOK])
        v_out = sb("v_out", [P, 2, 2, NKT, P], F32R)
        acc = ctx.enter_context(nc.psum_tensor(tag + "acc", [P, 2, 3, BANK], F32))
        turned_ps = ctx.enter_context(nc.psum_tensor(tag + "turned", [P, 2, BANK], F32))
        acc_done, copied, turned, v_hi, v_lo = (
            sem("acc_done"), sem("copied"), sem("turned"), sem("v_hi"), sem("v_lo"))
        stored = [sem("stored0"), sem("stored1")]
        norm = make_norm(ctx, sem, turned_ps) if make_norm else None
        block = ctx.enter_context(nc.Block(no_gpsimd_drain=True))

        @block.sync
        def _(sp):
            for u in range(2):
                sp.sem_inc(stored[u], 16)

            def load(i):
                for u in range(2):
                    sp.wait_ge(w.lo_done, 2 * i + u + 1)
                    sp.dma_start(w.raw[:, u, :], w_dram[bass.ds(2 * i + u, 1)].rearrange("a p n -> p (a n)")
                                 ).then_inc(w.loaded[u], 16)

            def store(i):
                for u in range(2):
                    sp.wait_ge(v_lo, 2 * n_g * i + n_g * (u + 1) + 2)
                    for h in range(2):
                        sp.dma_start(dst[bass.ds(4 * i + 2 * u + h, 1)].rearrange("a p n -> p (a n)"),
                                     v_out[:, u, h].rearrange("p k n -> p (k n)").bitcast(F32)).then_inc(stored[u], 16)

            load(0)
            if n_bodies > 1:
                with sp.Fori(0, n_bodies - 1) as i:
                    load(i + 1)
                    store(i)
            store(n_bodies - 1)
            for u in range(2):
                sp.wait_ge(stored[u], 16 + 32 * n_bodies)

        def run(engine, first_half, second_half):
            first_half(0, 0)
            if n_bodies > 1:
                with engine.Fori(0, n_bodies - 1) as i:
                    first_half(i, 1)
                    second_half(i, 0)
                    first_half(i + 1, 0)
                    second_half(i, 1)
            first_half(n_bodies - 1, 1)
            second_half(n_bodies - 1, 0)
            second_half(n_bodies - 1, 1)

        @block.gpsimd
        def _(pool):
            pool.sem_inc(w.lo_done, 2)
            with pool.Fori(0, n_bodies) as i:
                for u in range(2):
                    pool.wait_ge(w.hi_done, 2 * i + u + 1)
                    w.low(u)

        @block.tensor
        def _(pe):
            def main(i, u):
                pe.wait_ge(w.lo_done, 2 * i + u + 3)
                for c, (t0, n) in enumerate(ALL_CHUNKS):
                    pe.wait_ge(copied, per * i + n_c * u + c + 1)
                    if norm:
                        norm.wait_ready(pe, t0)
                    for k in range(n_k):
                        for j, (a, x) in enumerate(
                                w.passes(u, k, src_hi[:, k, t0:t0 + n], src_lo[:, k, t0:t0 + n])):
                            last = nc.tensor.matmul(acc[:, u, c, 0:n], a, x, start=(k == 0 and j == 0),
                                                    stop=(k == n_k - 1 and j == 2))
                    last.then_inc(acc_done, 1)

            def turn(i, u):
                pe.wait_ge(copied, per * i + n_c * (u + 1) + per)
                for q, (k0, m) in enumerate(groups):
                    pe.wait_ge(v_lo, 2 * n_g * i + n_g * u + q + 1)
                    for k in range(k0, k0 + m):
                        last = nc.tensor.transpose(turned_ps[:, (n_g * u + q) % 2, (k - k0) * P:(k - k0 + 1) * P],
                                                   v_t[:, u, k * P:(k + 1) * P], g.ident[:, :])
                    last.then_inc(turned, 1)

            pe.sem_inc(acc_done, per)
            if norm:
                norm.tensor(pe)
            run(pe, main, turn)

        def turned_view(u, q, m):
            return turned_ps[:, (n_g * u + q) % 2, 0:m * P].rearrange("p (k h f) -> p h k f", h=2, f=V_DIM)

        @block.scalar
        def _(act):
            def split(i, u):
                act.wait_ge(w.loaded[u], 16 * i + 16)
                act.wait_ge(acc_done, per * i + n_c * (u + 1))
                w.high(u)

            def high(i, u):
                for q, (k0, m) in enumerate(groups):
                    if q == 0:
                        act.wait_ge(stored[u], 32 * i + 16)
                    act.wait_ge(turned, 2 * n_g * i + n_g * u + q + 1)
                    nc.scalar.copy(v_out[:, u, :, k0:k0 + m, 0:V_DIM], turned_view(u, q, m)).then_inc(v_hi, 1)

            split(0, 0)
            split(0, 1)
            if norm:
                norm.scalar(act)
            if n_bodies > 1:
                with act.Fori(0, n_bodies - 1) as i:
                    split(i + 1, 0)
                    high(i, 0)
                    split(i + 1, 1)
                    high(i, 1)
            high(n_bodies - 1, 0)
            high(n_bodies - 1, 1)

        @block.vector
        def _(dve):
            dve.sem_inc(copied, per)
            dve.sem_inc(v_lo, 2)

            def copy(i, u):
                for c, (t0, n) in enumerate(ALL_CHUNKS):
                    dve.wait_ge(acc_done, per * i + n_c * u + c + 1 + per)
                    nc.vector.tensor_copy(v_t[:, u, t0:t0 + n], acc[:, u, c, 0:n]).then_inc(copied, 1)

            def low(i, u):
                for q, (k0, m) in enumerate(groups):
                    dve.wait_ge(v_hi, 2 * n_g * i + n_g * u + q + 1)
                    nc.vector.tensor_tensor(v_out[:, u, :, k0:k0 + m, V_DIM:2 * V_DIM], turned_view(u, q, m),
                                            v_out[:, u, :, k0:k0 + m, 0:V_DIM].bitcast(F32), ALU.subtract
                                            ).then_inc(v_lo, 1)

            if norm:
                norm.vector(dve)
            run(dve, copy, low)


def attention(nc, g, tag, load_q, load_k, load_v, rows, passes, o_t):
    n_bodies = HEADS // 2
    CTX_PIECE = 2
    starts = (4, 6, 9, 11)
    ways = ((0, 1, 1, 2, 3, 4), (0, 1, 2, 3, 4, 5))
    scores_at, ctx_exp_at, lat_exp_at, inverse_at = {}, {}, {}, {}
    for q, start in enumerate(starts):
        *pieces, ctx_exp_step, lat_exp_step, inverse_step = (start + d for d in ways[q % 2])
        for c, s in enumerate(pieces):
            scores_at.setdefault((s - 1) % NKT + 1, []).append(((2 - (s - 1) // NKT, q), c))
        for table, s in ((ctx_exp_at, ctx_exp_step), (lat_exp_at, lat_exp_step), (inverse_at, inverse_step)):
            table[(s - 1) % NKT + 1] = (2 - (s - 1) // NKT, q)
    with ExitStack() as ctx:
        sb = lambda n, s, d=F32: ctx.enter_context(nc.sbuf_tensor(tag + n, s, d))
        ps = lambda n, s, d=F32: ctx.enter_context(nc.psum_tensor(tag + n, s, d))
        sem = semaphores(nc, ctx, tag)
        n_qp = 1 + max(a for a, _ in passes)
        q_s = sb("q_s", [P, 2, n_qp, BANK], F32R)
        k_s = sb("k_s", [P, 2, 2, TOK], F32R)
        v_s = sb("v_s", [P, 2, NKT, P], F32R)
        prob = sb("prob", [P, 12, TOK])
        pt_hi = sb("pt_hi", [P, 2, BANK], F32R)
        pt_lo = sb("pt_lo", [P, 2, BANK], F32R)
        max_parts = sb("max_parts", [P, 2, 3])
        neg_max = sb("neg_max", [P, 2, 4])
        total_parts = sb("total_parts", [P, 2, 4, 2])
        total = sb("total", [P, 2, 4])
        r_total = sb("r_total", [P, 2, 4])
        o_a = sb("o_a", [P, 2, BANK])
        o_b = sb("o_b", [P, 2, BANK])
        lat_ps = ps("lat_ps", [P, 2, 2, BANK])
        ctx_ps = ps("ctx_ps", [P, BANK])
        t_ps = ps("t_ps", [P, 2, BANK])
        o_ps = ps("o_ps", [P, BANK])
        q_loaded = [sem("q_loaded0"), sem("q_loaded1")]
        k_loaded = [sem("k_loaded0"), sem("k_loaded1")]
        v_loaded = [sem("v_loaded0"), sem("v_loaded1")]
        ctx_scored, lat_scored, max_part, max_done, ctx_exp, lat_exp, total_done, r_done, normed = (
            sem("ctx_scored"), sem("lat_scored"), sem("max_part"), sem("max_done"), sem("ctx_exp"),
            sem("lat_exp"), sem("total_done"), sem("r_done"), sem("normed"))
        turned, hi_done, lo_done, pv_step = sem("turned"), sem("hi_done"), sem("lo_done"), sem("pv_step")
        o_read, o_added = sem("o_read"), sem("o_added")
        n_q, n_k = len(load_q(0, 0, CTX)), len(load_k(0, 0))
        block = ctx.enter_context(nc.Block(no_gpsimd_drain=True))

        def prob_tile(un, q):
            return prob[:, (un % 4) * 2 + q if q < 2 else 8 + (un % 2) * 2 + q - 2, :]

        def steps(units, more, step):
            for un in units:
                for k in range(1, NKT + 1):
                    step(un, k, k < NKT and un >= 0 or k == NKT and -1 <= un and (un < 3 or more))

        def exists(un, more):
            return 0 <= un and (un < 4 or more)

        def pieces_at(table, un, k, more):
            return [(un + ahead, q, c) for (ahead, q), c in table.get(k, []) if exists(un + ahead, more)]

        def tile_at(table, un, k, more):
            if k not in table:
                return None
            ahead, q = table[k]
            return (un + ahead, q) if exists(un + ahead, more) else None

        def o_rows(tile, un):
            r0 = V_DIM * (un // 2)
            return tile[r0:r0 + V_DIM, un % 2, :]

        way_in, whole_body = (-2, -1), range(4)

        @block.sync
        def _(sp):
            def get_q(i, un):
                for src, part, r0, r in load_q(i, un // 2, CTX + BANK * (un % 2)):
                    sp.dma_start(q_s[r0:r0 + r, un % 2, part, :].bitcast(F32), src).then_inc(q_loaded[un % 2], 16)

            def get_k(i, h):
                for src, part, r0, r in load_k(i, h):
                    sp.dma_start(k_s[r0:r0 + r, h, part, :].bitcast(F32), src).then_inc(k_loaded[h], 16)

            def get_v(i, h):
                sp.dma_start(v_s[:, h].rearrange("p k n -> p (k n)").bitcast(F32), load_v(i, h)
                             ).then_inc(v_loaded[h], 16)

            def output_of(i, un):
                sp.wait_ge(pv_step, 40 * i + 10 * un + 10 + 2)

            def scores_of(i, un):
                sp.wait_ge(ctx_scored, 16 * i + 4 * un + 4)

            def body(i, more):
                scores_of(i, 1)
                get_q(i, 3)
                if more:
                    get_k(i + 1, 0)
                    scores_of(i, 2)
                    get_q(i + 1, 0)
                    output_of(i, 1)
                    get_v(i + 1, 0)
                    scores_of(i, 3)
                    get_q(i + 1, 1)
                    get_k(i + 1, 1)
                    scores_of(i + 1, 0)
                    get_q(i + 1, 2)
                    output_of(i, 3)
                    get_v(i + 1, 1)

            get_q(0, 0)
            get_k(0, 0)
            get_q(0, 1)
            get_v(0, 0)
            get_k(0, 1)
            get_v(0, 1)
            scores_of(0, 0)
            get_q(0, 2)
            with sp.Fori(0, n_bodies - 1) as i:
                body(i, True)
            body(n_bodies - 1, False)

        @block.tensor
        def _(pe):
            def score(out, un, q, lo, hi):
                for j, (a, b) in enumerate(passes):
                    last = nc.tensor.matmul(out, q_s[0:rows, un % 2, a, q * P:(q + 1) * P],
                                            k_s[0:rows, (un // 2) % 2, b, lo:hi], start=(j == 0),
                                            stop=(j == len(passes) - 1))
                return last

            def scores(i, un, q, c):
                m = 16 * i + 4 * un + q
                if q == 0 and c == 0:
                    pe.wait_ge(q_loaded[un % 2], 16 * n_q * (2 * i + un // 2 + 1))
                    pe.wait_ge(k_loaded[(un // 2) % 2], 16 * n_k * (i + un // 4 + 1))
                if c == CTX_PIECE:
                    pe.wait_ge(ctx_exp, m + 1)
                    score(ctx_ps[:, 0:CTX], un, q, 0, CTX).then_inc(ctx_scored, 1)
                else:
                    if c == 0:
                        pe.wait_ge(lat_exp, m + 1)
                    score(lat_ps[:, q % 2, c, :], un, q, CTX + c * BANK, CTX + (c + 1) * BANK
                          ).then_inc(lat_scored, 1)

            def turn(i, un, k):
                if k == 0:
                    pe.wait_ge(normed, 16 * i + 4 * un + 4)
                pe.wait_ge(lo_done, 40 * i + 10 * un + k + 1)
                for q in range(4):
                    last = nc.tensor.transpose(t_ps[:, k % 2, q * P:(q + 1) * P],
                                               prob_tile(un, q)[:, k * P:(k + 1) * P], g.ident[:, :])
                last.then_inc(turned, 1)

            def weigh(i, un, k):
                if k == 0:
                    pe.wait_ge(v_loaded[un // 2], 16 * (i + 1))
                    pe.wait_ge(o_read, 4 * i + un + 1)
                pe.wait_ge(lo_done, 40 * i + 10 * un + k + 1 + 2)
                for j, pt in enumerate((pt_hi, pt_lo)):
                    last = nc.tensor.matmul(o_ps[:, :], v_s[:, un // 2, k, :], pt[:, k % 2, :],
                                            start=(k == 0 and j == 0), stop=(k == NKT - 1 and j == 1))
                last.then_inc(pv_step, 1)

            def body(i, more, units=whole_body):
                def step(un, k, turns):
                    if turns:
                        turn(i, un + k // NKT, k % NKT)
                    for piece in pieces_at(scores_at, un, k, more):
                        scores(i, *piece)
                    if un >= 0:
                        weigh(i, un, k - 1)

                steps(units, more, step)

            pe.sem_inc(pv_step, 2)
            body(0, True, way_in)
            with pe.Fori(0, n_bodies - 1) as i:
                body(i, True)
            body(n_bodies - 1, False)

        @block.vector
        def _(dve):
            def row_max(i, un, q, c):
                m = 16 * i + 4 * un + q
                if c == CTX_PIECE:
                    dve.wait_ge(ctx_scored, m + 1)
                    scores = ctx_ps[:, 0:CTX]
                else:
                    dve.wait_ge(lat_scored, 2 * m + c + 1)
                    scores = lat_ps[:, q % 2, c, :]
                nc.vector.tensor_reduce(max_parts[:, q % 2, c:c + 1], scores, AX_X, ALU.max).then_inc(max_part, 1)
                if c == CTX_PIECE:
                    dve.wait_ge(max_part, 3 * m + 3)
                    nc.vector.tensor_reduce(neg_max[:, un % 2, q:q + 1], max_parts[:, q % 2, :], AX_X, ALU.max,
                                            negate=True).then_inc(max_done, 1)

            def inverse(i, un, q):
                m = 16 * i + 4 * un + q
                dve.wait_ge(lat_exp, m + 1 + 2)
                nc.vector.tensor_tensor(total[:, un % 2, q:q + 1], total_parts[:, un % 2, q, 0:1],
                                        total_parts[:, un % 2, q, 1:2], ALU.add).then_inc(total_done, 1)
                dve.wait_ge(total_done, m + 1)
                nc.vector.reciprocal(r_total[:, un % 2, q:q + 1], total[:, un % 2, q:q + 1]).then_inc(r_done, 1)

            def low(i, un, k):
                dve.wait_ge(hi_done, 40 * i + 10 * un + k + 1)
                nc.vector.tensor_tensor(pt_lo[:, k % 2, :], t_ps[:, k % 2, :], pt_hi[:, k % 2, :].bitcast(F32),
                                        ALU.subtract).then_inc(lo_done, 1)

            def body(i, more, units=whole_body):
                def step(un, k, turns):
                    if turns:
                        low(i, un + k // NKT, k % NKT)
                    for piece in pieces_at(scores_at, un, k, more):
                        row_max(i, *piece)
                    if tile := tile_at(inverse_at, un, k, more):
                        inverse(i, *tile)

                steps(units, more, step)

            dve.sem_inc(lo_done, 2)
            body(0, True, way_in)
            with dve.Fori(0, n_bodies - 1) as i:
                body(i, True)
            body(n_bodies - 1, False)

        @block.scalar
        def _(act):
            def ctx_exponent(i, un, q):
                act.wait_ge(max_done, 16 * i + 4 * un + q + 1)
                nc.scalar.activation(prob_tile(un, q)[:, 0:CTX], ctx_ps[:, 0:CTX], ACT.Exp,
                                     bias=neg_max[:, un % 2, q:q + 1],
                                     accum_out=total_parts[:, un % 2, q, 1:2]).then_inc(ctx_exp, 1)

            def lat_exponent(i, un, q):
                act.wait_ge(max_done, 16 * i + 4 * un + q + 1)
                nc.scalar.activation(prob_tile(un, q)[:, CTX:TOK], lat_ps[:, q % 2].rearrange("p c n -> p (c n)"),
                                     ACT.Exp, bias=neg_max[:, un % 2, q:q + 1],
                                     accum_out=total_parts[:, un % 2, q, 0:1]).then_inc(lat_exp, 1)

            def high(i, un, k):
                act.wait_ge(pv_step, 40 * i + 10 * un + k + 1)
                act.wait_ge(turned, 40 * i + 10 * un + k + 1)
                nc.scalar.copy(pt_hi[:, k % 2, :], t_ps[:, k % 2, :]).then_inc(hi_done, 1)

            def read_out(i, un):
                act.wait_ge(o_added, 2 * i + un % 2 + 1)
                act.wait_ge(pv_step, 40 * i + 10 * un + 10 + 2)
                nc.scalar.copy(o_rows(o_a, un), o_ps[0:V_DIM, :])
                nc.scalar.copy(o_rows(o_b, un), o_ps[V_DIM:2 * V_DIM, :]).then_inc(o_read, 1)

            def body(i, more, units=whole_body):
                def step(un, k, turns):
                    if turns:
                        high(i, un + k // NKT, k % NKT)
                    if tile := tile_at(ctx_exp_at, un, k, more):
                        ctx_exponent(i, *tile)
                    if tile := tile_at(lat_exp_at, un, k, more):
                        lat_exponent(i, *tile)
                    if k == NKT and un >= 0:
                        read_out(i, un)

                steps(units, more, step)

            act.sem_inc(ctx_exp, 1)
            act.sem_inc(lat_exp, 2)
            act.sem_inc(o_read, 1)
            body(0, True, way_in)
            with act.Fori(0, n_bodies - 1) as i:
                body(i, True)
            body(n_bodies - 1, False)

        @block.gpsimd
        def _(pool):
            def normalise(i, un, q):
                pool.wait_ge(r_done, 16 * i + 4 * un + q + 1)
                nc.gpsimd.tensor_tensor(prob_tile(un, q), prob_tile(un, q),
                                        r_total[:, un % 2, q:q + 1].to_broadcast([P, TOK]), ALU.mult
                                        ).then_inc(normed, 1)

            def finish(i, un):
                t0 = CTX + BANK * (un % 2)
                pool.wait_ge(o_read, 4 * i + un + 1 + 1)
                out = o_t[:, bass.ds(i, 1), t0:t0 + BANK].rearrange("p a n -> p (a n)")
                nc.gpsimd.tensor_tensor(out, o_a[:, un % 2, :], o_b[:, un % 2, :], ALU.add).then_inc(o_added, 1)

            def body(i, more, units=whole_body):
                def step(un, k, turns):
                    if tile := tile_at(inverse_at, un, k, more):
                        normalise(i, *tile)
                    if k == NKT and un >= 2:
                        finish(i, un)

                steps(units, more, step)

            pool.sem_inc(o_added, 2)
            body(0, True, way_in)
            with pool.Fori(0, n_bodies - 1) as i:
                body(i, True)
            body(n_bodies - 1, False)


def context_attention(nc, g, tag, load_q, load_k, load_v, o_t):
    group = HEADS // GQA_KV
    n_t = 2 * group
    with ExitStack() as ctx:
        sb = lambda n, s, d=F32: ctx.enter_context(nc.sbuf_tensor(tag + n, s, d))
        ps = lambda n, s, d=F32: ctx.enter_context(nc.psum_tensor(tag + n, s, d))
        sem = semaphores(nc, ctx, tag)
        q_s = sb("q_s", [P, HEADS, CTX], F32R)
        k_s = sb("k_s", [P, GQA_KV, 2, CTX], F32R)
        v_s = sb("v_s", [P, GQA_KV, 2, P], F32R)
        prob = sb("prob", [P, 2, n_t, CTX])
        pt_hi = sb("pt_hi", [P, 2, 2, CTX], F32R)
        pt_lo = sb("pt_lo", [P, 2, 2, CTX], F32R)
        neg_max, total, r_total = sb("neg_max", [P, 2, n_t]), sb("total", [P, 2, n_t]), sb("r_total", [P, 2, n_t])
        o_a, o_b = (sb(n, [P, 2, CTX]) for n in ("o_a", "o_b"))
        s_ps = ps("s_ps", [P, n_t, CTX])
        t_ps = ps("t_ps", [P, 2, BANK])
        o_ps = ps("o_ps", [P, 2, 2 * CTX])
        scored, max_done, exp_done, r_done, normed = (
            sem("scored"), sem("max_done"), sem("exp_done"), sem("r_done"), sem("normed"))
        turned, hi_done, lo_done, weighed = sem("turned"), sem("hi_done"), sem("lo_done"), sem("weighed")
        o_read, o_added = sem("o_read"), sem("o_added")
        loaded = [sem(f"loaded{r}") for r in range(GQA_KV)]
        rounds = range(GQA_KV)
        block = ctx.enter_context(nc.Block(no_gpsimd_drain=True))

        def wide(tile):
            return tile.rearrange("p k n -> p (k n)")

        @block.sync
        def _(sp):
            for r in rounds:
                for part in range(2):
                    rows = slice(64 * part, 64 * part + 64)
                    sp.dma_start(q_s[rows, group * r:group * (r + 1), :].bitcast(F32), load_q(part, group * r, group)
                                 ).then_inc(loaded[r], 16)
                    for half in range(2):
                        sp.dma_start(k_s[64 * half:64 * half + 64, r, part, :].bitcast(F32), load_k(part, r)
                                     ).then_inc(loaded[r], 16)
                sp.dma_start(wide(v_s[:, r]).bitcast(F32), load_v(r)).then_inc(loaded[r], 16)

        @block.tensor
        def _(pe):
            def scores(r):
                if r:
                    pe.wait_ge(exp_done, n_t * r)
                pe.wait_ge(loaded[r], 16 * 7)
                for q in range(n_t):
                    for j in range(2):
                        last = nc.tensor.matmul(s_ps[:, q, :], q_s[:, group * r + q // 2, (q % 2) * P:(q % 2 + 1) * P],
                                                k_s[:, r, j, :], start=(j == 0), stop=(j == 1))
                last.then_inc(scored, 1)

            def turn(e):
                r, j = divmod(e, group)
                pe.wait_ge(normed, n_t * r + 2 * j + 2)
                if e >= 2:
                    pe.wait_ge(lo_done, e - 1)
                for k in range(2):
                    for q in range(2):
                        last = nc.tensor.transpose(t_ps[:, e % 2, (2 * k + q) * P:(2 * k + q + 1) * P],
                                                   prob[:, r % 2, 2 * j + q, k * P:(k + 1) * P], g.ident[:, :])
                last.then_inc(turned, 1)

            def weigh(e):
                r, j = divmod(e, group)
                b = j // 2
                pe.wait_ge(lo_done, e + 1)
                if j % 2 == 0 and r:
                    pe.wait_ge(o_read, 4 * (2 * (r - 1) + b) + 4)
                for k in range(2):
                    for m, pt in enumerate((pt_hi, pt_lo)):
                        last = nc.tensor.matmul(o_ps[:, b, (j % 2) * CTX:(j % 2 + 1) * CTX], v_s[:, r, k, :],
                                                pt[:, e % 2, k, :], start=(k == 0 and m == 0),
                                                stop=(k == 1 and m == 1))
                last.then_inc(weighed, 1)

            scores(0)
            for r in rounds:
                if r + 1 < GQA_KV:
                    scores(r + 1)
                for e in range(group * r, group * (r + 1)):
                    turn(e)
                    if e:
                        weigh(e - 1)
            weigh(group * GQA_KV - 1)

        @block.vector
        def _(dve):
            def low(e):
                dve.wait_ge(hi_done, e + 1)
                nc.vector.tensor_tensor(wide(pt_lo[:, e % 2]), t_ps[:, e % 2, :], wide(pt_hi[:, e % 2]).bitcast(F32),
                                        ALU.subtract).then_inc(lo_done, 1)

            def row_max(r):
                dve.wait_ge(scored, r + 1)
                nc.vector.tensor_reduce(neg_max[:, r % 2, :], s_ps[:, :, :], AX_X, ALU.max, negate=True
                                        ).then_inc(max_done, 1)

            def inverse(r):
                dve.wait_ge(exp_done, n_t * (r + 1))
                nc.vector.reciprocal(r_total[:, r % 2, :], total[:, r % 2, :]).then_inc(r_done, 1)

            row_max(0)
            inverse(0)
            for r in rounds:
                if r + 1 < GQA_KV:
                    row_max(r + 1)
                for e in range(group * r, group * (r + 1)):
                    low(e)
                if r + 1 < GQA_KV:
                    inverse(r + 1)

        @block.scalar
        def _(act):
            def exponents(r):
                act.wait_ge(max_done, r + 1)
                for q in range(n_t):
                    nc.scalar.activation(prob[:, r % 2, q, :], s_ps[:, q, :], ACT.Exp, bias=neg_max[:, r % 2, q:q + 1],
                                         accum_out=total[:, r % 2, q:q + 1]).then_inc(exp_done, 1)

            def high(e):
                if e >= 2:
                    act.wait_ge(weighed, e - 1)
                act.wait_ge(turned, e + 1)
                nc.scalar.copy(wide(pt_hi[:, e % 2]), t_ps[:, e % 2, :]).then_inc(hi_done, 1)

            def read_out(b):
                act.wait_ge(weighed, 2 * b + 2)
                if b >= 2:
                    act.wait_ge(o_added, b - 1)
                for half in range(2):
                    for tile, r0 in ((o_a, 0), (o_b, V_DIM)):
                        nc.scalar.copy(tile[V_DIM * half:V_DIM * (half + 1), b % 2, :],
                                       o_ps[r0:r0 + V_DIM, b % 2, CTX * half:CTX * (half + 1)]).then_inc(o_read, 1)

            exponents(0)
            for r in rounds:
                if r + 1 < GQA_KV:
                    exponents(r + 1)
                for e in range(group * r, group * (r + 1)):
                    high(e)
                    if e % 2 == 0 and e >= 2:
                        read_out(e // 2 - 1)
            read_out(2 * GQA_KV - 1)

        @block.gpsimd
        def _(pool):
            def normalise(r):
                pool.wait_ge(r_done, r + 1)
                for q in range(n_t):
                    nc.gpsimd.tensor_tensor(prob[:, r % 2, q, :], prob[:, r % 2, q, :],
                                            r_total[:, r % 2, q:q + 1].to_broadcast([P, CTX]), ALU.mult
                                            ).then_inc(normed, 1)

            def add_out(b):
                pool.wait_ge(o_read, 4 * b + 4)
                nc.gpsimd.tensor_tensor(o_t[:, b, 0:CTX], o_a[:, b % 2, :], o_b[:, b % 2, :], ALU.add
                                        ).then_inc(o_added, 1)

            normalise(0)
            for r in rounds:
                if r:
                    add_out(2 * r - 1)
                add_out(2 * r)
                if r + 1 < GQA_KV:
                    normalise(r + 1)
            add_out(2 * GQA_KV - 1)


def mlp(nc, g, tag, w_gu, w_down, src_hi, src_lo, chunks, dst, gate, make_norm):
    n_c = len(chunks)
    n_bodies = NFF // 2
    n_w = 3
    n_gu = 2 * n_c
    n_dn = KD * n_c
    with ExitStack() as ctx:
        sb = lambda n, s, d=F32: ctx.enter_context(nc.sbuf_tensor(tag + n, s, d))
        ps = lambda n, s, d=F32: ctx.enter_context(nc.psum_tensor(tag + n, s, d))
        sem = semaphores(nc, ctx, tag)
        w = Split(nc, ctx, tag, KD, sem, slots=n_w)
        a_hi = sb("a_hi", [P, 2, TOK], F32R)
        a_lo = sb("a_lo", [P, 2, TOK], F32R)
        silu = sb("silu", [P, 3, BANK])
        prod = sb("prod", [P, 2, BANK])
        g_ps = ps("g_ps", [P, 3, BANK])
        u_ps = ps("u_ps", [P, 3, BANK])
        d_ps = ps("d_ps", [P, 2, BANK])
        g_done, u_done, d_done = sem("g_done"), sem("u_done"), sem("d_done")
        silu_done, prod_done, a_high, a_low, added = (
            sem("silu_done"), sem("prod_done"), sem("a_high"), sem("a_low"), sem("added"))
        norm = make_norm(ctx, sem, d_ps)
        block = ctx.enter_context(nc.Block(no_gpsimd_drain=True))

        @block.sync
        def _(sp):
            with sp.Fori(0, n_bodies) as i:
                for t in range(6):
                    sp.wait_ge(w.lo_done, 6 * i + t + 1)
                    src = w_gu[bass.ds(4 * i + t, 1)] if t < 4 else w_down[bass.ds(2 * i + t - 4, 1)]
                    sp.dma_start(w.raw[:, t % n_w, :], src.rearrange("a p n -> p (a n)")
                                 ).then_inc(w.loaded[t % n_w], 16)

        @block.gpsimd
        def _(pool):
            pool.sem_inc(w.lo_done, n_w)
            with pool.Fori(0, n_bodies) as i:
                for t in range(6):
                    pool.wait_ge(w.hi_done, 6 * i + t + 1)
                    w.low(t % n_w)

        @block.tensor
        def _(pe):
            pe.sem_inc(u_done, n_gu)
            pe.sem_inc(d_done, n_dn)
            norm.tensor(pe)
            with pe.Fori(0, n_bodies) as i:
                for t in range(4):
                    j, up = divmod(t, 2)
                    bank, done, free = (u_ps, u_done, prod_done) if up else (g_ps, g_done, silu_done)
                    pe.wait_ge(w.lo_done, 6 * i + t + 1 + n_w)
                    for c, (t0, n) in enumerate(chunks):
                        pe.wait_ge(free, n_gu * i + n_c * j + c + 1)
                        norm.wait_ready(pe, t0)
                        for k in range(KD):
                            for m, (a, x) in enumerate(
                                    w.passes(t % n_w, k, src_hi[:, k, t0:t0 + n], src_lo[:, k, t0:t0 + n])):
                                last = nc.tensor.matmul(bank[:, c, 0:n], a, x, start=(k == 0 and m == 0),
                                                        stop=(k == KD - 1 and m == 2))
                        last.then_inc(done, 1)
                pe.wait_ge(w.lo_done, 6 * i + 6 + n_w)
                for c, (t0, n) in enumerate(chunks):
                    pe.wait_ge(a_low, n_gu * i + n_c + c + 1 + 2)
                    for m in range(KD):
                        e = c * KD + m
                        pe.wait_ge(added, n_dn * i + e + 1)
                        for j in range(2):
                            for q, (a, x) in enumerate(
                                    w.passes(1 + j, m, a_hi[:, j, t0:t0 + n], a_lo[:, j, t0:t0 + n])):
                                last = nc.tensor.matmul(d_ps[:, e % 2, 0:n], a, x, start=(j == 0 and q == 0),
                                                        stop=(j == 1 and q == 2))
                        last.then_inc(d_done, 1)

        @block.scalar
        def _(act):
            def body(i, first=False):
                last_use = ((u_done, n_gu * i + n_gu), (d_done, n_dn * i + n_dn), (d_done, n_dn * i + n_dn),
                            (g_done, n_gu * i + n_c), (u_done, n_gu * i + n_c + n_gu), (g_done, n_gu * i + n_gu))

                def split(t):
                    act.wait_ge(w.loaded[t % n_w], 32 * i + 16 * (t // n_w + 1))
                    act.wait_ge(*last_use[t])
                    w.high(t % n_w)

                def activate(j):
                    for c, (_, n) in enumerate(chunks):
                        act.wait_ge(prod_done, n_gu * i + n_c * j + c + 1)
                        act.wait_ge(g_done, n_gu * i + n_c * j + c + 1)
                        nc.scalar.activation(silu[:, c, 0:n], g_ps[:, c, 0:n], ACT.Silu).then_inc(silu_done, 1)

                def high(j):
                    for c, (t0, n) in enumerate(chunks):
                        act.wait_ge(prod_done, n_gu * i + n_c * j + c + 1 + n_c)
                        nc.scalar.copy(a_hi[:, j, t0:t0 + n], prod[:, (n_c * j + c) % 2, 0:n]).then_inc(a_high, 1)

                for t in range(n_w):
                    split(t)
                if first:
                    norm.scalar(act)
                activate(0)
                split(3)
                high(0)
                split(4)
                activate(1)
                split(5)
                high(1)

            body(0, first=True)
            with act.Fori(1, n_bodies) as i:
                body(i)

        @block.vector
        def _(dve):
            dve.sem_inc(silu_done, n_c)
            dve.sem_inc(prod_done, n_c)
            dve.sem_inc(a_low, 2)
            dve.sem_inc(added, 2)
            norm.vector(dve)
            with dve.Fori(0, n_bodies) as i:
                def multiply(e):
                    c = e % n_c
                    n = chunks[c][1]
                    dve.wait_ge(a_low, n_gu * i + e + 1)
                    dve.wait_ge(silu_done, n_gu * i + e + 1 + n_c)
                    dve.wait_ge(u_done, n_gu * i + e + 1 + n_gu)
                    nc.vector.tensor_tensor(prod[:, e % 2, 0:n], silu[:, c, 0:n], u_ps[:, c, 0:n], ALU.mult
                                            ).then_inc(prod_done, 1)

                def low(e):
                    j, c = divmod(e, n_c)
                    t0, n = chunks[c]
                    dve.wait_ge(a_high, n_gu * i + e + 1)
                    nc.vector.tensor_tensor(a_lo[:, j, t0:t0 + n], prod[:, e % 2, 0:n],
                                            a_hi[:, j, t0:t0 + n].bitcast(F32), ALU.subtract).then_inc(a_low, 1)

                for e in range(n_gu):
                    multiply(e)
                    low(e)
                for c, (t0, n) in enumerate(chunks):
                    for m in range(KD):
                        e = c * KD + m
                        dve.wait_ge(d_done, n_dn * i + e + 1 + n_dn)
                        nc.vector.scalar_tensor_tensor(dst[:, m, t0:t0 + n], d_ps[:, e % 2, 0:n],
                                                       gate(m, stream_of(chunks[c])), dst[:, m, t0:t0 + n],
                                                       ALU.mult, ALU.add).then_inc(added, 1)


def rotate_rows(nc, g, tag, src, turn, cos, sin, out_dram):
    n_c = len(ALL_CHUNKS)
    with ExitStack() as ctx:
        sb = lambda n, s, d=F32: ctx.enter_context(nc.sbuf_tensor(tag + n, s, d))
        sem = semaphores(nc, ctx, tag)
        with_cos, with_sin, whole = sb("with_cos", [P, TOK]), sb("with_sin", [P, TOK]), sb("whole", [P, TOK])
        hi, lo = sb("hi", [P, TOK], F32R), sb("lo", [P, TOK], F32R)
        turned_ps = ctx.enter_context(nc.psum_tensor(tag + "turned", [P, 3, BANK], F32))
        turned, cos_done, sin_done, whole_done, hi_done, lo_done, stored = (
            sem("turned"), sem("cos_done"), sem("sin_done"), sem("whole_done"), sem("hi_done"), sem("lo_done"),
            sem("stored"))
        block = ctx.enter_context(nc.Block(no_gpsimd_drain=True))

        @block.tensor
        def _(pe):
            for c, (t0, n) in enumerate(ALL_CHUNKS):
                nc.tensor.matmul(turned_ps[:, c, 0:n], turn[:, :], src[:, t0:t0 + n], start=True, stop=True
                                 ).then_inc(turned, 1)

        @block.gpsimd
        def _(pool):
            nc.gpsimd.tensor_tensor(with_cos[:, :], src, cos[:, :], ALU.mult).then_inc(cos_done, 1)

        @block.vector
        def _(dve):
            for c, (t0, n) in enumerate(ALL_CHUNKS):
                dve.wait_ge(turned, c + 1)
                nc.vector.tensor_tensor(with_sin[:, t0:t0 + n], turned_ps[:, c, 0:n], sin[:, t0:t0 + n],
                                        ALU.mult).then_inc(sin_done, 1)
            dve.wait_ge(sin_done, n_c)
            dve.wait_ge(cos_done, 1)
            nc.vector.tensor_tensor(whole[:, :], with_cos[:, :], with_sin[:, :], ALU.add).then_inc(whole_done, 1)
            dve.wait_ge(hi_done, 1)
            nc.vector.tensor_tensor(lo[:, :], whole[:, :], hi[:, :].bitcast(F32), ALU.subtract).then_inc(lo_done, 1)

        @block.scalar
        def _(act):
            act.wait_ge(whole_done, 1)
            nc.scalar.copy(hi[:, :], whole[:, :]).then_inc(hi_done, 1)

        @block.sync
        def _(sp):
            sp.wait_ge(lo_done, 1)
            for part, tile in ((0, hi), (1, lo)):
                sp.dma_start(out_dram[part], tile[0:ROPE, :].bitcast(F32)).then_inc(stored, 16)
            sp.wait_ge(stored, 32)


def fetch(nc, tag, pairs):
    with ExitStack() as ctx:
        loaded = semaphores(nc, ctx, tag)("loaded")
        block = ctx.enter_context(nc.Block(no_gpsimd_drain=True))

        @block.sync
        def _(sp):
            for dst, src in pairs:
                sp.dma_start(dst, src).then_inc(loaded, 16)
            sp.wait_ge(loaded, 16 * len(pairs))


class Globals:
    pass


def flat(ap):
    return ap.rearrange("a p n -> p (a n)")


def dit_kernel(nc, a, out):
    g = Globals()
    g.w_mod = [a["w_mod"][layer] for layer in range(2)]
    scratch = {}

    def dram(name, shape):
        scratch[name] = nc.dram_tensor(name, shape, F32, kind="Internal").ap()
        return scratch[name]

    with ExitStack() as ctx:
        sb = lambda n, s, d=F32: ctx.enter_context(nc.sbuf_tensor(n, s, d))
        x_t = sb("x_t", [P, KD, TOK])
        g.ident, g.ones, g.head_ones = sb("ident", [P, P]), sb("ones", [P, P]), sb("head_ones", [P, P])
        turn64, turn32 = sb("turn64", [P, P]), sb("turn32", [P, P])
        g.eps = sb("eps", [P, 1])
        g.mod_t = sb("mod_t", [P, MOD_COLS, 2])
        g.gain1, g.gain2 = sb("gain1", [P, KD, 2]), sb("gain2", [P, KD, 2])
        g.b_mod = sb("b_mod", [P, 2, MOD_COLS, 2])
        g.norms = sb("norms", [P, 2, 2, KD, 2])
        c_t = sb("c_t", [P, KD, 2])
        silu_c = sb("silu_c", [P, KD, 2])
        g.silu_parts = sb("silu_parts", [P, KD, 4], F32R)
        g.pair_sum = sb("pair_sum", [4, 2])
        final_gain, qa_gain, kva_gain = sb("final_gain", [P, KD]), sb("qa_gain", [P, 3]), sb("kva_gain", [P, 2])
        qk_gain_in, qk_gains = sb("qk_gain_in", [P, 2]), sb("qk_gains", [P, 10])

        fetch(nc, "in_", [
            (x_t[:, :, CTX:TOK], a["x_t"].rearrange("(k p) n -> p k n", p=P)),
            (x_t[:, :, 0:CTX], a["ctx_t"].rearrange("(k p) n -> p k n", p=P)),
            (g.ident[:, :], a["ident"]), (g.ones[:, :], a["ones"]), (g.head_ones[:, :], a["head_ones"]),
            (turn64[:, :], a["turn64"]), (turn32[:, :], a["turn32"]), (g.pair_sum[:, :], a["pair_sum"]),
            (g.b_mod[:, :, :, :], a["b_mod"]), (g.norms[:, :, :, :, :], a["norms"]), (c_t[:, :, :], a["c_t"]),
            (final_gain[:, :], a["final_gain"]), (qa_gain[:, :], a["qa_gain"]), (kva_gain[:, :], a["kva_gain"]),
            (qk_gain_in[:, :], a["qk_gain"]),
        ])
        setup_done, silu_done, silu_high = (
            nc.alloc_semaphore(n) for n in ("setup_done", "silu_done", "silu_high"))
        with nc.Block(no_gpsimd_drain=True) as block:
            @block.vector
            def _(dve):
                nc.vector.memset(g.eps[:, :], EPS).then_inc(setup_done, 1)
                nc.vector.tensor_scalar(qk_gains[:, 0:8], qk_gain_in[:, 0:1].to_broadcast([P, 8]),
                                        GQA_HD ** -0.5, None, ALU.mult).then_inc(setup_done, 1)
                nc.vector.tensor_copy(qk_gains[:, 8:10], qk_gain_in[:, 1:2].to_broadcast([P, 2])
                                      ).then_inc(setup_done, 1)
                dve.wait_ge(silu_high, 1)
                nc.vector.tensor_tensor(g.silu_parts[:, :, 2:4], silu_c[:, :, :],
                                        g.silu_parts[:, :, 0:2].bitcast(F32), ALU.subtract).then_inc(setup_done, 1)

            @block.scalar
            def _(act):
                nc.scalar.activation(silu_c[:, :, :], c_t[:, :, :], ACT.Silu).then_inc(silu_done, 1)
                act.wait_ge(silu_done, 1)
                nc.scalar.copy(g.silu_parts[:, :, 0:2], silu_c[:, :, :]).then_inc(silu_high, 1)

        def mod(split):
            return lambda k, s: flat_column(g.mod_t, split * KD + k, s)

        def flat_column(table, col, s):
            return table[:, bass.ds(col, 1), s:s + 1].rearrange("p a b -> p (a b)")

        def attention_output(layer):
            octx = ExitStack()
            return octx.enter_context(nc.sbuf_tensor(f"o{layer}", [P, KD, TOK], F32)), octx

        def norm_of(tag, *args):
            return lambda ctx, sem, ssq: Norm(nc, g, ctx, sem, tag, *args, ssq)

        modulation(nc, g, 0)
        qk0 = dram("qk0", (2, 10, P, TOK))
        qk0_heads = qk0.rearrange("s t (h p) n -> s (t h) p n", p=GQA_HD)
        v0 = dram("v0", (GQA_KV, P, NKT * P))

        with ExitStack() as hctx:
            h_hi = hctx.enter_context(nc.sbuf_tensor("h0_hi", [P, KD, TOK], F32R))
            h_lo = hctx.enter_context(nc.sbuf_tensor("h0_lo", [P, KD, TOK], F32R))
            values(nc, g, "v0_", a["w_v0"], h_hi, h_lo, KD, 2, v0, norm_of(
                "n01_", x_t, KD, lambda k, s: g.gain1[:, k, s:s + 1], mod(0), h_hi, h_lo, ALL_CHUNKS))
            with ExitStack() as rctx:
                cos = rctx.enter_context(nc.sbuf_tensor("cos64", [P, TOK], F32))
                sin = rctx.enter_context(nc.sbuf_tensor("sin64", [P, TOK], F32))
                fetch(nc, "rope64_", [(cos[:, :], a["cos64"]), (sin[:, :], a["sin64"])])
                project(nc, g, "qk0_", a["w_qk0"], h_hi, h_lo, KD, 10, ALL_CHUNKS, "norm_rope",
                        lambda part, t, t0, n: flat(qk0[part, bass.ds(t, 1), :, t0:t0 + n]),
                        gains=qk_gains, turn=turn64, cos=cos, sin=sin)

        def q0(i, h, t0):
            return [(flat(qk0_heads[part, bass.ds(2 * i + h, 1), :, t0:t0 + BANK]), 0, 64 * part, 64)
                    for part in range(2)]

        def k0(i, h):
            return [(flat(qk0_heads[part, bass.ds(HEADS + i // 2, 1), :, :]), part, 64 * half, 64)
                    for part in range(2) for half in range(2)]

        o_t, o_ctx = attention_output(0)
        attention(nc, g, "at0_", q0, k0, lambda i, h: flat(v0[bass.ds(i // 2, 1)]), P, ((0, 0), (0, 1)), o_t)
        context_attention(
            nc, g, "ca0_", lambda part, h, n: qk0_heads[part, h:h + n, :, 0:CTX].rearrange("h p n -> p h n"),
            lambda part, r: qk0_heads[part, HEADS + r, :, 0:CTX], lambda r: v0[r, :, 0:CTX], o_t)

        def out_and_mlp(layer, o_t, o_ctx, w_o, w_gu, w_down, chunks):
            with o_ctx:
                o_hi = o_ctx.enter_context(nc.sbuf_tensor(f"o{layer}_hi", [P, KD, TOK], F32R))
                o_lo = o_ctx.enter_context(nc.sbuf_tensor(f"o{layer}_lo", [P, KD, TOK], F32R))
                accumulate(nc, g, f"wo{layer}_", w_o, o_hi, o_lo, KD, KD, chunks, x_t, mod(2), whole=o_t)
            with ExitStack() as hctx:
                h_hi = hctx.enter_context(nc.sbuf_tensor(f"m{layer}_hi", [P, KD, TOK], F32R))
                h_lo = hctx.enter_context(nc.sbuf_tensor(f"m{layer}_lo", [P, KD, TOK], F32R))
                mlp(nc, g, f"mlp{layer}_", w_gu, w_down, h_hi, h_lo, chunks, x_t, mod(5), norm_of(
                    f"n{layer}2_", x_t, KD, lambda k, s: g.gain2[:, k, s:s + 1], mod(3), h_hi, h_lo, chunks))

        out_and_mlp(0, o_t, o_ctx, a["w_o0"], a["w_gu0"], a["w_down0"], ALL_CHUNKS)

        modulation(nc, g, 1)
        q_nope, q_rope = dram("q_nope", (2, 8, P, TOK)), dram("q_rope", (2, 4, P, TOK))
        k_nope, k_rope, v1 = dram("k_nope", (2, 8, P, TOK)), dram("k_rope", (2, ROPE, TOK)), dram(
            "v1", (HEADS, P, NKT * P))
        q_nope_heads = q_nope.rearrange("s t (h p) n -> s (t h) p n", p=NOPE)
        q_rope_heads = q_rope.rearrange("s t (h p) n -> s (t h) p n", p=ROPE)
        k_nope_heads = k_nope.rearrange("s t (h p) n -> s (t h) p n", p=NOPE)
        mla_scale = float(np.float32(QK_MLA ** -0.5))

        with ExitStack() as lctx:
            low_rank = lctx.enter_context(nc.sbuf_tensor("low_rank", [P, W_IN_TILES, TOK], F32))
            with ExitStack() as hctx:
                h_hi = hctx.enter_context(nc.sbuf_tensor("h1_hi", [P, KD, TOK], F32R))
                h_lo = hctx.enter_context(nc.sbuf_tensor("h1_lo", [P, KD, TOK], F32R))
                accumulate(nc, g, "win_", a["w_in"], h_hi, h_lo, KD, W_IN_TILES, ALL_CHUNKS, low_rank,
                           make_norm=norm_of("n11_", x_t, KD, lambda k, s: g.gain1[:, k, s:s + 1], mod(0),
                                             h_hi, h_lo, ALL_CHUNKS))
            q_hi = lctx.enter_context(nc.sbuf_tensor("q_hi", [P, 3, TOK], F32R))
            q_lo = lctx.enter_context(nc.sbuf_tensor("q_lo", [P, 3, TOK], F32R))
            kv_hi = lctx.enter_context(nc.sbuf_tensor("kv_hi", [P, 2, TOK], F32R))
            kv_lo = lctx.enter_context(nc.sbuf_tensor("kv_lo", [P, 2, TOK], F32R))
            cos = lctx.enter_context(nc.sbuf_tensor("cos32", [P, TOK], F32))
            sin = lctx.enter_context(nc.sbuf_tensor("sin32", [P, TOK], F32))
            fetch(nc, "rope32_", [(cos[:, :], a["cos32"]), (sin[:, :], a["sin32"])])
            norm_q = norm_of("nqa_", low_rank[:, 0:3], 3, lambda k, s: qa_gain[:, k:k + 1], None, q_hi, q_lo, LAT_CHUNKS)
            norm_kv = norm_of("nkv_", low_rank[:, 3:5], 2, lambda k, s: kva_gain[:, k:k + 1], None, kv_hi, kv_lo,
                              ALL_CHUNKS)
            rotate_rows(nc, g, "kr_", low_rank[:, 5, :], turn32, cos, sin, k_rope)
            project(nc, g, "qn_", a["w_q_nope"], q_hi, q_lo, 3, 8, LAT_CHUNKS, "plain",
                    lambda part, t, t0, n: flat(q_nope[part, bass.ds(t, 1), :, t0:t0 + n]), scale=mla_scale,
                    make_norm=norm_q)
            project(nc, g, "qr_", a["w_q_rope"], q_hi, q_lo, 3, 4, LAT_CHUNKS, "rope",
                    lambda part, t, t0, n: flat(q_rope[part, bass.ds(t, 1), :, t0:t0 + n]), scale=mla_scale,
                    turn=turn32, cos=cos, sin=sin)
            project(nc, g, "kn_", a["w_k_nope"], kv_hi, kv_lo, 2, 8, ALL_CHUNKS, "plain",
                    lambda part, t, t0, n: flat(k_nope[part, bass.ds(t, 1), :, t0:t0 + n]), make_norm=norm_kv)
            values(nc, g, "v1_", a["w_v1"], kv_hi, kv_lo, 2, 8, v1)

        def q1(i, h, t0):
            return ([(flat(q_nope_heads[part, bass.ds(2 * i + h, 1), :, t0:t0 + BANK]), part, 0, NOPE)
                     for part in range(2)]
                    + [(flat(q_rope_heads[part, bass.ds(2 * i + h, 1), :, t0:t0 + BANK]), part, NOPE, ROPE)
                       for part in range(2)])

        def k1(i, h):
            return ([(flat(k_nope_heads[part, bass.ds(2 * i + h, 1), :, :]), part, 0, NOPE) for part in range(2)]
                    + [(k_rope[part], part, NOPE, ROPE) for part in range(2)])

        o_t, o_ctx = attention_output(1)
        attention(nc, g, "at1_", q1, k1, lambda i, h: flat(v1[bass.ds(2 * i + h, 1)]), QK_MLA,
                  ((0, 0), (1, 0), (0, 1)), o_t)
        out_and_mlp(1, o_t, o_ctx, a["w_o1"], a["w_gu1"], a["w_down1"], LAT_CHUNKS)

        final_norm(nc, g, "fin_", x_t, KD, lambda k, s: final_gain[:, k:k + 1], LAT_CHUNKS, out)




def tiles(w):
    k, n = w.shape
    return np.ascontiguousarray(w.reshape(k // P, P, n // P, P).transpose(2, 1, 0, 3).reshape(n // P, P, k))


def per_feature(v):
    return np.ascontiguousarray(v.reshape(-1, P).T)


def rope_tables(rot_dim):
    n = rot_dim // 4
    inv = np.power(np.float32(10000.0), -np.arange(n, dtype=np.float32) / np.float32(n))
    rows = SEQ // GRID_W
    row = np.repeat(np.arange(rows, dtype=np.float32), GRID_W)
    col = np.tile(np.arange(GRID_W, dtype=np.float32), rows)
    ang = np.concatenate([row[:, None] * inv, col[:, None] * inv], axis=-1).astype(np.float64)
    cos = np.ones((rot_dim // 2, TOK), np.float32)
    sin = np.zeros((rot_dim // 2, TOK), np.float32)
    cos[:, CTX:], sin[:, CTX:] = np.cos(ang).T, np.sin(ang).T
    return np.tile(cos, (2 * P // rot_dim, 1)), np.tile(sin, (2 * P // rot_dim, 1))


def turn_matrix(rot_dim):
    half = rot_dim // 2
    m = np.zeros((P, P), np.float32)
    for g0 in range(0, P, rot_dim):
        for j in range(half):
            m[g0 + half + j, g0 + j] = -1.0
            m[g0 + j, g0 + half + j] = 1.0
    return m


def kernel(**inputs):
    import concourse.bacc as bacc
    from concourse.bass_utils import run_bass_kernel_spmd

    v = {name: np.asarray(x) for name, x in inputs.items()}
    arrays = {
        "x_t": v["x"][0].T,
        "ctx_t": v["ctx"][0].T,
        "c_t": np.stack([v["c"][0], v["c_ctx"]], axis=-1).reshape(KD, P, 2).transpose(1, 0, 2),
        "w_mod": v["w_mod"].reshape(2, KD, P, 12, BANK).transpose(0, 3, 2, 1, 4).reshape(2, 12, P, KD * BANK),
        "b_mod": np.repeat(v["b_mod"].reshape(2, MOD_COLS, P).transpose(2, 0, 1)[..., None], 2, axis=-1),
        "norms": np.repeat(np.stack([v["norm1"], v["norm2"]], axis=1).reshape(2, 2, KD, P).transpose(3, 0, 1, 2)
                           [..., None], 2, axis=-1),
        "final_gain": per_feature(v["final_norm"]),
        "qa_gain": per_feature(v["mla_q_a_norm"][0]),
        "kva_gain": per_feature(v["mla_kv_a_norm"][0]),
        "qk_gain": np.stack([np.tile(v["gqa_q_norm"][0], 2), np.tile(v["gqa_k_norm"][0], 2)], axis=-1),
    }
    qkv = v["gqa_w_qkv"][0]
    n_qk = (HEADS + GQA_KV) * GQA_HD
    arrays["w_qk0"] = tiles(qkv[:, :n_qk])
    arrays["w_v0"] = tiles(qkv[:, n_qk:])
    w_in = v["mla_w_in"][0]
    padded = np.zeros((D, W_IN_TILES * P), w_in.dtype)
    padded[:, :w_in.shape[1]] = w_in
    arrays["w_in"] = tiles(padded)
    q_b = v["mla_q_b"][0].reshape(Q_RANK, HEADS, QK_MLA)
    arrays["w_q_nope"] = tiles(q_b[:, :, :NOPE].reshape(Q_RANK, HEADS * NOPE))
    arrays["w_q_rope"] = tiles(q_b[:, :, NOPE:].reshape(Q_RANK, HEADS * ROPE))
    kv_b = v["mla_kv_b"][0].reshape(KV_RANK, HEADS, NOPE + V_DIM)
    arrays["w_k_nope"] = tiles(kv_b[:, :, :NOPE].reshape(KV_RANK, HEADS * NOPE))
    arrays["w_v1"] = tiles(kv_b[:, :, NOPE:].reshape(KV_RANK, HEADS * V_DIM))
    for layer, w_o in enumerate((v["gqa_w_o"][0], v["mla_w_o"][0])):
        arrays[f"w_o{layer}"] = tiles(w_o)
        gu = v["w_gate_up"][layer]
        arrays[f"w_gu{layer}"] = np.stack([tiles(gu[:, :DFF]), tiles(gu[:, DFF:])], axis=1).reshape(2 * NFF, P, D)
        arrays[f"w_down{layer}"] = v["w_down"][layer].reshape(NFF, P, D)
    arrays["ident"] = np.eye(P, dtype=np.float32)
    arrays["pair_sum"] = np.tile(np.eye(2, dtype=np.float32), (2, 1))
    arrays["ones"] = np.ones((P, P), np.float32)
    arrays["head_ones"] = np.kron(np.eye(2, dtype=np.float32), np.ones((64, 64), np.float32))
    arrays["turn64"], arrays["turn32"] = turn_matrix(64), turn_matrix(32)
    arrays["cos64"], arrays["sin64"] = rope_tables(64)
    arrays["cos32"], arrays["sin32"] = rope_tables(32)
    arrays = {name: np.ascontiguousarray(x) for name, x in arrays.items()}

    nc = bacc.Bacc("TRN2", target_bir_lowering=False, num_devices=1)
    aps = {name: nc.dram_tensor(f"in_{name}", x.shape, mybir.dt.from_np(x.dtype), kind="ExternalInput").ap()
           for name, x in arrays.items()}
    out = nc.dram_tensor("out_t", (D, SEQ), F32, kind="ExternalOutput").ap()
    dit_kernel(nc, aps, out)
    r = run_bass_kernel_spmd(nc, [{f"in_{name}": x for name, x in arrays.items()}], core_ids=[0])
    return np.ascontiguousarray(r.results[0]["out_t"].T)[None]
```
